# Optimizing a Trainium2 kernel written in Bass

```python
import math
import jax, jax.numpy as jnp
from jax import lax
import numpy as np

D_MODEL = 2048
BATCH = 1
SEQ = 256
DEPTH = 2

S5_WIDTH = D_MODEL // 4
S5_GROUP = 16
S5_GROUPS = S5_WIDTH // S5_GROUP
S5_STATE = 64
HEAD_DIM = 64
ATTN_HEADS = 8
ATTN_KV_HEADS = 2
ATTN_WIDTH = ATTN_HEADS * HEAD_DIM
IDX_HEADS = 4
IDX_DIM = 64
TOPK_MAX = 256
Q_BLOCK = 128
SSD_WIDTH = D_MODEL // 2
SSD_HEAD_DIM = 64
SSD_HEADS = SSD_WIDTH // SSD_HEAD_DIM
SSD_GROUPS = 2
SSD_STATE = 128
SSD_CONV = 4
SSD_CHUNK = 128
SSD_XBC = SSD_WIDTH + 2 * SSD_GROUPS * SSD_STATE
MEM_LEN = 256
MEM_HEADS = 4
MEM_WIDTH = MEM_HEADS * HEAD_DIM
N_BRANCH = 4
ROPE_THETA = 500000.0
ROPE_DIM = HEAD_DIM // 4
DEEPNORM_ALPHA = (2 * DEPTH) ** 0.25
DEEPNORM_BETA = (8 * DEPTH) ** -0.25
LN_EPS = 1e-5
RMS_EPS = 1e-5

SPLITS = (
    ('s5_u', S5_WIDTH), ('s5_z', S5_WIDTH),
    ('att_q', ATTN_WIDTH), ('att_k', ATTN_KV_HEADS * HEAD_DIM), ('att_v', ATTN_KV_HEADS * HEAD_DIM), ('att_z', ATTN_WIDTH),
    ('idx_q', IDX_HEADS * IDX_DIM), ('idx_k', IDX_DIM), ('idx_w', IDX_HEADS),
    ('ssd_z', SSD_WIDTH), ('ssd_xbc', SSD_XBC), ('ssd_dt', SSD_HEADS),
    ('mem_q', MEM_WIDTH), ('mem_z', MEM_WIDTH),
    ('gates', N_BRANCH * D_MODEL),
)
IN_WIDTH = sum(w for _, w in SPLITS)

kernel_name = "hybrid_s5_dsa_ssd_deepnorm"

def split_columns(h):
    offs = np.cumsum([w for _, w in SPLITS])[:-1].tolist()
    return dict(zip([n for n, _ in SPLITS], jnp.split(h, offs, axis=-1)))

def layer_norm(x, g, b):
    xf = x.astype(jnp.float32)
    mu = jnp.mean(xf, -1, keepdims=True)
    var = jnp.mean(jnp.square(xf - mu), -1, keepdims=True)
    return ((xf - mu) * lax.rsqrt(var + LN_EPS) * g + b).astype(x.dtype)

def partial_rope(x, pos):
    half = ROPE_DIM // 2
    inv = ROPE_THETA ** (-jnp.arange(half, dtype=jnp.float32) * 2.0 / ROPE_DIM)
    ang = pos.astype(jnp.float32)[:, :, None, None] * inv
    cos, sin = jnp.cos(ang), jnp.sin(ang)
    xr = x[..., :ROPE_DIM].astype(jnp.float32)
    x1, x2 = xr[..., :half], xr[..., half:]
    rot = jnp.concatenate([x1 * cos - x2 * sin, x2 * cos + x1 * sin], -1).astype(x.dtype)
    return jnp.concatenate([rot, x[..., ROPE_DIM:]], -1)

def _complex_affine_combine(e1, e2):
    a1r, a1i, b1r, b1i = e1
    a2r, a2i, b2r, b2i = e2
    ar = a2r * a1r - a2i * a1i
    ai = a2r * a1i + a2i * a1r
    br = a2r * b1r - a2i * b1i + b2r
    bi = a2r * b1i + a2i * b1r + b2i
    return (ar, ai, br, bi)

def s5_mixer(u, lam_re, lam_im, log_dt, b_re, b_im, c_re, c_im, d_skip, w_glu, b_glu):
    bsz, L, _ = u.shape
    f32 = jnp.float32
    uf = u.reshape(bsz, L, S5_GROUPS, S5_GROUP).astype(f32)
    dt = jnp.exp(log_dt.astype(f32))[:, None]
    lr, li = lam_re.astype(f32), lam_im.astype(f32)
    mag = jnp.exp(lr * dt)
    ar, ai = mag * jnp.cos(li * dt), mag * jnp.sin(li * dt)
    den = lr * lr + li * li
    nr, ni = ar - 1.0, ai
    fr, fi = (nr * lr + ni * li) / den, (ni * lr - nr * li) / den
    bbr = fr[..., None] * b_re - fi[..., None] * b_im
    bbi = fr[..., None] * b_im + fi[..., None] * b_re
    bu_r = jnp.einsum('blgh,gph->blgp', uf, bbr.astype(f32))
    bu_i = jnp.einsum('blgh,gph->blgp', uf, bbi.astype(f32))
    a_r = jnp.broadcast_to(ar, bu_r.shape)
    a_i = jnp.broadcast_to(ai, bu_r.shape)
    _, _, s_r, s_i = lax.associative_scan(_complex_affine_combine, (a_r, a_i, bu_r, bu_i), axis=1)
    y = (jnp.einsum('blgp,ghp->blgh', s_r, c_re.astype(f32))
         - jnp.einsum('blgp,ghp->blgh', s_i, c_im.astype(f32))
         + d_skip.astype(f32) * uf)
    y = jax.nn.gelu(y.reshape(bsz, L, S5_WIDTH))
    y = y * jax.nn.sigmoid(y @ w_glu.astype(f32) + b_glu.astype(f32))
    return y.astype(u.dtype)

def dsa_attention(q, k, v, qi, ki, wi):
    bsz, L = q.shape[:2]
    f32 = jnp.float32
    topk = min(TOPK_MAX, L // 4)
    nb = L // Q_BLOCK
    grp = ATTN_HEADS // ATTN_KV_HEADS
    key_pos = jnp.arange(L)
    kif = ki.astype(f32)

    def blockify(t):
        return jnp.moveaxis(t.reshape((bsz, nb, Q_BLOCK) + t.shape[2:]), 1, 0)

    def block(args):
        qb, qib, wib, start = args
        qpos = start + jnp.arange(Q_BLOCK)
        visible = key_pos[None, :] <= qpos[:, None]
        s = jax.nn.relu(jnp.einsum('bqhd,bsd->bqhs', qib.astype(f32), kif))
        score = jnp.einsum('bqhs,bqh->bqs', s, wib.astype(f32))
        score = jnp.where(visible[None], score, -jnp.inf)
        _, sel = lax.top_k(score, topk)
        valid = sel <= qpos[None, :, None]
        kg = jax.vmap(lambda kk, ii: kk[ii])(k, sel)
        vg = jax.vmap(lambda vv, ii: vv[ii])(v, sel)
        qg = qb.reshape(bsz, Q_BLOCK, ATTN_KV_HEADS, grp, HEAD_DIM)
        logits = jnp.einsum('bqgjd,bqkgd->bqgjk', qg, kg).astype(f32) * (HEAD_DIM ** -0.5)
        logits = jnp.where(valid[:, :, None, None, :], logits, -jnp.inf)
        p = jax.nn.softmax(logits, axis=-1).astype(vg.dtype)
        o = jnp.einsum('bqgjk,bqkgd->bqgjd', p, vg)
        return o.reshape(bsz, Q_BLOCK, ATTN_WIDTH)

    starts = jnp.arange(nb) * Q_BLOCK
    out = lax.map(block, (blockify(q), blockify(qi), blockify(wi), starts))
    return jnp.moveaxis(out, 0, 1).reshape(bsz, L, ATTN_WIDTH)

def causal_depthwise_conv(x, w, b):
    y = lax.conv_general_dilated(x, w[:, None, :].astype(x.dtype), window_strides=(1,),
                                 padding=[(SSD_CONV - 1, 0)], dimension_numbers=('NWC', 'WIO', 'NWC'),
                                 feature_group_count=x.shape[-1])
    return y + b

def ssd_mixer(z, xbc, dt_raw, conv_w, conv_b, dt_bias, a_log, d_skip, norm_g):
    bsz, L, _ = xbc.shape
    f32 = jnp.float32
    hpg = SSD_HEADS // SSD_GROUPS
    nc = L // SSD_CHUNK
    xbc = jax.nn.silu(causal_depthwise_conv(xbc, conv_w, conv_b))
    xs, bm, cm = jnp.split(xbc, [SSD_WIDTH, SSD_WIDTH + SSD_GROUPS * SSD_STATE], axis=-1)
    x5 = xs.reshape(bsz, nc, SSD_CHUNK, SSD_GROUPS, hpg, SSD_HEAD_DIM).astype(f32)
    bm = bm.reshape(bsz, nc, SSD_CHUNK, SSD_GROUPS, SSD_STATE).astype(f32)
    cm = cm.reshape(bsz, nc, SSD_CHUNK, SSD_GROUPS, SSD_STATE).astype(f32)
    dt = jax.nn.softplus(dt_raw.astype(f32) + dt_bias.astype(f32))
    dt = dt.reshape(bsz, nc, SSD_CHUNK, SSD_GROUPS, hpg)
    a = -jnp.exp(a_log.astype(f32)).reshape(SSD_GROUPS, hpg)
    acs = jnp.cumsum(jnp.moveaxis(dt * a, 2, -1), axis=-1)
    xdt = x5 * dt[..., None]
    idx = jnp.arange(SSD_CHUNK)
    causal = idx[:, None] >= idx[None, :]
    seg = acs[..., :, None] - acs[..., None, :]
    lmat = jnp.exp(jnp.where(causal, seg, -jnp.inf))
    cb = jnp.einsum('bclgn,bcsgn->bcgls', cm, bm)
    y_diag = jnp.einsum('bcgls,bcgjls,bcsgjp->bclgjp', cb, lmat, xdt)
    decay_states = jnp.exp(acs[..., -1:] - acs)
    states = jnp.einsum('bclgn,bcgjl,bclgjp->bcgjpn', bm, decay_states, xdt)
    chunk_decay = jnp.exp(acs[..., -1])

    def step(h, inp):
        st, dec = inp
        return h * dec[..., None, None] + st, h

    h0 = jnp.zeros_like(states[:, 0])
    _, prev = lax.scan(step, h0, (jnp.moveaxis(states, 1, 0), jnp.moveaxis(chunk_decay, 1, 0)))
    prev = jnp.moveaxis(prev, 0, 1)
    y_off = jnp.einsum('bclgn,bcgjpn,bcgjl->bclgjp', cm, prev, jnp.exp(acs))
    y = y_diag + y_off + x5 * d_skip.astype(f32).reshape(SSD_GROUPS, hpg)[..., None]
    y = y.reshape(bsz, L, SSD_WIDTH) * jax.nn.silu(z.astype(f32))
    yg = y.reshape(bsz, L, SSD_GROUPS, SSD_WIDTH // SSD_GROUPS)
    yg = yg * lax.rsqrt(jnp.mean(yg * yg, -1, keepdims=True) + RMS_EPS)
    return (yg.reshape(bsz, L, SSD_WIDTH) * norm_g.astype(f32)).astype(z.dtype)

def memory_attention(q, k, v):
    logits = jnp.einsum('blhd,bmhd->bhlm', q, k).astype(jnp.float32) * (HEAD_DIM ** -0.5)
    p = jax.nn.softmax(logits, axis=-1).astype(v.dtype)
    return jnp.einsum('bhlm,bmhd->blhd', p, v)

def nrm(k, shape, scale):
    return jax.random.normal(k, shape, jnp.float32) * scale

def setup_inputs(seed: int = 0) -> dict:
    key = jax.random.key(seed)
    ks = list(jax.random.split(key, 32))
    nd = DEPTH
    G, P, H = S5_GROUPS, S5_STATE, S5_GROUP
    x = nrm(ks[0], (BATCH, SEQ, D_MODEL), 1.0)
    mem = nrm(ks[1], (BATCH, MEM_LEN, D_MODEL), 1.0)
    positions = (jax.random.randint(ks[2], (BATCH, 1), 0, 4096) + jnp.arange(SEQ)[None, :]).astype(jnp.int32)
    w_in = nrm(ks[3], (nd, D_MODEL, IN_WIDTH), D_MODEL ** -0.5)
    b_gate = nrm(ks[4], (nd, N_BRANCH * D_MODEL), 0.02)
    s5_lam_re = -0.5 + nrm(ks[5], (nd, G, P), 0.01)
    s5_lam_im = math.pi * jnp.arange(P, dtype=jnp.float32) + nrm(ks[6], (nd, G, P), 0.01)
    s5_log_dt = jax.random.uniform(ks[7], (nd, G), jnp.float32, math.log(1e-3), math.log(1e-1))
    s5_b_re = nrm(ks[8], (nd, G, P, H), (2 * H) ** -0.5)
    s5_b_im = nrm(ks[9], (nd, G, P, H), (2 * H) ** -0.5)
    s5_c_re = nrm(ks[10], (nd, G, H, P), (2 * P) ** -0.5)
    s5_c_im = nrm(ks[11], (nd, G, H, P), (2 * P) ** -0.5)
    s5_d = nrm(ks[12], (nd, G, H), 1.0)
    s5_w_glu = nrm(ks[13], (nd, S5_WIDTH, S5_WIDTH), S5_WIDTH ** -0.5)
    s5_b_glu = nrm(ks[14], (nd, S5_WIDTH), 0.02)
    ssd_conv_w = nrm(ks[15], (nd, SSD_CONV, SSD_XBC), SSD_CONV ** -0.5)
    ssd_conv_b = nrm(ks[16], (nd, SSD_XBC), 0.02)
    dt0 = jnp.exp(jax.random.uniform(ks[17], (nd, SSD_HEADS), jnp.float32, math.log(1e-3), math.log(1e-1)))
    ssd_dt_bias = dt0 + jnp.log(-jnp.expm1(-dt0))
    ssd_a_log = jnp.log(jax.random.uniform(ks[18], (nd, SSD_HEADS), jnp.float32, 1.0, 16.0))
    ssd_d = 1.0 + nrm(ks[19], (nd, SSD_HEADS), 0.1)
    ssd_norm_g = 1.0 + nrm(ks[20], (nd, SSD_WIDTH), 0.02)
    mem_w_kv = nrm(ks[21], (nd, D_MODEL, 2 * MEM_WIDTH), D_MODEL ** -0.5)
    w_br_s5 = nrm(ks[22], (nd, S5_WIDTH, D_MODEL), S5_WIDTH ** -0.5)
    w_br_attn = nrm(ks[23], (nd, ATTN_WIDTH, D_MODEL), ATTN_WIDTH ** -0.5)
    w_br_ssd = nrm(ks[24], (nd, SSD_WIDTH, D_MODEL), SSD_WIDTH ** -0.5)
    w_br_mem = nrm(ks[25], (nd, MEM_WIDTH, D_MODEL), MEM_WIDTH ** -0.5)
    w_out = nrm(ks[26], (nd, D_MODEL, D_MODEL), DEEPNORM_BETA * D_MODEL ** -0.5)
    ln_g = 1.0 + nrm(ks[27], (nd, D_MODEL), 0.02)
    ln_b = nrm(ks[28], (nd, D_MODEL), 0.02)
    return {"x": x, "mem": mem, "positions": positions, "w_in": w_in, "b_gate": b_gate,
            "s5_lam_re": s5_lam_re, "s5_lam_im": s5_lam_im, "s5_log_dt": s5_log_dt,
            "s5_b_re": s5_b_re, "s5_b_im": s5_b_im, "s5_c_re": s5_c_re, "s5_c_im": s5_c_im,
            "s5_d": s5_d, "s5_w_glu": s5_w_glu, "s5_b_glu": s5_b_glu,
            "ssd_conv_w": ssd_conv_w, "ssd_conv_b": ssd_conv_b, "ssd_dt_bias": ssd_dt_bias,
            "ssd_a_log": ssd_a_log, "ssd_d": ssd_d, "ssd_norm_g": ssd_norm_g,
            "mem_w_kv": mem_w_kv, "w_br_s5": w_br_s5, "w_br_attn": w_br_attn,
            "w_br_ssd": w_br_ssd, "w_br_mem": w_br_mem, "w_out": w_out,
            "ln_g": ln_g, "ln_b": ln_b}

def reference(x, mem, positions, w_in, b_gate, s5_lam_re, s5_lam_im, s5_log_dt, s5_b_re, s5_b_im,
              s5_c_re, s5_c_im, s5_d, s5_w_glu, s5_b_glu, ssd_conv_w, ssd_conv_b, ssd_dt_bias,
              ssd_a_log, ssd_d, ssd_norm_g, mem_w_kv, w_br_s5, w_br_attn, w_br_ssd, w_br_mem,
              w_out, ln_g, ln_b):
    bsz, L, _ = x.shape
    idx_scale = (IDX_HEADS ** -0.5) * (IDX_DIM ** -0.5)
    for i in range(DEPTH):
        p = split_columns(x @ w_in[i])
        y_s5 = s5_mixer(p['s5_u'], s5_lam_re[i], s5_lam_im[i], s5_log_dt[i], s5_b_re[i], s5_b_im[i],
                        s5_c_re[i], s5_c_im[i], s5_d[i], s5_w_glu[i], s5_b_glu[i])
        y_s5 = y_s5 * jax.nn.silu(p['s5_z'])
        q = partial_rope(p['att_q'].reshape(bsz, L, ATTN_HEADS, HEAD_DIM), positions)
        k = partial_rope(p['att_k'].reshape(bsz, L, ATTN_KV_HEADS, HEAD_DIM), positions)
        v = p['att_v'].reshape(bsz, L, ATTN_KV_HEADS, HEAD_DIM)
        qi = partial_rope(p['idx_q'].reshape(bsz, L, IDX_HEADS, IDX_DIM), positions)
        ki = partial_rope(p['idx_k'].reshape(bsz, L, 1, IDX_DIM), positions)[:, :, 0]
        wi = p['idx_w'] * idx_scale
        y_att = dsa_attention(q, k, v, qi, ki, wi) * jax.nn.silu(p['att_z'])
        y_ssd = ssd_mixer(p['ssd_z'], p['ssd_xbc'], p['ssd_dt'], ssd_conv_w[i], ssd_conv_b[i],
                          ssd_dt_bias[i], ssd_a_log[i], ssd_d[i], ssd_norm_g[i])
        mk, mv = jnp.split(mem @ mem_w_kv[i], 2, axis=-1)
        y_mem = memory_attention(p['mem_q'].reshape(bsz, L, MEM_HEADS, HEAD_DIM),
                                 mk.reshape(bsz, MEM_LEN, MEM_HEADS, HEAD_DIM),
                                 mv.reshape(bsz, MEM_LEN, MEM_HEADS, HEAD_DIM)).reshape(bsz, L, MEM_WIDTH)
        y_mem = y_mem * jax.nn.silu(p['mem_z'])
        g = jax.nn.sigmoid(p['gates'] + b_gate[i]).reshape(bsz, L, N_BRANCH, D_MODEL)
        merged = (g[:, :, 0] * (y_s5 @ w_br_s5[i]) + g[:, :, 1] * (y_att @ w_br_attn[i])
                  + g[:, :, 2] * (y_ssd @ w_br_ssd[i]) + g[:, :, 3] * (y_mem @ w_br_mem[i]))
        out = merged @ w_out[i]
        x = layer_norm(DEEPNORM_ALPHA * x + out, ln_g[i], ln_b[i])
    return x


_drawn_inputs = setup_inputs


def setup_inputs(seed=0):
    import zlib

    import numpy as np

    out = dict(_drawn_inputs(seed))
    spreads = {}
    factors = {'mem': 3.453,
     'b_gate': 8.0,
     's5_lam_re': 64.0,
     's5_lam_im': 64.0,
     's5_log_dt': 64.0,
     's5_b_re': 64.0,
     's5_b_im': 64.0,
     's5_c_re': 64.0,
     's5_c_im': 64.0,
     's5_w_glu': 9.722,
     's5_b_glu': 64.0,
     'ssd_conv_b': 8.0,
     'ssd_norm_g': 8.0,
     'mem_w_kv': 3.316,
     'w_br_mem': 3.318}
    for name, (base, spread) in spreads.items():
        noise = np.random.default_rng([zlib.crc32(name.encode()), seed]).standard_normal(out[name].shape)
        drawn = base * np.exp(spread * noise) if base else spread * noise
        out[name] = __import__('jax').numpy.asarray(drawn.astype(out[name].dtype))
    for name, factor in factors.items():
        out[name] = (out[name] * factor).astype(out[name].dtype)
    return out
```

```python
import math
from contextlib import ExitStack

import numpy as np
import concourse.bass as bass
from concourse import mybir

F32 = mybir.dt.float32
I32 = mybir.dt.int32
ALU = mybir.AluOpType
ACT = mybir.ActivationFunctionType
AX = mybir.AxisListType

P = 128
D = 2048
SEQ = 256
DEPTH = 2
KT = D // P
MT = SEQ // P
BANK = 512
S5W, G5, H5, P5 = 512, 32, 16, 64
PAIRS = G5 // 2
Q5 = 4
C5 = SEQ // Q5
HD = 64
AH, AKV, IH = 8, 2, 4
TOPK = 64
SSDW, SSDH, SSDN, SSDG = 1024, 16, 128, 2
XBC = SSDW + 2 * SSDG * SSDN
XT = XBC // P
CONV = 4
MEMH = 4
NB = 4
ROPE = 16
THETA = 500000.0
ALPHA = (2 * DEPTH) ** 0.25
LN_EPS = 1e-5
RMS_EPS = 1e-5
IDX_SCALE = (IH ** -0.5) * (HD ** -0.5)
ATT_SCALE = HD ** -0.5
MASKED = -1e30
TAKEN = -3e38
GELU_C = math.sqrt(2.0 / math.pi)
ROUND = 12582912.0
TWO_PI = (6.28125, 0.0019340515136718750, 1.2556659146e-06)
PI_LO = 3.1415925

UNIT = KT * P
KB = (S5W + AH * HD + SSDW + MEMH * HD) // P
SLOT = KB * P
NSLOT = 3

ROPED = AH + AKV + IH + 1
C_V = ROPED * HD
C_IW = C_V + AKV * HD
C_DT = C_IW + IH
TOKW = C_DT + SSDH
SMALL = TOKW - 2 * BANK

PARAMS = (('lre', PAIRS), ('lim', PAIRS), ('ldt', PAIRS), ('bre', PAIRS * H5), ('bim', PAIRS * H5),
          ('cre', PAIRS * H5), ('cim', PAIRS * H5), ('dsk', PAIRS), ('bglu', S5W // P), ('cw', XT * CONV),
          ('cb', XT), ('dtb', SSDH), ('alog', SSDH), ('dh', SSDH), ('ng', SSDW // P), ('bg', KT * NB))
PW = sum(n for _, n in PARAMS)
PO = {}
_o = 0
for _n, _w in PARAMS:
    PO[_n] = (_o, _o + _w)
    _o += _w

STREAM = ([('u5', i) for i in range(4)] + [('small', 0)] + [('xbc', i) for i in range(XT)]
          + [('tok', i) for i in range(8)] + [('z5', i) for i in range(4)] + [('glu', 0)]
          + [('zssd', i) for i in range(8)] + [('zatt', i) for i in range(4)]
          + [('qmem', i) for i in range(2)] + [('kmem', i) for i in range(2)] + [('zmem', i) for i in range(2)]
          + [('vmem', i) for i in range(2)])
for _d in range(KT):
    STREAM += [('gate', NB * _d + _b) for _b in range(NB)] + [('branch', _d)]
STREAM += [('out', i) for i in range(16)]
AT = {u: n for n, u in enumerate(STREAM)}
WIDTH = {'small': KT * SMALL, 'branch': SLOT}


def build(nc, x, x_t, mem_t, pos, w, par, ln_g, ln_b, out):
    ctx = ExitStack()
    with ctx:
        def sb(name, shape, dt=F32):
            return ctx.enter_context(nc.sbuf_tensor(name, shape, dt))

        sems = []

        def sem(name):
            s = ctx.enter_context(nc.semaphore(name))
            sems.append(s)
            return s

        xT = sb("xT", [P, KT, SEQ])
        ring = sb("ring", [P, NSLOT, SLOT])
        memT = sb("memT", [P, KT, SEQ])
        merged = memT
        yT = sb("yT", [P, KB, SEQ])
        prm = sb("prm", [P, PW])
        ident = sb("ident", [P, P])
        tri = sb("tri", [P, P])
        maskT = sb("maskT", [P, P])
        seen = sb("seen", [P, SEQ])
        ones = sb("ones", [P, P])
        cs = sb("cs", [P, 2, MT, ROPE // 2])
        posi = sb("posi", [P, MT], I32)
        angw = sb("angw", [P, 4, MT * ROPE // 2])
        expo = sb("expo", [P, MT])

        U = sb("U", [P, PAIRS, C5])
        wide = sb("wide", [P, 2 * D])
        W5 = wide[:, :].rearrange("p (r g n) -> p r g n", r=2, g=PAIRS)
        xs = wide[:, 0:D].rearrange("p (m n) -> p m n", m=MT)
        xdt = wide[:, D:2 * D].rearrange("p (m n) -> p m n", m=MT)
        xtok = wide[:, :].rearrange("p (m n) -> p m n", m=MT)
        T5 = sb("T5", [P, PAIRS, P])
        GD = sb("GD", [P, 2, PAIRS, Q5 + 1, 2 * H5])
        BD = sb("BD", [P, 2, PAIRS, 2 * H5])
        ST = sb("ST", [P, C5 + 1, 2, PAIRS])
        y5 = sb("y5", [P, 4, SEQ])
        z5 = sb("z5", [P, 4, SEQ])
        sflat = ST[:, 1:C5 + 1, :, :].rearrange("p c r g -> p (c r g)")
        K5 = sflat[0:32, :]
        zssd = sflat.rearrange("p (m n) -> p m n", m=MT)
        V5 = yT[:, 0:16, :].rearrange("p (r a) t -> p r (a t)", r=2)
        s5s = sb("s5s", [P, 16, PAIRS])
        pw5 = sb("pw5", [P, 3, PAIRS, Q5 + 1])
        sc5 = sb("sc5", [P, 2, 2, PAIRS])
        am5 = sb("am5", [P, 2, 2, PAIRS])

        tok = sb("tok", [P, MT, TOKW])
        ik2 = sb("ik2", [P, MT, 2, HD])
        qkT = sb("qkT", [P, 8, SEQ])
        gflat = GD[:, :, :, :, :].rearrange("p r g j h -> p (r g j h)")
        LG = gflat[:, 0:2 * BANK].rearrange("p (a n) -> p a n", a=2)
        pT = gflat[:, 2 * BANK:4 * BANK].rearrange("p (a n) -> p a n", a=2)
        sco = gflat[:, 2048:2048 + SEQ]
        stm = gflat[:, 2304:2304 + SEQ]
        amask = gflat[:, 2560:2560 + 2 * SEQ].rearrange("p (m n) -> p m n", m=MT)
        top = sb("top", [P, 8])
        wi = sb("wi", [P, MT, IH])
        smx = sb("smx", [P, 3, 2, 4])

        xb = sb("xb", [P, XT, SEQ + CONV - 1])
        xflat = xb[:, :, :].rearrange("p f t -> p (f t)")
        zatt = xflat[:, 0:1024].rearrange("p (f t) -> p f t", f=4)
        qmT = xflat[:, 1024:1536].rearrange("p (f t) -> p f t", f=2)
        kmT = xflat[:, 1536:2048].rearrange("p (f t) -> p f t", f=2)
        zmem = xflat[:, 2048:2560].rearrange("p (f t) -> p f t", f=2)
        vm = xflat[:, 2560:3072].rearrange("p (m n) -> p m n", m=MT)
        cvth = sb("cvth", [P, 4, SEQ])
        cv, th = cvth[:, 0:2, :], cvth[:, 2:4, :]
        mg = cvth[:, :, :].rearrange("p (a b) n -> p a (b n)", a=2)
        Bt = sb("Bt", [P, SSDG, SSDN])
        prev = U[:, :, :].rearrange("p g c -> p (g c)")
        cbT = sb("cbT", [P, MT, SSDG, P])
        seg = sb("seg", [P, 2, BANK])
        rt = seg[:, :, :].rearrange("p a n -> p (a n)")[:, 0:4 * MT * ROPED * ROPE // 2].rearrange(
            "p (i m h f) -> p i m h f", i=4, m=MT, h=ROPED)
        dts = sb("dts", [P, 10, MT, SSDH])
        wconv = sb("wconv", [P, XT * (CONV + 1)])
        rms = sb("rms", [P, 2, MT, SSDG])

        tg = sb("tg", [P, 2, NB, SEQ])
        bgh = sb("bgh", [P, KT * NB + 4])
        lng = tok[:, :, :].rearrange("p m n -> p (m n)")[:, 0:D]
        lnb = qkT[:, :, :].rearrange("p f t -> p (f t)")
        st6 = sb("st6", [P, MT, 4, 6])
        mv = sb("mv", [P, MT, 4])

        gp = [ctx.enter_context(nc.psum_tensor(f"gp{i}", [P, BANK], F32)) for i in range(4)]
        sp = [ctx.enter_context(nc.psum_tensor(f"sp{i}", [P, BANK], F32)) for i in range(4)]

        slot_full = [sem(f"slot_full{i}") for i in range(NSLOT)]
        (units_done, taken, par_in, mem_in, x_in, lng_in, lnb_in, xout, v_step, a_step, g_step,
         disc_arg, disc_act, v5_ready, g5_ready, w5_ps, w5_out, k5_ps, k5_out, k5_diag, t5_out,
         in5_ps, in5_out, scan_done, y5_ps, y5_out, gelu_arg, gelu_t, gelu_done, glu_t, s5_done,
         dt_arg, dt_exp, dt_u, dt_ln, da_done, acs_ps, acs_out, acs_arg, acs_exp,
         conv_done, conv_t, xbc_done, xs_ps, xs_out, cb_ps, cb_out, xdt_done, st_ps, st_out,
         ab_ps, seg_done, seg_exp, m_done, yd_ps, yd_out, yo_ps, yo_out, rms_arg, rms_pow, ys_done, ys_ps, ys_out,
         z_done, rope_done, qk_ps, qk_out, ix_ps, ix_out, lg_ps, lg_out, lg_exp, p_done, pt_ps, pt_out, o_ps, o_out,
         half_done, gate_t, mg_done, ax_done, res_done, var_done, rstd_done, ln_done, xt_ps, xt_out,
         c_in, c_out, c_arg, gd_zero) = [sem(n) for n in (
            "units_done taken par_in mem_in x_in lng_in lnb_in xout v_step a_step g_step "
            "disc_arg disc_act v5_ready g5_ready w5_ps w5_out k5_ps k5_out k5_diag t5_out "
            "in5_ps in5_out scan_done y5_ps y5_out gelu_arg gelu_t gelu_done glu_t s5_done "
            "dt_arg dt_exp dt_u dt_ln da_done acs_ps acs_out acs_arg acs_exp "
            "conv_done conv_t xbc_done xs_ps xs_out cb_ps cb_out xdt_done st_ps st_out "
            "ab_ps seg_done seg_exp m_done yd_ps yd_out yo_ps yo_out rms_arg rms_pow ys_done ys_ps ys_out "
            "z_done rope_done qk_ps qk_out ix_ps ix_out lg_ps lg_out lg_exp p_done pt_ps pt_out o_ps o_out "
            "half_done gate_t mg_done ax_done res_done var_done rstd_done ln_done xt_ps xt_out "
            "c_in c_out c_arg gd_zero").split()]

        def pv(name, rows=P):
            a, b = PO[name]
            return prm[0:rows, a:b]

        def after(eng, s):
            n = [0]

            def link(ins, also=None):
                n[0] += 1
                ins.then_inc(s, 1)
                eng.wait_ge(s, n[0])
            return link

        def signals(eng, step):
            count = {}

            def tell(ins, s):
                count[s.num] = count.get(s.num, 0) + 1
                ins.then_inc(s, 1)
                eng.wait_ge(s, count[s.num])

            return (lambda ins: tell(ins, step)), tell

        def wrap_angle(v, link, src, dst, t, quarter):
            link(v.tensor_scalar(t, src, 1.0 / (2 * math.pi), quarter, ALU.mult, ALU.add))
            link(v.tensor_scalar(t, t, ROUND, None, ALU.add))
            link(v.tensor_scalar(t, t, -ROUND, None, ALU.add))
            link(v.scalar_tensor_tensor(dst, t, -TWO_PI[0], src, ALU.mult, ALU.add))
            for part in TWO_PI[1:]:
                link(v.scalar_tensor_tensor(dst, t, -part, dst, ALU.mult, ALU.add))
            if quarter:
                link(v.tensor_scalar(dst, dst, quarter * 2 * math.pi, PI_LO, ALU.add, ALU.min))
            else:
                link(v.tensor_scalar(dst, dst, PI_LO, None, ALU.min))
            return v.tensor_scalar(dst, dst, -PI_LO, None, ALU.max)

        with nc.Block() as block:
            @block.sync
            def _(s):
                s.dma_start(posi[:], pos).then_inc(c_in, 16)
                s.dma_start(xT[:], x_t).then_inc(x_in, 16)
                s.dma_start(out, x).then_inc(xout, 16)
                s.wait_ge(x_in, 16)
                s.wait_ge(xout, 16)

            @block.gpsimd
            def _(g):
                link = after(g, g_step)
                link(g.memset(ident[:], 0.0))
                link(g.affine_select(out=ident[:], in_=ident[:], compare_op=ALU.not_equal, fill=1.0, base=0,
                                     pattern=[[-1, P]], channel_multiplier=1))
                link(g.memset(ones[:], 1.0))
                link(g.affine_select(out=tri[:], in_=ones[:], compare_op=ALU.is_ge, fill=0.0, base=0,
                                     pattern=[[1, P]], channel_multiplier=-1))
                link(g.memset(maskT[:], 0.0))
                link(g.affine_select(out=maskT[:], in_=maskT[:], compare_op=ALU.is_ge, fill=MASKED, base=0,
                                     pattern=[[1, P]], channel_multiplier=-1))
                link(g.memset(seen[:], 0.0))
                link(g.affine_select(out=seen[:, P:SEQ], in_=seen[:, P:SEQ], compare_op=ALU.is_ge, fill=MASKED,
                                     base=0, pattern=[[-1, P]], channel_multiplier=1))
                link(g.memset(expo[:], -0.5))
                link(g.memset(T5[:], 0.0))
                link(g.memset(BD[:], 0.0))
                link(g.memset(ST[:], 0.0))

            @block.vector
            def _(v):
                link = after(v, v_step)
                inv = angw[:, 3, 0:ROPE // 2]
                for i in range(ROPE // 2):
                    last = v.memset(angw[:, 3, i:i + 1], float(np.float32(THETA) ** np.float32(-i * 2.0 / ROPE)))
                link(last)
                v.wait_ge(c_in, 16)
                link(v.tensor_copy(mv[:, :, 0], posi[:]))
                ang = angw[:, 0, :].rearrange("p (m f) -> p m f", m=MT)
                link(v.tensor_tensor(ang, mv[:, :, 0:1].to_broadcast([P, MT, ROPE // 2]),
                                     inv.unsqueeze(1).to_broadcast([P, MT, ROPE // 2]), ALU.mult))
                link(wrap_angle(v, link, angw[:, 0, :], cs[:, 0].rearrange("p m f -> p (m f)"), angw[:, 1, :], 0.25))
                wrap_angle(v, link, angw[:, 0, :], cs[:, 1].rearrange("p m f -> p (m f)"), angw[:, 1, :],
                           0.0).then_inc(c_arg, 1)

            @block.scalar
            def _(a):
                a.wait_ge(c_arg, 1)
                a.activation(cs[:], cs[:], ACT.Sin).then_inc(c_out, 1)
                a.wait_ge(c_out, 1)

        first, last_sem = min(s.num for s in sems), max(s.num for s in sems)
        clear = range(first, last_sem + 1)
        nc.multi_engine_barrier(mybir.ALL_ENGINES, sems_to_clear=clear)

        JOBS = ([('u5', i, 1) for i in range(4)] + [('small', 0, 2)] + [('xbc', i, 1) for i in range(XT)]
                + [('tok', 0, 2), ('tok', 1, 2)] + [('z5', i, 1) for i in range(4)]
                + [('zssd', 0, 2), ('zssd', 1, 2)] + [('zatt', i, 1) for i in range(4)]
                + [('qmem', i, 1) for i in range(2)] + [('kmem', i, 1) for i in range(2)]
                + [('zmem', i, 1) for i in range(2)] + [('vmem', 0, 2)])
        START = {}
        nbank = 0
        for name, i, b in JOBS:
            START[name, i] = nbank
            nbank += b
        NPROJ = nbank
        LAST = {('small', 0): AT['small', 0], ('tok', 0): AT['tok', 3], ('tok', 1): AT['tok', 7],
                ('zssd', 0): AT['zssd', 3], ('zssd', 1): AT['zssd', 7], ('vmem', 0): AT['vmem', 1]}

        BATCH = ([(True, 0, [(2 * j, 0), (2 * j + 1, 0), (2 * j, 1), (2 * j + 1, 1)]) for j in range(2)]
                 + [(True, 1, [(j, 0), (j, 1)]) for j in range(4)]
                 + [(False, qb, [(j, 0), (j, 1)]) for qb in range(MT) for j in range(2)])
        KOF = [(0, 4), (4, 8), (8, 16), (16, 18)]

        def keys_of(b):
            sparse, qb, _ = BATCH[b]
            return P if sparse and qb == 0 else SEQ

        def steps(c):
            return slice(CONV - 1 + c * P, CONV - 1 + (c + 1) * P)

        dt, da, acs, eacs, dec = (dts[:, i] for i in range(5))
        xdd = mg[:, :, :].rearrange("p a n -> p (a n)")

        with nc.Fori(0, DEPTH) as layer:
            with nc.Block() as block:
                @block.sync
                def _(s):
                    s.dma_start(prm[:], par[bass.ds(layer, 1)].rearrange("a p n -> p (a n)")).then_inc(par_in, 16)
                    for n, (kind, i) in enumerate(STREAM):
                        if n >= NSLOT:
                            s.wait_ge(units_done, n - NSLOT + 1)
                        wd = WIDTH.get(kind, UNIT)
                        src = w[kind][bass.ds(layer, 1), i].rearrange("a p n -> p (a n)")
                        s.dma_start(ring[:, n % NSLOT, 0:wd], src).then_inc(slot_full[n % NSLOT], 16)
                        if n == 3:
                            s.dma_start(memT[:], mem_t).then_inc(mem_in, 16)
                        if n == AT['gate', NSLOT + 1]:
                            s.wait_ge(ys_ps, 4)
                            s.dma_start(xtok, out.rearrange("(m p) n -> p m n", p=P)).then_inc(x_in, 16)
                            s.wait_ge(o_ps, len(BATCH))
                            s.dma_start(lng, ln_g[bass.ds(layer, 1)].to_broadcast([P, D])).then_inc(lng_in, 16)
                            s.dma_start(lnb, ln_b[bass.ds(layer, 1)].to_broadcast([P, D])).then_inc(lnb_in, 16)
                    for m in range(MT):
                        s.wait_ge(ln_done, m + 1)
                        s.dma_start(out[m * P:(m + 1) * P, :], xtok[:, m, :]).then_inc(xout, 16)
                    s.wait_ge(xout, 16 * MT)

                @block.gpsimd
                def _(g):
                    link = after(g, g_step)
                    g.memset(GD[:], 0.0).then_inc(gd_zero, 1)
                    g.wait_ge(in5_out, 4)
                    for c in range(C5):
                        g.tensor_tensor(sc5[:, 0], ST[:, c, :, :], am5[:, 0], ALU.mult)
                        link(g.tensor_tensor(sc5[:, 1], ST[:, c, ::-1, :], am5[:, 1], ALU.mult))
                        link(g.tensor_tensor(sc5[:, 0], sc5[:, 0], sc5[:, 1], ALU.add))
                        link(g.tensor_tensor(ST[:, c + 1], ST[:, c + 1], sc5[:, 0], ALU.add))
                    g.memset(sc5[:, 0], 0.0).then_inc(scan_done, 1)
                    g.wait_ge(rms_arg, 1)
                    g.tensor_tensor(rms[:, 1], rms[:, 0], expo[:].unsqueeze(2).to_broadcast([P, MT, SSDG]),
                                    ALU.pow).then_inc(rms_pow, 1)
                    g.wait_ge(x_in, 16)
                    g.tensor_scalar(xtok, xtok, ALPHA, None, ALU.mult).then_inc(ax_done, 1)
                    for m in range(MT):
                        g.wait_ge(var_done, m + 1)
                        g.tensor_tensor(mv[:, m, 2:3], mv[:, m, 2:3], expo[:, 0:1], ALU.pow).then_inc(rstd_done, 1)

                @block.tensor
                def _(t):
                    def unit(kind, i=0):
                        n = AT[kind, i]
                        t.wait_ge(slot_full[n % NSLOT], 16 * (n // NSLOT + 1))
                        return ring[:, n % NSLOT, :]

                    def bank_free(n):
                        if n >= 4:
                            t.wait_ge(taken, n - 3)

                    def proj_t(kind, i, moving=xT):
                        b = START[kind, i]
                        wt = unit(kind, i)
                        bank_free(b)
                        for k in range(KT):
                            mm = t.matmul(gp[b % 4][:, 0:SEQ], wt[:, k * P:(k + 1) * P], moving[:, k, :],
                                          start=k == 0, stop=k == KT - 1)
                        mm.then_inc(units_done, 1)

                    def proj_m(kind, i, n, cols, src=xT):
                        b = START[kind, i]
                        per = KT // n
                        bank_free(b + 1)
                        for j in range(n):
                            wt = unit(kind, i * n + j)
                            for m in range(MT):
                                for k in range(per):
                                    kk = j * per + k
                                    mm = t.matmul(gp[(b + m) % 4][:, 0:cols], src[:, kk, m * P:(m + 1) * P],
                                                  wt[:, k * cols:(k + 1) * cols], start=kk == 0, stop=kk == KT - 1)
                            mm.then_inc(units_done, 1)

                    def four(out_bank, tiles, done):
                        for j, tile in enumerate(tiles):
                            mm = t.transpose(out_bank[:, j * P:(j + 1) * P], tile, ident[:])
                        mm.then_inc(done, 1)

                    for i in range(4):
                        proj_t('u5', i)
                    proj_m('small', 0, 1, SMALL)
                    t.wait_ge(v5_ready, 1)
                    for r in range(2):
                        for q in range(4):
                            if r:
                                t.wait_ge(w5_out, q + 1)
                            four(sp[q], [V5[:, r, gi * P:(gi + 1) * P] for gi in range(4 * q, 4 * q + 4)], w5_ps)
                    t.wait_ge(g5_ready, 1)
                    for q in range(4):
                        t.wait_ge(w5_out, 5 + q)
                        for j in range(4):
                            gi = 4 * q + j
                            for r in range(2):
                                mm = t.matmul(sp[q][0:32, j * P:(j + 1) * P], BD[:, r, gi, :],
                                              GD[:, r, gi, 0:Q5, :].rearrange("p j h -> p (j h)"),
                                              start=r == 0, stop=r == 1)
                        mm.then_inc(k5_ps, 1)
                    for i in range(0, 6):
                        proj_t('xbc', i)
                    t.wait_ge(taken, 4)
                    t.wait_ge(k5_out, 4)
                    for q in range(4):
                        r, half = q % 2, q // 2
                        for j in range(8):
                            gi = 8 * half + j
                            mm = t.matmul(sp[q][:, j * C5:(j + 1) * C5], W5[:, r, gi, :], U[:, gi, :],
                                          start=True, stop=True)
                        mm.then_inc(in5_ps, 1)
                    for i in range(6, XT):
                        proj_t('xbc', i)
                    for i in range(2):
                        proj_m('tok', i, 4, BANK)
                    t.wait_ge(da_done, 1)
                    t.wait_ge(in5_out, 4)
                    t.matmul(sp[0][:, 0:MT * SSDH], tri[:], da.rearrange("p m h -> p (m h)"), start=True, stop=True)
                    t.matmul(sp[0][:, 64:64 + SSDH], ones[:], da[:, 0, :], start=True, stop=True).then_inc(acs_ps, 1)
                    t.wait_ge(xbc_done, XT)
                    for c in range(MT):
                        for g in range(SSDG):
                            n = c * SSDG + g
                            mm = t.matmul(sp[1][:, n * P:(n + 1) * P], xb[:, 8 + g, steps(c)],
                                          xb[:, 10 + g, steps(c)], start=True, stop=True)
                    mm.then_inc(cb_ps, 1)
                    for n in range(5):
                        if n >= 2:
                            t.wait_ge(xs_out, n - 1)
                        four(sp[2 + n % 2], [xb[:, 4 * (n % 2) + j, steps(n // 2)] for j in range(4)] if n < 4 else
                             [xb[:, 8 + g, steps(0)] for g in range(SSDG)], xs_ps)
                    for i in range(4):
                        proj_t('z5', i)
                    t.wait_ge(scan_done, 1)
                    t.wait_ge(t5_out, 1)
                    t.wait_ge(xs_out, 5)
                    for half in range(2):
                        for j in range(8):
                            gi = 8 * half + j
                            o = sp[2 + half][:, j * C5:(j + 1) * C5]
                            t.matmul(o, T5[:, gi, :], U[:, gi, :], start=True, stop=False)
                            for r in range(2):
                                mm = t.matmul(o, GD[:, r, gi, 1:Q5 + 1, :].rearrange("p j h -> p (j h)"),
                                              ST[:, 0:C5, r, gi], start=False, stop=r == 1)
                        mm.then_inc(y5_ps, 1)
                    t.wait_ge(rope_done, 1)
                    t.wait_ge(cb_out, 1)
                    t.wait_ge(acs_arg, 1)
                    for n in range(4):
                        m, h = n // 2, n % 2
                        if n >= 2:
                            t.wait_ge(qk_out, n - 1)
                        four(sp[n % 2], [tok[:, m, f * P:(f + 1) * P] if f < 7 else
                                         ik2[:, m].rearrange("p a e -> p (a e)")
                                         for f in range(4 * h, 4 * h + 4)], qk_ps)
                    t.wait_ge(gelu_done, 1)
                    wt = unit('glu')
                    t.wait_ge(y5_out, 2)
                    for j in range(4):
                        for k in range(4):
                            mm = t.matmul(sp[2 + j // 2][:, (j % 2) * SEQ:(j % 2 + 1) * SEQ],
                                          wt[:, k * BANK + j * P:k * BANK + (j + 1) * P], y5[:, k, :],
                                          start=k == 0, stop=k == 3)
                    mm.then_inc(units_done, 1)
                    t.wait_ge(qk_out, 4)
                    for qb in range(MT):
                        nk = (qb + 1) * P
                        if qb:
                            t.wait_ge(ix_out, 1)
                        for h in range(IH):
                            r = slice(HD * (h % 2), HD * (h % 2 + 1))
                            mm = t.matmul(sp[h % 2][:, (h // 2) * SEQ:(h // 2) * SEQ + nk],
                                          qkT[r, 5 + h // 2, qb * P:(qb + 1) * P], qkT[r, 7, 0:nk],
                                          start=True, stop=True)
                        mm.then_inc(ix_ps, 1)
                    for i in range(2):
                        proj_m('zssd', i, 4, BANK)
                    t.wait_ge(xdt_done, 1)
                    t.wait_ge(xs_out, 5)
                    t.wait_ge(glu_t, 4)
                    for g in range(SSDG):
                        t.matmul(sp[2 + g][:], Bt[:, g, :], xdd[:, g * BANK:(g + 1) * BANK], start=True,
                                 stop=True).then_inc(st_ps, 1)
                    t.wait_ge(ix_out, 2)

                    def diag(n):
                        c, rd = n // 4, n % 4
                        t.wait_ge(m_done, n + 1)
                        for j in range(4):
                            h = 4 * rd + j
                            mm = t.matmul(sp[2 + h // 8][:, (h % 8) * HD:(h % 8 + 1) * HD],
                                          seg[:, n % 2, j * P:(j + 1) * P], xdt[:, c, h * HD:(h + 1) * HD],
                                          start=True, stop=True)
                        mm.then_inc(yd_ps, 1)

                    t.wait_ge(st_out, 2)
                    for n in range(8):
                        if n:
                            t.wait_ge(seg_done, n)
                        for j in range(4):
                            h = 4 * (n % 4) + j
                            mm = t.matmul(sp[0][:, j * P:(j + 1) * P], da[:, n // 4, h:h + 1].to_broadcast([P, P]),
                                          tri[:], start=True, stop=True)
                        mm.then_inc(ab_ps, 1)
                        if n == 5:
                            t.wait_ge(yd_out, 2)
                        if n:
                            diag(n - 1)
                    for g in range(SSDG):
                        if g:
                            t.wait_ge(yo_out, 1)
                        t.matmul(sp[1][:], xb[:, 10 + g, steps(1)], prev[:, g * BANK:(g + 1) * BANK],
                                 start=True, stop=True).then_inc(yo_ps, 1)
                    diag(7)
                    for i in range(4):
                        proj_t('zatt', i)
                    for i in range(2):
                        proj_t('qmem', i)
                    t.wait_ge(mem_in, 16)
                    for i in range(2):
                        proj_t('kmem', i, memT)
                    for i in range(2):
                        proj_t('zmem', i)
                    proj_m('vmem', 0, 2, MEMH * HD, memT)
                    t.wait_ge(yd_out, 4)
                    for n in range(4):
                        t.wait_ge(ys_done, n // 2 + 1)
                        if n >= 2:
                            t.wait_ge(ys_out, n - 1)
                        h = 4 * (n % 2)
                        four(sp[2 + n % 2], [xs[:, n // 2, (h + j) * P:(h + j + 1) * P] for j in range(4)], ys_ps)
                    t.wait_ge(ys_out, 4)
                    t.wait_ge(yo_out, 2)
                    t.wait_ge(taken, NPROJ)

                    def logits(b):
                        sparse, qb, heads = BATCH[b]
                        nk = keys_of(b)
                        if b >= 2:
                            t.wait_ge(lg_out, b - 1)
                        for n, (f, half) in enumerate(heads):
                            r = slice(HD * half, HD * (half + 1))
                            q = (qkT if sparse else qmT)[r, f, qb * P:(qb + 1) * P]
                            k = qkT[r, 4, 0:nk] if sparse else kmT[r, f, 0:nk]
                            c = (n % (len(heads) // 2)) * nk
                            mm = t.matmul(gp[2 * (b % 2) + half][:, c:c + nk], q, k, start=True, stop=True)
                        mm.then_inc(lg_ps, 1)

                    logits(0)
                    for b, (sparse, qb, heads) in enumerate(BATCH):
                        if b + 1 < len(BATCH):
                            logits(b + 1)
                        t.wait_ge(p_done, b + 1)
                        if b:
                            t.wait_ge(pt_out, b)
                        four(sp[2], [LG[:, b % 2, j * P:(j + 1) * P] for j in range(4)], pt_ps)
                        t.wait_ge(pt_out, b + 1)
                        if b:
                            t.wait_ge(o_out, b)
                        tiles = keys_of(b) // P
                        for n, (f, half) in enumerate(heads):
                            for s in range(tiles):
                                v = (tok[:, s, C_V + half * HD:C_V + (half + 1) * HD] if sparse else
                                     vm[:, s, (2 * f + half) * HD:(2 * f + half + 1) * HD])
                                blk = n * tiles + s
                                o = n % (len(heads) // 2)
                                mm = t.matmul(sp[3][HD * half:HD * (half + 1), o * P:(o + 1) * P], v,
                                              pT[:, b % 2, blk * P:(blk + 1) * P], start=s == 0, stop=s == tiles - 1)
                        mm.then_inc(o_ps, 1)
                    t.wait_ge(s5_done, 1)
                    t.wait_ge(o_out, len(BATCH))
                    for d in range(KT):
                        pair = 2 * (d % 2)
                        for b in range(NB):
                            wt = unit('gate', NB * d + b)
                            if b == 0 and d >= 2:
                                t.wait_ge(gate_t, NB * (d - 1))
                            for k in range(KT):
                                mm = t.matmul(gp[pair + b // 2][:, (b % 2) * SEQ:(b % 2 + 1) * SEQ],
                                              wt[:, k * P:(k + 1) * P], xT[:, k, :], start=k == 0, stop=k == KT - 1)
                            mm.then_inc(units_done, 1)
                        wt = unit('branch', d)
                        if d >= 2:
                            t.wait_ge(mg_done, d - 1)
                        for b, (lo, hi) in enumerate(KOF):
                            for k in range(lo, hi):
                                mm = t.matmul(sp[pair + b // 2][:, (b % 2) * SEQ:(b % 2 + 1) * SEQ],
                                              wt[:, k * P:(k + 1) * P], yT[:, k, :], start=k == lo, stop=k == hi - 1)
                        mm.then_inc(units_done, 1)
                    t.wait_ge(mg_done, KT)
                    t.wait_ge(gate_t, NB * KT)
                    for c in range(4):
                        for j in range(4):
                            wt = unit('out', 4 * c + j)
                            for m in range(MT):
                                if j == 0 and c >= 2:
                                    t.wait_ge(res_done, 2 * (c - 2) + m + 1)
                                for k in range(4):
                                    kk = 4 * j + k
                                    mm = t.matmul(gp[2 * (c % 2) + m][:], merged[:, kk, m * P:(m + 1) * P],
                                                  wt[:, k * BANK:(k + 1) * BANK], start=kk == 0, stop=kk == KT - 1)
                            mm.then_inc(units_done, 1)
                    for n in range(8):
                        m, q = n // 4, n % 4
                        t.wait_ge(ln_done, m + 1)
                        if n >= 4:
                            t.wait_ge(xt_out, n - 3)
                        four(sp[q], [xtok[:, m, f * P:(f + 1) * P] for f in range(4 * q, 4 * q + 4)], xt_ps)

                @block.scalar
                def _(a):
                    def done(kind, i=0):
                        a.wait_ge(units_done, LAST.get((kind, i), AT[kind, 0] + i) + 1)
                        return START[kind, i]

                    def copy(o, i, **k):
                        return a.activation(o, i, ACT.Copy, **k)

                    a.wait_ge(par_in, 16)
                    a.activation(s5s[:, 0], pv('ldt'), ACT.Exp).then_inc(disc_act, 1)
                    a.wait_ge(disc_arg, 1)
                    a.activation(s5s[:, 1], s5s[:, 1], ACT.Exp)
                    a.activation(dts[:, 5, 0], pv('alog'), ACT.Exp).then_inc(a_step, 1)
                    a.activation(s5s[:, 3:5], s5s[:, 3:5], ACT.Sin).then_inc(disc_act, 1)
                    for i in range(4):
                        b = done('u5', i)
                        for pr in range(4):
                            src = gp[b % 4][32 * pr:32 * pr + 32, 0:SEQ].rearrange("p (c q) -> p q c", q=Q5)
                            for q in range(Q5):
                                ins = copy(U[32 * q:32 * q + 32, 4 * i + pr, :], src[:, q, :])
                        ins.then_inc(taken, 1)
                    b = done('small')
                    for m in range(MT):
                        copy(tok[:, m, 2 * BANK:TOKW], gp[(b + m) % 4][:, 0:SMALL]).then_inc(taken, 1)
                    a.wait_ge(dt_arg, 1)
                    a.activation(dts[:, 6], dts[:, 6], ACT.Exp).then_inc(dt_exp, 1)
                    for n in range(8):
                        a.wait_ge(w5_ps, n + 1)
                        copy(W5[:, n // 4, 4 * (n % 4):4 * (n % 4) + 4, :],
                             sp[n % 4][:].rearrange("p (g n) -> p g n", g=4)).then_inc(w5_out, 1)
                    for q in range(4):
                        a.wait_ge(k5_ps, q + 1)
                        copy(K5[:, q * BANK:(q + 1) * BANK], sp[q][0:32, :]).then_inc(k5_out, 1)
                    a.wait_ge(dt_u, 1)
                    a.activation(dts[:, 8], dts[:, 7], ACT.Ln).then_inc(dt_ln, 1)
                    a.wait_ge(k5_diag, 1)
                    k5v = K5.rearrange("p (g n) -> p g n", g=PAIRS)
                    for s in range(Q5):
                        ins = copy(T5[32 * s:32 * s + 32, :, 32 * s:P], k5v[:, :, 0:P - 32 * s])
                    ins.then_inc(t5_out, 1)

                    def xbc_evac(i):
                        b = done('xbc', i)
                        copy(xb[:, i, CONV - 1:], gp[b % 4][:, 0:SEQ]).then_inc(taken, 1)

                    def xbc_tanh(i):
                        a.wait_ge(conv_done, i + 1)
                        if i >= 2:
                            a.wait_ge(xbc_done, i - 1)
                        a.activation(th[:, i % 2], cv[:, i % 2], ACT.Tanh).then_inc(conv_t, 1)

                    for i in range(6):
                        xbc_evac(i)
                        if i:
                            xbc_tanh(i - 1)
                    a.wait_ge(t5_out, 1)
                    for q in range(4):
                        r, half = q % 2, q // 2
                        a.wait_ge(in5_ps, q + 1)
                        copy(ST[:, 1:C5 + 1, r, 8 * half:8 * half + 8],
                             sp[q][:].rearrange("p (g c) -> p c g", g=8)).then_inc(in5_out, 1)
                    for i in range(6, XT):
                        xbc_evac(i)
                        xbc_tanh(i - 1)
                    xbc_tanh(XT - 1)
                    for i in range(2):
                        b = done('tok', i)
                        for m in range(MT):
                            copy(tok[:, m, i * BANK:(i + 1) * BANK], gp[(b + m) % 4][:]).then_inc(taken, 1)
                    a.wait_ge(acs_out, 1)
                    a.activation(eacs, acs, ACT.Exp)
                    a.wait_ge(acs_arg, 1)
                    a.activation(dec[:, 0], dec[:, 0], ACT.Exp).then_inc(acs_exp, 1)
                    for n in range(5):
                        a.wait_ge(xs_ps, n + 1)
                        bank = sp[2 + n % 2]
                        (copy(xs[:, n // 2, (n % 2) * BANK:(n % 2 + 1) * BANK], bank[:]) if n < 4 else
                         copy(Bt[:].rearrange("p g n -> p (g n)"), bank[:, 0:SSDG * P])).then_inc(xs_out, 1)

                    def z_evac(bank, cols, dst, th_dst):
                        copy(dst, bank[:, 0:cols])
                        a.activation(th_dst, bank[:, 0:cols], ACT.Tanh, scale=0.5).then_inc(taken, 1)

                    for i in range(4):
                        b = done('z5', i)
                        z_evac(gp[b % 4], SEQ, z5[:, i, :], tg[:, 0, i, :])
                    for n in range(4):
                        a.wait_ge(qk_ps, n + 1)
                        m, h = n // 2, n % 2
                        copy(qkT[:, 4 * h:4 * h + 4, m * P:(m + 1) * P],
                             sp[n % 2][:].rearrange("p (f t) -> p f t", f=4)).then_inc(qk_out, 1)
                    a.wait_ge(gelu_arg, 1)
                    a.activation(LG.rearrange("p a n -> p (a n)"), LG.rearrange("p a n -> p (a n)"), ACT.Tanh,
                                 scale=GELU_C).then_inc(gelu_t, 1)
                    a.wait_ge(units_done, AT['glu', 0] + 1)
                    a.wait_ge(half_done, 1)
                    for j in range(4):
                        a.activation(pT[:, j // 2, (j % 2) * SEQ:(j % 2 + 1) * SEQ],
                                     sp[2 + j // 2][:, (j % 2) * SEQ:(j % 2 + 1) * SEQ], ACT.Tanh, scale=0.5,
                                     bias=bgh[:, KT * NB + j:KT * NB + j + 1]).then_inc(glu_t, 1)
                    a.wait_ge(z_done, 1)
                    tgf = tg[:].rearrange("p a b n -> p (a b n)").rearrange("p (m n) -> p m n", m=MT)
                    for i in range(2):
                        b = done('zssd', i)
                        for m in range(MT):
                            z_evac(gp[(b + m) % 4], BANK, zssd[:, m, i * BANK:(i + 1) * BANK],
                                   tgf[:, m, i * BANK:(i + 1) * BANK])
                    for g in range(SSDG):
                        a.wait_ge(st_ps, g + 1)
                        copy(prev[:, g * BANK:(g + 1) * BANK], sp[2 + g][:]).then_inc(st_out, 1)
                    for n in range(8):
                        a.wait_ge(seg_done, n + 1)
                        a.activation(seg[:, n % 2], seg[:, n % 2], ACT.Exp).then_inc(seg_exp, 1)
                    a.wait_ge(z_done, 2)
                    for i in range(4):
                        b = done('zatt', i)
                        z_evac(gp[b % 4], SEQ, zatt[:, i, :], tg[:, 0, i, :])
                    for i in range(2):
                        b = done('qmem', i)
                        copy(qmT[:, i, :], gp[b % 4][:, 0:SEQ]).then_inc(taken, 1)
                    for i in range(2):
                        b = done('kmem', i)
                        copy(kmT[:, i, :], gp[b % 4][:, 0:SEQ]).then_inc(taken, 1)
                    for i in range(2):
                        b = done('zmem', i)
                        z_evac(gp[b % 4], SEQ, zmem[:, i, :], tg[:, 1, i, :])
                    b = done('vmem')
                    for m in range(MT):
                        copy(vm[:, m, :], gp[(b + m) % 4][:, 0:MEMH * HD]).then_inc(taken, 1)
                    ng = pv('ng')
                    for n in range(4):
                        a.wait_ge(ys_ps, n + 1)
                        for j in range(4):
                            f = 4 * (n % 2) + j
                            ins = copy(yT[:, 8 + f, (n // 2) * P:(n // 2 + 1) * P], sp[2 + n % 2][:, j * P:(j + 1) * P],
                                       scale=ng[:, f:f + 1])
                        ins.then_inc(ys_out, 1)
                    for b, (sparse, qb, heads) in enumerate(BATCH):
                        nk = keys_of(b)
                        a.wait_ge(lg_out, b + 1)
                        for n in range(len(heads)):
                            v = LG[:, b % 2, n * nk:(n + 1) * nk]
                            ins = a.activation(v, v, ACT.Exp, bias=smx[:, 0, b % 2, n:n + 1],
                                               accum_out=smx[:, 1, b % 2, n:n + 1])
                        ins.then_inc(lg_exp, 1)
                        a.wait_ge(pt_ps, b + 1)
                        if b >= 2:
                            a.wait_ge(o_ps, b - 1)
                        copy(pT[:, b % 2], sp[2][:]).then_inc(pt_out, 1)
                    for d in range(KT):
                        if d >= 2:
                            a.wait_ge(mg_done, d - 1)
                        else:
                            a.wait_ge(z_done, 3)
                        for b in range(NB):
                            a.wait_ge(units_done, AT['gate', NB * d + (b | 1)] + 1)
                            a.activation(tg[:, d % 2, b, :], gp[2 * (d % 2) + b // 2][:, (b % 2) * SEQ:(b % 2 + 1) * SEQ],
                                         ACT.Tanh, scale=0.5,
                                         bias=bgh[:, NB * d + b:NB * d + b + 1]).then_inc(gate_t, 1)
                    for n in range(8):
                        m, q = n // 4, n % 4
                        a.wait_ge(xt_ps, n + 1)
                        copy(xT[:, 4 * q:4 * q + 4, m * P:(m + 1) * P],
                             sp[q][:].rearrange("p (f t) -> p f t", f=4)).then_inc(xt_out, 1)
                    a.wait_ge(xt_out, 8)

                @block.vector
                def _(v):
                    link, tell = signals(v, v_step)
                    tt, ts, stt = v.tensor_tensor, v.tensor_scalar, v.scalar_tensor_tensor

                    v.wait_ge(par_in, 16)
                    lre, lim = pv('lre'), pv('lim')
                    v.wait_ge(disc_act, 1)
                    link(tt(s5s[:, 1], lre, s5s[:, 0], ALU.mult))
                    link(tt(s5s[:, 2], lim, s5s[:, 0], ALU.mult))
                    link(wrap_angle(v, link, s5s[:, 2], s5s[:, 3], s5s[:, 5], 0.25))
                    tell(wrap_angle(v, link, s5s[:, 2], s5s[:, 4], s5s[:, 5], 0.0), disc_arg)
                    v.wait_ge(disc_act, 2)
                    link(tt(s5s[:, 6], s5s[:, 1], s5s[:, 3], ALU.mult))
                    link(tt(s5s[:, 7], s5s[:, 1], s5s[:, 4], ALU.mult))
                    link(tt(s5s[:, 8], lre, lre, ALU.mult))
                    link(tt(s5s[:, 5], lim, lim, ALU.mult))
                    link(tt(s5s[:, 8], s5s[:, 8], s5s[:, 5], ALU.add))
                    link(v.reciprocal(s5s[:, 8], s5s[:, 8]))
                    link(ts(s5s[:, 9], s5s[:, 6], -1.0, None, ALU.add))
                    link(tt(s5s[:, 10], s5s[:, 9], lre, ALU.mult))
                    link(tt(s5s[:, 5], s5s[:, 7], lim, ALU.mult))
                    link(tt(s5s[:, 10], s5s[:, 10], s5s[:, 5], ALU.add))
                    link(tt(s5s[:, 10], s5s[:, 10], s5s[:, 8], ALU.mult))
                    link(tt(s5s[:, 11], s5s[:, 7], lre, ALU.mult))
                    link(tt(s5s[:, 5], s5s[:, 9], lim, ALU.mult))
                    link(tt(s5s[:, 11], s5s[:, 11], s5s[:, 5], ALU.subtract))
                    link(tt(s5s[:, 11], s5s[:, 11], s5s[:, 8], ALU.mult))
                    link(v.memset(pw5[:, 0, :, 0], 1.0))
                    link(v.memset(pw5[:, 1, :, 0], 0.0))
                    link(v.tensor_copy(pw5[:, 0, :, 1], s5s[:, 6]))
                    link(v.tensor_copy(pw5[:, 1, :, 1], s5s[:, 7]))
                    for j in range(2, Q5 + 1):
                        x1, x2 = j // 2, j - j // 2
                        link(tt(s5s[:, 12], pw5[:, 0, :, x1], pw5[:, 0, :, x2], ALU.mult))
                        link(tt(s5s[:, 13], pw5[:, 1, :, x1], pw5[:, 1, :, x2], ALU.mult))
                        link(tt(pw5[:, 0, :, j], s5s[:, 12], s5s[:, 13], ALU.subtract))
                        link(tt(s5s[:, 12], pw5[:, 0, :, x1], pw5[:, 1, :, x2], ALU.mult))
                        link(tt(s5s[:, 13], pw5[:, 1, :, x1], pw5[:, 0, :, x2], ALU.mult))
                        link(tt(pw5[:, 1, :, j], s5s[:, 12], s5s[:, 13], ALU.add))
                    link(ts(pw5[:, 2], pw5[:, 1], -1.0, None, ALU.mult))
                    for i, k in ((0, 0), (1, 0)):
                        link(v.tensor_copy(am5[:, 0, i], pw5[:, k, :, Q5]))
                    link(v.tensor_copy(am5[:, 1, 0], pw5[:, 2, :, Q5]))
                    link(v.tensor_copy(am5[:, 1, 1], pw5[:, 1, :, Q5]))
                    bre = pv('bre').rearrange("p (g h) -> p g h", g=PAIRS)
                    bim = pv('bim').rearrange("p (g h) -> p g h", g=PAIRS)
                    cre = pv('cre').rearrange("p (g h) -> p g h", g=PAIRS)
                    cim = pv('cim').rearrange("p (g h) -> p g h", g=PAIRS)
                    fr = s5s[:, 10].unsqueeze(2).to_broadcast([P, PAIRS, H5])
                    fi = s5s[:, 11].unsqueeze(2).to_broadcast([P, PAIRS, H5])
                    xsf = wide[:, 0:D]
                    gflat1 = sflat
                    gflat2 = tg[:].rearrange("p a b n -> p (a b n)")
                    v.memset(xb[:, :, 0:CONV - 1], 0.0)
                    t1 = xsf[:, 0:PAIRS * H5].rearrange("p (g h) -> p g h", g=PAIRS)
                    t2 = xsf[:, BANK:BANK + PAIRS * H5].rearrange("p (g h) -> p g h", g=PAIRS)
                    for r, (fa, fb, op) in enumerate(((fr, fi, ALU.subtract), (fi, fr, ALU.add))):
                        link(tt(t1, bre, fa, ALU.mult))
                        link(tt(t2, bim, fb, ALU.mult))
                        for h in range(2):
                            rows = slice(P5 * h, P5 * (h + 1))
                            link(tt(BD[rows, r, :, H5 * h:H5 * (h + 1)], t1[rows], t2[rows], op))
                    big = xsf.rearrange("p (g s h) -> p g s h", g=PAIRS, s=Q5)
                    for r in range(2):
                        dst = V5[:, r, :].rearrange("p (g s h) -> p g s h", g=PAIRS, s=Q5)
                        pa, pb = (0, 1) if r == 0 else (1, 0)

                        def pw(k):
                            return pw5[:, k, :, 0:Q5][:, :, ::-1].unsqueeze(3).to_broadcast([P, PAIRS, Q5, 2 * H5])

                        def bd(k):
                            return BD[:, k].unsqueeze(2).to_broadcast([P, PAIRS, Q5, 2 * H5])

                        link(tt(dst, bd(0), pw(pa), ALU.mult))
                        link(tt(big, bd(1), pw(pb), ALU.mult))
                        ins = tt(dst, dst, big, ALU.subtract if r == 0 else ALU.add)
                        if r == 0:
                            link(ins)
                    tell(ins, v5_ready)
                    g1 = gflat1[:, 0:PAIRS * (Q5 + 1) * H5].rearrange("p (g j h) -> p g j h", g=PAIRS, j=Q5 + 1)
                    g2 = gflat2[:, 0:PAIRS * (Q5 + 1) * H5].rearrange("p (g j h) -> p g j h", g=PAIRS, j=Q5 + 1)
                    v.wait_ge(v5_ready, 1)
                    v.wait_ge(gd_zero, 1)
                    full = [P, PAIRS, Q5 + 1, H5]
                    for r, (ka, kb) in enumerate(((0, 1), (2, 0))):
                        link(tt(g1, cre.unsqueeze(2).to_broadcast(full), pw5[:, ka].unsqueeze(3).to_broadcast(full),
                                ALU.mult))
                        link(tt(g2, cim.unsqueeze(2).to_broadcast(full), pw5[:, kb].unsqueeze(3).to_broadcast(full),
                                ALU.mult))
                        for h in range(2):
                            rows = slice(P5 * h, P5 * (h + 1))
                            ins = tt(GD[rows, r, :, :, H5 * h:H5 * (h + 1)], g1[rows], g2[rows], ALU.subtract)
                        if r == 0:
                            link(ins)
                    tell(ins, g5_ready)
                    v.wait_ge(g5_ready, 1)
                    link(ts(bgh[:, 0:KT * NB], pv('bg'), 0.5, None, ALU.mult))
                    tell(ts(bgh[:, KT * NB:], pv('bglu'), 0.5, None, ALU.mult), half_done)
                    link(ts(wconv[:], prm[:, PO['cw'][0]:PO['cb'][1]], 0.5, None, ALU.mult))
                    b = START['small', 0]
                    v.wait_ge(taken, b + 2)
                    link(tt(dts[:, 9], tok[:, :, C_DT:TOKW], pv('dtb').unsqueeze(1).to_broadcast([P, MT, SSDH]),
                            ALU.add))
                    tell(stt(dts[:, 6], dts[:, 9], -1.0, dts[:, 9], ALU.mult, ALU.min), dt_arg)
                    v.wait_ge(dt_exp, 1)
                    tell(ts(dts[:, 7], dts[:, 6], 1.0, None, ALU.add), dt_u)
                    v.wait_ge(dt_u, 1)
                    link(ts(dts[:, 2], dts[:, 7], -1.0, None, ALU.add))
                    link(tt(dts[:, 2], dts[:, 6], dts[:, 2], ALU.subtract))
                    link(v.reciprocal(dts[:, 3], dts[:, 7]))
                    link(tt(dts[:, 2], dts[:, 2], dts[:, 3], ALU.mult))
                    v.wait_ge(k5_out, 4)
                    kd = gflat2[0:32, 0:PAIRS * 32].rearrange("p (g n) -> p g n", g=PAIRS)
                    link(tt(kd, ident[0:32, 0:32].unsqueeze(1).to_broadcast([32, PAIRS, 32]),
                            pv('dsk', 32).unsqueeze(2).to_broadcast([32, PAIRS, 32]), ALU.mult))
                    k0 = K5.rearrange("p (g n) -> p g n", g=PAIRS)[:, :, 0:32]
                    tell(tt(k0, k0, kd, ALU.add), k5_diag)
                    v.wait_ge(dt_ln, 1)
                    link(tt(dts[:, 2], dts[:, 8], dts[:, 2], ALU.add))
                    link(stt(dt, dts[:, 9], 0.0, dts[:, 2], ALU.max, ALU.add))
                    v.wait_ge(a_step, 1)
                    link(tt(da, dt, dts[:, 5, 0].unsqueeze(1).to_broadcast([P, MT, SSDH]), ALU.mult))
                    tell(ts(da, da, -1.0, None, ALU.mult), da_done)

                    def conv(i):
                        v.wait_ge(taken, START['xbc', i] + 1)
                        c = cv[:, i % 2]
                        wc = wconv[:, CONV * i:CONV * (i + 1)]
                        link(ts(c, xb[:, i, 0:SEQ], wc[:, 0:1], wconv[:, XT * CONV + i:XT * CONV + i + 1],
                                ALU.mult, ALU.add))
                        for j in range(1, CONV):
                            ins = stt(c, xb[:, i, j:j + SEQ], wc[:, j:j + 1], c, ALU.mult, ALU.add)
                            if j < CONV - 1:
                                link(ins)
                        tell(ins, conv_done)

                    def silu(i):
                        v.wait_ge(conv_t, i + 1)
                        tell(stt(xb[:, i, CONV - 1:], th[:, i % 2], 1.0, cv[:, i % 2], ALU.add,
                            ALU.mult), xbc_done)

                    for i in range(XT):
                        conv(i)
                        if i:
                            silu(i - 1)
                    silu(XT - 1)
                    v.wait_ge(taken, START['tok', 1] + 2)
                    heads = tok[:, :, 0:ROPED * HD].rearrange("p m (h e) -> p m h e", e=HD)
                    half = ROPE // 2
                    xa, xc = heads[:, :, :, 0:half], heads[:, :, :, half:ROPE]
                    shape = [P, MT, ROPED, half]
                    co = cs[:, 0].unsqueeze(2).to_broadcast(shape)
                    si = cs[:, 1].unsqueeze(2).to_broadcast(shape)
                    for m in range(MT):
                        link(tt(rt[:, 0, m], xa[:, m], co[:, m], ALU.mult))
                        link(tt(rt[:, 1, m], xc[:, m], si[:, m], ALU.mult))
                        link(tt(rt[:, 2, m], xc[:, m], co[:, m], ALU.mult))
                        link(tt(rt[:, 3, m], xa[:, m], si[:, m], ALU.mult))
                        link(tt(xa[:, m], rt[:, 0, m], rt[:, 1, m], ALU.subtract))
                        ins = tt(xc[:, m], rt[:, 2, m], rt[:, 3, m], ALU.add)
                        if m == 0:
                            link(ins)
                    link(ins)
                    v.tensor_copy(ik2[:, :, 0], tok[:, :, 14 * HD:15 * HD])
                    tell(v.tensor_copy(ik2[:, :, 1], tok[:, :, 14 * HD:15 * HD]), rope_done)
                    link(ts(wi[:], tok[:, :, C_IW:C_DT], IDX_SCALE, None, ALU.mult))
                    v.wait_ge(acs_ps, 1)
                    tell(v.tensor_copy(acs, sp[0][:, 0:MT * SSDH].rearrange("p (m h) -> p m h", m=MT)), acs_out)
                    v.wait_ge(acs_out, 1)
                    tell(tt(dec[:, 0], sp[0][:, 64:64 + SSDH], acs[:, 0], ALU.subtract), acs_arg)
                    v.wait_ge(cb_ps, 1)
                    tell(v.tensor_copy(cbT[:].rearrange("p c g n -> p (c g n)"), sp[1][:]), cb_out)
                    v.wait_ge(xs_out, 4)
                    hp = [P, MT, SSDH, HD]
                    x4 = xs.rearrange("p m (h e) -> p m h e", e=HD)
                    d4 = xdt.rearrange("p m (h e) -> p m h e", e=HD)
                    for m in range(MT):
                        link(tt(d4[:, m], x4[:, m], dt[:, m].unsqueeze(2).to_broadcast(hp[0:1] + hp[2:]), ALU.mult))
                    v.wait_ge(acs_exp, 1)
                    tell(tt(xdd.rearrange("p (h e) -> p h e", e=HD), d4[:, 0],
                       dec[:, 0].unsqueeze(2).to_broadcast([P, SSDH, HD]), ALU.mult), xdt_done)
                    for m in range(MT):
                        link(tt(x4[:, m], x4[:, m], pv('dh').unsqueeze(2).to_broadcast([P, SSDH, HD]), ALU.mult))
                    for hf in range(2):
                        v.wait_ge(y5_ps, hf + 1)
                        for j in range(8):
                            gi = 8 * hf + j
                            dst = y5[32 * (gi % 4):32 * (gi % 4) + 32, gi // 4, :].rearrange("p (c q) -> p q c", q=Q5)
                            for q in range(Q5):
                                ins = v.tensor_copy(dst[:, q, :], sp[2 + hf][32 * q:32 * q + 32, j * C5:(j + 1) * C5])
                        tell(ins, y5_out)
                    v.wait_ge(y5_out, 2)
                    yf = y5[:].rearrange("p a t -> p (a t)")
                    lf = LG.rearrange("p a n -> p (a n)")
                    link(tt(lf, yf, yf, ALU.mult))
                    link(ts(lf, lf, 0.044715, 1.0, ALU.mult, ALU.add))
                    tell(tt(lf, lf, yf, ALU.mult), gelu_arg)
                    link(ts(yf, yf, 0.5, None, ALU.mult))
                    zf = z5[:].rearrange("p a t -> p (a t)")
                    v.wait_ge(taken, START['z5', 3] + 1)
                    tell(stt(zf, tg[:, 0].rearrange("p b n -> p (b n)"), 1.0, zf, ALU.add, ALU.mult), z_done)
                    v.wait_ge(gelu_t, 1)
                    tell(stt(yf, lf, 1.0, yf, ALU.add, ALU.mult), gelu_done)

                    for qb in range(MT):
                        nk = (qb + 1) * P
                        sc, sm = sco[:, 0:nk], stm[:, 0:nk]
                        v.wait_ge(ix_ps, qb + 1)
                        for h in range(IH):
                            ps = sp[h % 2][:, (h // 2) * SEQ:(h // 2) * SEQ + nk]
                            ins = ts(sm if h else sc, ps, 0.0, wi[:, qb, h:h + 1], ALU.max, ALU.mult)
                            if h == IH - 1:
                                tell(ins, ix_out)
                                v.wait_ge(ix_out, qb + 1)
                            else:
                                link(ins)
                            if h:
                                link(tt(sc, sc, sm, ALU.add))
                        vis = seen[:, SEQ - nk:SEQ]
                        link(tt(sc, sc, vis, ALU.add))
                        for _r in range(TOPK // 8):
                            link(v.max(top[:], sc))
                            link(v.match_replace(sc, top[:], sc, TAKEN))
                        link(ts(sc, sc, TAKEN / 1.5, MASKED, ALU.is_gt, ALU.mult))
                        link(tt(amask[:, qb, 0:nk], sc, vis, ALU.add))
                    v.wait_ge(glu_t, 4)
                    link(stt(yf, pT.rearrange("p a n -> p (a n)"), 1.0, yf, ALU.add, ALU.mult))
                    tell(stt(yT[:, 0:4, :].rearrange("p a t -> p (a t)"), yf, 0.25, zf, ALU.mult,
                        ALU.mult), s5_done)
                    v.wait_ge(taken, START['zssd', 1] + 2)
                    zsf = zssd.rearrange("p m n -> p (m n)")
                    tell(stt(zsf, tg[:].rearrange("p a b n -> p (a b n)"), 1.0, zsf, ALU.add, ALU.mult), z_done)

                    def seg_arg(n):
                        c, rd = n // 4, n % 4
                        sg = seg[:, n % 2].rearrange("p (h l) -> p h l", h=4)
                        if n >= 2:
                            v.wait_ge(yd_ps, n - 1)
                        v.wait_ge(ab_ps, n + 1)
                        link(tt(sg, sp[0][:].rearrange("p (h l) -> p h l", h=4),
                                acs[:, c, 4 * rd:4 * rd + 4].unsqueeze(2).to_broadcast([P, 4, P]), ALU.subtract))
                        tell(tt(sg, sg, maskT[:].unsqueeze(1).to_broadcast([P, 4, P]), ALU.add), seg_done)

                    def seg_mul(n):
                        c, rd = n // 4, n % 4
                        sg = seg[:, n % 2].rearrange("p (h l) -> p h l", h=4)
                        v.wait_ge(seg_exp, n + 1)
                        tell(tt(sg, sg, cbT[:, c, rd // 2].unsqueeze(1).to_broadcast([P, 4, P]), ALU.mult), m_done)

                    def y_in(c):
                        v.wait_ge(yd_ps, 4 * (c + 1))
                        for b in range(2):
                            d = xs[:, c, b * BANK:(b + 1) * BANK]
                            tell(tt(d, d, sp[2 + b][:], ALU.add), yd_out)

                    for n in range(8):
                        seg_arg(n)
                        if n:
                            seg_mul(n - 1)
                        if n == 4:
                            y_in(0)
                    for g in range(SSDG):
                        v.wait_ge(yo_ps, g + 1)
                        tmp = cv.rearrange("p a n -> p (a n)").rearrange("p (h e) -> p h e", e=HD)
                        tell(tt(tmp, sp[1][:].rearrange("p (h e) -> p h e", e=HD),
                           eacs[:, 1, 8 * g:8 * g + 8].unsqueeze(2).to_broadcast([P, 8, HD]),
                           ALU.mult), yo_out)
                        v.wait_ge(yo_out, g + 1)
                        d = x4[:, 1, 8 * g:8 * g + 8]
                        link(tt(d, d, tmp, ALU.add))
                        if g == 0:
                            seg_mul(7)
                    y_in(1)
                    v.wait_ge(yd_out, 4)
                    v.wait_ge(z_done, 2)
                    link(stt(xsf, xsf, 0.5, zsf, ALU.mult, ALU.mult))
                    for m in range(MT):
                        for g in range(SSDG):
                            y = xs[:, m, g * BANK:(g + 1) * BANK]
                            link(stt(cv.rearrange("p a n -> p (a n)"), y, 1.0, y, ALU.mult, ALU.mult,
                                     accum_out=rms[:, 0, m, g:g + 1]))
                    tell(ts(rms[:, 0], rms[:, 0], 1.0 / BANK, RMS_EPS, ALU.mult, ALU.add), rms_arg)
                    v.wait_ge(rms_pow, 1)
                    for m in range(MT):
                        for g in range(SSDG):
                            y = xs[:, m, g * BANK:(g + 1) * BANK]
                            ins = ts(y, y, rms[:, 1, m, g:g + 1], None, ALU.mult)
                        tell(ins, ys_done)
                    v.wait_ge(taken, START['zmem', 1] + 1)
                    zaf = zatt[:].rearrange("p a t -> p (a t)")
                    zmf = zmem[:].rearrange("p a t -> p (a t)")
                    link(stt(zaf, tg[:, 0].rearrange("p b n -> p (b n)"), 1.0, zaf, ALU.add, ALU.mult))
                    tell(stt(zmf, tg[:, 1, 0:2].rearrange("p b n -> p (b n)"), 1.0, zmf, ALU.add,
                        ALU.mult), z_done)
                    v.wait_ge(z_done, 3)

                    def scaled(b):
                        sparse, qb, heads = BATCH[b]
                        nk, nh = keys_of(b), len(BATCH[b][2])
                        v.wait_ge(lg_ps, b + 1)
                        if b >= 2:
                            v.wait_ge(pt_ps, b - 1)
                        lg = LG[:, b % 2].rearrange("p (h k) -> p h k", h=nh)
                        for half in range(2):
                            ps = gp[2 * (b % 2) + half][:, 0:SEQ].rearrange("p (h k) -> p h k", k=nk)
                            lh = lg[:, half * nh // 2:(half + 1) * nh // 2]
                            if sparse:
                                link(stt(lh, ps, ATT_SCALE,
                                         amask[:, qb, 0:nk].unsqueeze(1).to_broadcast([P, nh // 2, nk]),
                                         ALU.mult, ALU.add))
                            else:
                                link(ts(lh, ps, ATT_SCALE, None, ALU.mult))
                        tell(v.tensor_reduce(smx[:, 0, b % 2, 0:nh], lg, AX.X, ALU.max, negate=True), lg_out)

                    def normed(b):
                        nk, nh = keys_of(b), len(BATCH[b][2])
                        v.wait_ge(lg_exp, b + 1)
                        link(v.reciprocal(smx[:, 2, b % 2, 0:nh], smx[:, 1, b % 2, 0:nh]))
                        lg = LG[:, b % 2].rearrange("p (h k) -> p h k", h=nh)
                        tell(tt(lg, lg, smx[:, 2, b % 2, 0:nh].unsqueeze(2).to_broadcast([P, nh, nk]),
                           ALU.mult), p_done)

                    def gated(b):
                        sparse, qb, heads = BATCH[b]
                        v.wait_ge(o_ps, b + 1)
                        f, n = heads[0][0], len(heads) // 2
                        z = (zatt if sparse else zmem)[:, f:f + n, qb * P:(qb + 1) * P]
                        k = KOF[1 if sparse else 3][0]
                        tell(stt(yT[:, k + f:k + f + n, qb * P:(qb + 1) * P], sp[3][:, 0:n * P].rearrange("p (f t) -> p f t", f=n),
                            0.5, z, ALU.mult, ALU.mult), o_out)

                    scaled(0)
                    for b in range(len(BATCH)):
                        if b + 1 < len(BATCH):
                            scaled(b + 1)
                        normed(b)
                        if b:
                            gated(b - 1)
                    gated(len(BATCH) - 1)
                    for d in range(KT):
                        pair = 2 * (d % 2)
                        v.wait_ge(units_done, AT['branch', d] + 1)
                        v.wait_ge(gate_t, NB * (d + 1))
                        for i in range(2):
                            link(stt(mg[:, i], tg[:, d % 2, 2 * i:2 * i + 2].rearrange("p b n -> p (b n)"), 1.0,
                                     sp[pair + i][:], ALU.add, ALU.mult))
                        link(tt(mg[:, 0], mg[:, 0], mg[:, 1], ALU.add))
                        tell(tt(merged[:, d, :], mg[:, 0, 0:SEQ], mg[:, 0, SEQ:], ALU.add), mg_done)
                        v.wait_ge(mg_done, d + 1)
                    v.wait_ge(ax_done, 1)
                    for c in range(4):
                        v.wait_ge(units_done, AT['out', 4 * c + 3] + 1)
                        for m in range(MT):
                            n = MT * c + m
                            xv = xtok[:, m, c * BANK:(c + 1) * BANK]
                            tell(stt(xv, gp[2 * (c % 2) + m][:], 0.5, xv, ALU.mult, ALU.add), res_done)
                            v.wait_ge(res_done, n + 1)
                            link(v.bn_stats(st6[:, m, c, :], xv))
                    v.wait_ge(lng_in, 16)
                    v.wait_ge(lnb_in, 16)
                    gf, bf = lng, lnb
                    for m in range(MT):
                        link(v.bn_aggr(mv[:, m, 0:2], st6[:, m].rearrange("p c s -> p (c s)")))
                        tell(ts(mv[:, m, 2:3], mv[:, m, 1:2], LN_EPS, None, ALU.add), var_done)
                    for m in range(MT):
                        v.wait_ge(rstd_done, m + 1)
                        xm = xtok[:, m, :]
                        link(ts(xm, xm, mv[:, m, 0:1], mv[:, m, 2:3], ALU.subtract, ALU.mult))
                        link(tt(xm, xm, gf, ALU.mult))
                        tell(tt(xm, xm, bf, ALU.add), ln_done)
            nc.multi_engine_barrier(mybir.ALL_ENGINES, sems_to_clear=clear)


def kernel(**inputs):
    import concourse.bacc as bacc
    from concourse.bass_utils import run_bass_kernel_spmd

    a = {k: np.asarray(v) for k, v in inputs.items()}
    sizes = (('s5_u', 512), ('s5_z', 512), ('att_q', 512), ('att_k', 128), ('att_v', 128), ('att_z', 512),
             ('idx_q', 256), ('idx_k', 64), ('idx_w', 4), ('ssd_z', 1024), ('ssd_xbc', XBC), ('ssd_dt', 16),
             ('mem_q', 256), ('mem_z', 256), ('gates', NB * D))
    col, o = {}, 0
    for name, n in sizes:
        col[name] = np.arange(o, o + n)
        o += n
    order = np.concatenate([np.arange(HD) + HD * (j + AKV * 2 * h) for j in range(4) for h in range(2)])
    win, wkv = a['w_in'], a['mem_w_kv']

    def t_units(m):
        n = m.shape[2] // P
        return m.reshape(DEPTH, KT, P, n, P).transpose(0, 3, 2, 1, 4).reshape(DEPTH, n, P, KT * P)

    def m_units(m, cols, per):
        k, n = m.shape[1] // P, m.shape[2] // cols
        u = m.reshape(DEPTH, k // per, per, P, n, cols).transpose(0, 4, 1, 3, 2, 5)
        return u.reshape(DEPTH, n * (k // per), P, per * cols)

    tokc = np.concatenate([col['att_q'][order], col['att_k'], col['idx_q'], col['idx_k'], col['att_v'],
                           col['idx_w'], col['ssd_dt']])
    gates = win[:, :, col['gates']].reshape(DEPTH, D, NB, KT, P).transpose(0, 1, 3, 2, 4).reshape(DEPTH, D, NB * D)
    wbr = np.concatenate([a['w_br_s5'], a['w_br_attn'][:, order], a['w_br_ssd'], a['w_br_mem']], axis=1)
    arrays = {
        'u5': t_units(win[:, :, col['s5_u']]), 'z5': t_units(win[:, :, col['s5_z']]),
        'xbc': t_units(win[:, :, col['ssd_xbc']]), 'zatt': t_units(win[:, :, col['att_z'][order]]),
        'qmem': t_units(win[:, :, col['mem_q']]), 'zmem': t_units(win[:, :, col['mem_z']]),
        'kmem': t_units(wkv[:, :, :MEMH * HD]), 'vmem': m_units(wkv[:, :, MEMH * HD:], MEMH * HD, 8),
        'gate': t_units(gates), 'tok': m_units(win[:, :, tokc[:2 * BANK]], BANK, 4),
        'small': m_units(win[:, :, tokc[2 * BANK:]], SMALL, KT), 'zssd': m_units(win[:, :, col['ssd_z']], BANK, 4),
        'glu': m_units(a['s5_w_glu'], BANK, 4), 'out': m_units(a['w_out'], BANK, 4),
        'branch': wbr.reshape(DEPTH, KB, P, KT, P).transpose(0, 3, 2, 1, 4).reshape(DEPTH, KT, P, SLOT),
    }
    kinds = list(arrays)

    def state(m):
        rest = m.shape[3:]
        m = m.reshape((DEPTH, PAIRS, 2, P5) + rest)
        return np.moveaxis(m, 1, 3).reshape(DEPTH, P, -1)

    def rows(m):
        return np.broadcast_to(m[:, None, :], (DEPTH, P, m.shape[1]))

    def per_feature(m):
        return m.reshape(DEPTH, -1, P).transpose(0, 2, 1)

    dsk = a['s5_d'].reshape(DEPTH, PAIRS, 2 * H5).transpose(0, 2, 1)
    parts = {
        'lre': state(a['s5_lam_re']), 'lim': state(a['s5_lam_im']),
        'ldt': state(np.broadcast_to(a['s5_log_dt'][:, :, None], (DEPTH, G5, P5))),
        'bre': state(a['s5_b_re']), 'bim': state(a['s5_b_im']),
        'cre': state(a['s5_c_re'].transpose(0, 1, 3, 2)), 'cim': state(a['s5_c_im'].transpose(0, 1, 3, 2)),
        'dsk': np.tile(dsk, (1, 4, 1)), 'bglu': per_feature(a['s5_b_glu']),
        'cw': a['ssd_conv_w'].reshape(DEPTH, CONV, XT, P).transpose(0, 3, 2, 1).reshape(DEPTH, P, XT * CONV),
        'cb': per_feature(a['ssd_conv_b']), 'dtb': rows(a['ssd_dt_bias']), 'alog': rows(a['ssd_a_log']),
        'dh': rows(a['ssd_d']), 'ng': per_feature(a['ssd_norm_g']),
        'bg': a['b_gate'].reshape(DEPTH, NB, KT, P).transpose(0, 3, 2, 1).reshape(DEPTH, P, KT * NB),
    }
    arrays['par'] = np.concatenate([parts[n] for n, _ in PARAMS], axis=2)

    def t_tokens(m):
        return m[0].T.reshape(KT, P, SEQ).transpose(1, 0, 2)

    arrays['x'] = a['x'][0]
    arrays['x_t'] = t_tokens(a['x'])
    arrays['mem_t'] = t_tokens(a['mem'])
    arrays['pos'] = a['positions'][0].reshape(MT, P).T
    arrays['ln_g'] = a['ln_g']
    arrays['ln_b'] = a['ln_b']
    arrays = {f"in_{k}": np.ascontiguousarray(v) for k, v in arrays.items()}
    nc = bacc.Bacc("TRN2", target_bir_lowering=False, num_devices=1)
    ap = {k: nc.dram_tensor(k, v.shape, mybir.dt.from_np(v.dtype), kind="ExternalInput").ap()
          for k, v in arrays.items()}
    out = nc.dram_tensor("out", (SEQ, D), F32, kind="ExternalOutput").ap()
    build(nc, ap['in_x'], ap['in_x_t'], ap['in_mem_t'], ap['in_pos'], {k: ap[f"in_{k}"] for k in kinds},
          ap['in_par'], ap['in_ln_g'], ap['in_ln_b'], out)
    r = run_bass_kernel_spmd(nc, [arrays], core_ids=[0])
    return r.results[0]["out"].reshape(1, SEQ, D)
```

```python
import math
from contextlib import ExitStack

import numpy as np
import concourse.bass as bass
from concourse import mybir

F32 = mybir.dt.float32
F32R = mybir.dt.float32r
I32 = mybir.dt.int32
ALU = mybir.AluOpType
ACT = mybir.ActivationFunctionType
AX = mybir.AxisListType

P = 128
D = 2048
SEQ = 256
DEPTH = 2
KT = D // P
MT = SEQ // P
BANK = 512
S5W, G5, H5, P5 = 512, 32, 16, 64
PAIRS = G5 // 2
Q5 = 4
C5 = SEQ // Q5
HD = 64
AH, AKV, IH = 8, 2, 4
TOPK = 64
SSDW, SSDH, SSDN, SSDG = 1024, 16, 128, 2
XBC = SSDW + 2 * SSDG * SSDN
XT = XBC // P
CONV = 4
MEMH = 4
NB = 4
ROPE = 16
THETA = 500000.0
ALPHA = (2 * DEPTH) ** 0.25
LN_EPS = 1e-5
RMS_EPS = 1e-5
IDX_SCALE = (IH ** -0.5) * (HD ** -0.5)
ATT_SCALE = HD ** -0.5
MASKED = -1e30
TAKEN = -3e38
GELU_C = math.sqrt(2.0 / math.pi)
ROUND = 12582912.0
TWO_PI = (6.28125, 0.0019340515136718750, 1.2556659146e-06)
PI_LO = 3.1415925

UNIT = KT * P
KB = (S5W + AH * HD + SSDW + MEMH * HD) // P
SLOT = KB * P
NSLOT = 3

ROPED = AH + AKV + IH + 1
C_V = ROPED * HD
C_IW = C_V + AKV * HD
C_DT = C_IW + IH
TOKW = C_DT + SSDH
SMALL = TOKW - 2 * BANK

PARAMS = (('lre', PAIRS), ('lim', PAIRS), ('ldt', PAIRS), ('bre', PAIRS * H5), ('bim', PAIRS * H5),
          ('cre', PAIRS * H5), ('cim', PAIRS * H5), ('dsk', PAIRS), ('bglu', S5W // P), ('cw', XT * CONV),
          ('cb', XT), ('dtb', SSDH), ('alog', SSDH), ('dh', SSDH), ('ng', SSDW // P), ('bg', KT * NB))
PW = sum(n for _, n in PARAMS)
PO = {}
_o = 0
for _n, _w in PARAMS:
    PO[_n] = (_o, _o + _w)
    _o += _w

STREAM = ([('u5', i) for i in range(4)] + [('small', 0)] + [('xbc', i) for i in range(XT)]
          + [('tok', i) for i in range(8)] + [('z5', i) for i in range(4)]
          + [('zssd', 0), ('glu', 0)] + [('zssd', i) for i in range(1, 8)] + [('zatt', i) for i in range(4)]
          + [('qmem', i) for i in range(2)] + [('kmem', i) for i in range(2)] + [('zmem', i) for i in range(2)]
          + [('vmem', i) for i in range(2)])
for _d in range(KT):
    STREAM += [('gate', NB * _d + _b) for _b in range(NB)]
    if _d:
        STREAM += [('branch', 0), ('branch', 1)] if _d == 1 else [('branch', _d)]
STREAM += [('out', i) for i in range(16)]
AT = {u: n for n, u in enumerate(STREAM)}
SPLIT = {u: n for n, u in enumerate(u for u in STREAM if u[0] == 'out' or u[0] == 'gate' and u[1] >= 2 * NB)}
WHOLE = {u: n for n, u in enumerate(u for u in STREAM if u not in SPLIT)}
PIECE = UNIT // 2
NPIECE = 2 * len(SPLIT)
NPART = 4
WIDTH = {'small': KT * SMALL, 'branch': SLOT}


def build(nc, x, x_t, mem_t, pos, w, par, ln_g, ln_b, out):
    ctx = ExitStack()
    with ctx:
        def sb(name, shape, dt=F32):
            return ctx.enter_context(nc.sbuf_tensor(name, shape, dt))

        def place():
            return -(-nc.sbuf_base // 32) * 32

        sems = []

        def sem(name):
            s = ctx.enter_context(nc.semaphore(name))
            sems.append(s)
            return s

        x_at = place()
        xT = sb("xT", [P, KT, SEQ])
        ring = sb("ring", [P, NSLOT, SLOT])
        mem_at = place()
        memT = sb("memT", [P, KT, SEQ])
        yT = sb("yT", [P, KB, SEQ])
        prm = sb("prm", [P, PW])
        ident = sb("ident", [P, P])
        tri = sb("tri", [P, P])
        maskT = sb("maskT", [P, P])
        seen = sb("seen", [P, SEQ])
        ones = sb("ones", [P, P])
        cs = sb("cs", [P, 2, MT, ROPE // 2])
        posi = sb("posi", [P, MT], I32)
        angw = sb("angw", [P, 4, MT * ROPE // 2])
        expo = sb("expo", [P, MT])

        U = sb("U", [P, PAIRS, C5])
        wide_at = place()
        wide = sb("wide", [P, 2 * D])
        W5 = wide[:, :].rearrange("p (r g n) -> p r g n", r=2, g=PAIRS)
        xs = wide[:, 0:D].rearrange("p (m n) -> p m n", m=MT)
        xdt = wide[:, D:2 * D].rearrange("p (m n) -> p m n", m=MT)
        xtok = wide[:, :].rearrange("p (m n) -> p m n", m=MT)
        gd_at = place()
        GD = sb("GD", [P, 2, PAIRS, Q5 + 1, 2 * H5])
        BD = sb("BD", [P, 2, PAIRS, 2 * H5])
        xb_at = place()
        xb = sb("xb", [P, XT, SEQ + CONV - 1])
        ST = sb("ST", [P, C5 + 1, 2, PAIRS])
        t5_at = place()
        T5 = sb("T5", [P, PAIRS, P])
        y5 = sb("y5", [P, 4, SEQ])
        z5 = sb("z5", [P, 4, SEQ])
        sflat = ST[:, 1:C5 + 1, :, :].rearrange("p c r g -> p (c r g)")
        K5 = sflat[0:32, :]
        zssd = sflat.rearrange("p (m n) -> p m n", m=MT)
        V5 = yT[:, 0:16, :].rearrange("p (r a) t -> p r (a t)", r=2)
        s5s = sb("s5s", [P, 16, PAIRS])
        pw5 = sb("pw5", [P, 3, PAIRS, Q5 + 1])
        sc5 = sb("sc5", [P, 2, 2, PAIRS])
        am5 = sb("am5", [P, 2, 2, PAIRS])

        tok = sb("tok", [P, MT, TOKW])
        ik2 = sb("ik2", [P, MT, 2, HD])
        qkT = sb("qkT", [P, 8, SEQ])
        gflat = GD[:, :, :, :, :].rearrange("p r g j h -> p (r g j h)")
        LG = gflat[:, 0:2 * BANK].rearrange("p (a n) -> p a n", a=2)
        pT = gflat[:, 2 * BANK:4 * BANK].rearrange("p (a n) -> p a n", a=2)
        sco = gflat[:, 2048:2048 + SEQ]
        stm = gflat[:, 2304:2304 + SEQ]
        amask = gflat[:, 2560:2560 + 2 * SEQ].rearrange("p (m n) -> p m n", m=MT)
        top = sb("top", [P, 8])
        wi = sb("wi", [P, MT, IH])
        smx = sb("smx", [P, 3, 2, 4])

        xflat = xb[:, :, :].rearrange("p f t -> p (f t)")
        zatt = xflat[:, 0:1024].rearrange("p (f t) -> p f t", f=4)
        qmT = xflat[:, 1024:1536].rearrange("p (f t) -> p f t", f=2)
        kmT = xflat[:, 1536:2048].rearrange("p (f t) -> p f t", f=2)
        zmem = xflat[:, 2048:2560].rearrange("p (f t) -> p f t", f=2)
        vm = xflat[:, 2560:3072].rearrange("p (m n) -> p m n", m=MT)
        cvth = sb("cvth", [P, 4, SEQ])
        cv, th = cvth[:, 0:2, :], cvth[:, 2:4, :]
        mg = cvth[:, :, :].rearrange("p (a b) n -> p a (b n)", a=2)
        Bt = sb("Bt", [P, SSDG, SSDN])
        prev = U[:, :, :].rearrange("p g c -> p (g c)")
        cbT = sb("cbT", [P, MT, SSDG, P])
        seg = sb("seg", [P, 2, BANK])
        rt = seg[:, :, :].rearrange("p a n -> p (a n)")[:, 0:4 * MT * ROPED * ROPE // 2].rearrange(
            "p (i m h f) -> p i m h f", i=4, m=MT, h=ROPED)
        dts = sb("dts", [P, 10, MT, SSDH])
        wconv = sb("wconv", [P, XT * (CONV + 1)])
        rms = sb("rms", [P, 2, MT, SSDG])

        def over(name, shape, at):
            return nc.alloc_sbuf_tensor_at(name, shape, F32R, offset=at)

        x_hi = over("x_hi", [P, KT, SEQ], wide_at)
        x_lo = over("x_lo", [P, KT, SEQ], gd_at)
        w_hi = over("w_hi", [P, NPART, PIECE], xb_at)
        w_lo = over("w_lo", [P, NPART, PIECE], t5_at)
        m_hi = over("m_hi", [P, KT, SEQ], mem_at)
        m_lo = over("m_lo", [P, KT, SEQ], x_at)

        tg = sb("tg", [P, 2, NB, SEQ])
        bgh = sb("bgh", [P, KT * NB + 4])
        lng = tok[:, :, :].rearrange("p m n -> p (m n)")[:, 0:D]
        lnb = qkT[:, :, :].rearrange("p f t -> p (f t)")
        st6 = sb("st6", [P, MT, 4, 6])
        mv = sb("mv", [P, MT, 4])

        gp = [ctx.enter_context(nc.psum_tensor(f"gp{i}", [P, BANK], F32)) for i in range(4)]
        sp = [ctx.enter_context(nc.psum_tensor(f"sp{i}", [P, BANK], F32)) for i in range(4)]

        slot_full = [sem(f"slot_full{i}") for i in range(NSLOT)]
        (units_done, taken, par_in, mem_in, x_in, lng_in, lnb_in, xout, v_step, a_step, g_step,
         disc_arg, disc_act, v5_ready, g5_ready, w5_ps, w5_out, k5_ps, k5_out, k5_diag, t5_out,
         in5_ps, in5_out, scan_done, y5_ps, y5_out, gelu_arg, gelu_t, gelu_done, glu_t, s5_done,
         dt_arg, dt_exp, dt_u, dt_ln, da_done, acs_ps, acs_out, acs_arg, acs_exp,
         conv_done, conv_t, xbc_done, xs_ps, xs_out, cb_ps, cb_out, xdt_done, st_ps, st_out,
         ab_ps, seg_done, seg_exp, m_done, yd_ps, yd_out, yo_ps, yo_out, rms_arg, rms_pow, ys_done, ys_ps, ys_out,
         z_done, rope_done, qk_ps, qk_out, ix_ps, ix_out, lg_ps, lg_out, lg_exp, p_done, pt_ps, pt_out, o_ps, o_out,
         half_done, gate_t, mg_done, ax_done, res_done, var_done, rstd_done, ln_done, xt_ps, xt_out,
         c_in, c_out, c_arg, gd_zero, hi_done, lo_done, pieces_done, xhi_done, xlo_done) = [sem(n) for n in (
            "units_done taken par_in mem_in x_in lng_in lnb_in xout v_step a_step g_step "
            "disc_arg disc_act v5_ready g5_ready w5_ps w5_out k5_ps k5_out k5_diag t5_out "
            "in5_ps in5_out scan_done y5_ps y5_out gelu_arg gelu_t gelu_done glu_t s5_done "
            "dt_arg dt_exp dt_u dt_ln da_done acs_ps acs_out acs_arg acs_exp "
            "conv_done conv_t xbc_done xs_ps xs_out cb_ps cb_out xdt_done st_ps st_out "
            "ab_ps seg_done seg_exp m_done yd_ps yd_out yo_ps yo_out rms_arg rms_pow ys_done ys_ps ys_out "
            "z_done rope_done qk_ps qk_out ix_ps ix_out lg_ps lg_out lg_exp p_done pt_ps pt_out o_ps o_out "
            "half_done gate_t mg_done ax_done res_done var_done rstd_done ln_done xt_ps xt_out "
            "c_in c_out c_arg gd_zero hi_done lo_done pieces_done xhi_done xlo_done").split()]

        def pv(name, rows=P):
            a, b = PO[name]
            return prm[0:rows, a:b]

        def after(eng, s):
            n = [0]

            def link(ins, also=None):
                n[0] += 1
                ins.then_inc(s, 1)
                eng.wait_ge(s, n[0])
            return link

        def signals(eng, step):
            count = {}

            def tell(ins, s):
                count[s.num] = count.get(s.num, 0) + 1
                ins.then_inc(s, 1)
                eng.wait_ge(s, count[s.num])

            return (lambda ins: tell(ins, step)), tell

        def wrap_angle(v, link, src, dst, t, quarter):
            link(v.tensor_scalar(t, src, 1.0 / (2 * math.pi), quarter, ALU.mult, ALU.add))
            link(v.tensor_scalar(t, t, ROUND, None, ALU.add))
            link(v.tensor_scalar(t, t, -ROUND, None, ALU.add))
            link(v.scalar_tensor_tensor(dst, t, -TWO_PI[0], src, ALU.mult, ALU.add))
            for part in TWO_PI[1:]:
                link(v.scalar_tensor_tensor(dst, t, -part, dst, ALU.mult, ALU.add))
            if quarter:
                link(v.tensor_scalar(dst, dst, quarter * 2 * math.pi, PI_LO, ALU.add, ALU.min))
            else:
                link(v.tensor_scalar(dst, dst, PI_LO, None, ALU.min))
            return v.tensor_scalar(dst, dst, -PI_LO, None, ALU.max)

        with nc.Block() as block:
            @block.sync
            def _(s):
                s.dma_start(posi[:], pos).then_inc(c_in, 16)
                s.dma_start(xT[:], x_t).then_inc(x_in, 16)
                s.dma_start(out, x).then_inc(xout, 16)
                s.wait_ge(x_in, 16)
                s.wait_ge(xout, 16)

            @block.gpsimd
            def _(g):
                link = after(g, g_step)
                link(g.memset(ident[:], 0.0))
                link(g.affine_select(out=ident[:], in_=ident[:], compare_op=ALU.not_equal, fill=1.0, base=0,
                                     pattern=[[-1, P]], channel_multiplier=1))
                link(g.memset(ones[:], 1.0))
                link(g.affine_select(out=tri[:], in_=ones[:], compare_op=ALU.is_ge, fill=0.0, base=0,
                                     pattern=[[1, P]], channel_multiplier=-1))
                link(g.memset(maskT[:], 0.0))
                link(g.affine_select(out=maskT[:], in_=maskT[:], compare_op=ALU.is_ge, fill=MASKED, base=0,
                                     pattern=[[1, P]], channel_multiplier=-1))
                link(g.memset(seen[:], 0.0))
                link(g.affine_select(out=seen[:, P:SEQ], in_=seen[:, P:SEQ], compare_op=ALU.is_ge, fill=MASKED,
                                     base=0, pattern=[[-1, P]], channel_multiplier=1))
                link(g.memset(expo[:], -0.5))
                link(g.memset(BD[:], 0.0))

            @block.vector
            def _(v):
                link = after(v, v_step)
                inv = angw[:, 3, 0:ROPE // 2]
                for i in range(ROPE // 2):
                    last = v.memset(angw[:, 3, i:i + 1], float(np.float32(THETA) ** np.float32(-i * 2.0 / ROPE)))
                link(last)
                v.wait_ge(c_in, 16)
                link(v.tensor_copy(mv[:, :, 0], posi[:]))
                ang = angw[:, 0, :].rearrange("p (m f) -> p m f", m=MT)
                link(v.tensor_tensor(ang, mv[:, :, 0:1].to_broadcast([P, MT, ROPE // 2]),
                                     inv.unsqueeze(1).to_broadcast([P, MT, ROPE // 2]), ALU.mult))
                link(wrap_angle(v, link, angw[:, 0, :], cs[:, 0].rearrange("p m f -> p (m f)"), angw[:, 1, :], 0.25))
                wrap_angle(v, link, angw[:, 0, :], cs[:, 1].rearrange("p m f -> p (m f)"), angw[:, 1, :],
                           0.0).then_inc(c_arg, 1)

            @block.scalar
            def _(a):
                a.wait_ge(c_arg, 1)
                a.activation(cs[:], cs[:], ACT.Sin).then_inc(c_out, 1)
                a.wait_ge(c_out, 1)

        first, last_sem = min(s.num for s in sems), max(s.num for s in sems)
        clear = range(first, last_sem + 1)
        nc.multi_engine_barrier(mybir.ALL_ENGINES, sems_to_clear=clear)

        JOBS = ([('u5', i, 1) for i in range(4)] + [('small', 0, 2)] + [('xbc', i, 1) for i in range(XT)]
                + [('tok', 0, 2), ('tok', 1, 2)] + [('z5', i, 1) for i in range(4)]
                + [('zssd', 0, 2), ('zssd', 1, 2)] + [('zatt', i, 1) for i in range(4)]
                + [('qmem', i, 1) for i in range(2)] + [('kmem', i, 1) for i in range(2)]
                + [('zmem', i, 1) for i in range(2)] + [('vmem', 0, 2)])
        START = {}
        nbank = 0
        for name, i, b in JOBS:
            START[name, i] = nbank
            nbank += b
        NPROJ = nbank
        LAST = {('small', 0): AT['small', 0], ('tok', 0): AT['tok', 3], ('tok', 1): AT['tok', 7],
                ('zssd', 0): AT['zssd', 3], ('zssd', 1): AT['zssd', 7], ('vmem', 0): AT['vmem', 1]}

        BATCH = ([(True, 0, [(2 * j, 0), (2 * j + 1, 0), (2 * j, 1), (2 * j + 1, 1)]) for j in range(2)]
                 + [(True, 1, [(j, 0), (j, 1)]) for j in range(4)]
                 + [(False, qb, [(j, 0), (j, 1)]) for qb in range(MT) for j in range(2)])
        NSPARSE = sum(sparse for sparse, _, _ in BATCH)
        KOF = [(0, 4), (4, 8), (8, 16), (16, 18)]

        def keys_of(b):
            sparse, qb, _ = BATCH[b]
            return P if sparse and qb == 0 else SEQ

        def steps(c):
            return slice(CONV - 1 + c * P, CONV - 1 + (c + 1) * P)

        dt, da, acs, eacs, dec = (dts[:, i] for i in range(5))
        xdd = mg[:, :, :].rearrange("p a n -> p (a n)")

        with nc.Fori(0, DEPTH) as layer:
            with nc.Block() as block:
                @block.sync
                def _(s):
                    s.dma_start(prm[:], par[bass.ds(layer, 1)].rearrange("a p n -> p (a n)")).then_inc(par_in, 16)
                    for n, (kind, i) in enumerate(STREAM):
                        if n >= NSLOT:
                            last = STREAM[n - NSLOT]
                            if last in SPLIT:
                                s.wait_ge(lo_done, 2 * (SPLIT[last] + 1))
                            else:
                                s.wait_ge(units_done, WHOLE[last] + 1)
                        wd = WIDTH.get(kind, UNIT)
                        src = w[kind][bass.ds(layer, 1), i].rearrange("a p n -> p (a n)")
                        s.dma_start(ring[:, n % NSLOT, 0:wd], src).then_inc(slot_full[n % NSLOT], 16)
                        if n == 3:
                            s.dma_start(memT[:], mem_t).then_inc(mem_in, 16)
                        if n == AT['gate', NSLOT + 2 * NB]:
                            s.wait_ge(o_ps, len(BATCH))
                            s.dma_start(lng, ln_g[bass.ds(layer, 1)].to_broadcast([P, D])).then_inc(lng_in, 16)
                            s.dma_start(lnb, ln_b[bass.ds(layer, 1)].to_broadcast([P, D])).then_inc(lnb_in, 16)
                        if n == AT['out', 2]:
                            s.wait_ge(pieces_done, 2 * (SPLIT['gate', NB * KT - 1] + 1))
                            s.dma_start(xtok, out.rearrange("(m p) n -> p m n", p=P)).then_inc(x_in, 16)
                    for m in range(MT):
                        s.wait_ge(ln_done, m + 1)
                        s.dma_start(out[m * P:(m + 1) * P, :], xtok[:, m, :]).then_inc(xout, 16)
                    s.wait_ge(xout, 16 * MT)

                @block.gpsimd
                def _(g):
                    link = after(g, g_step)
                    g.memset(T5[:], 0.0)
                    g.memset(ST[:, 0], 0.0)
                    g.memset(GD[:], 0.0).then_inc(gd_zero, 1)
                    g.wait_ge(in5_out, 4)
                    for c in range(C5):
                        g.tensor_tensor(sc5[:, 0], ST[:, c, :, :], am5[:, 0], ALU.mult)
                        link(g.tensor_tensor(sc5[:, 1], ST[:, c, ::-1, :], am5[:, 1], ALU.mult))
                        link(g.tensor_tensor(sc5[:, 0], sc5[:, 0], sc5[:, 1], ALU.add))
                        link(g.tensor_tensor(ST[:, c + 1], ST[:, c + 1], sc5[:, 0], ALU.add))
                    g.memset(sc5[:, 0], 0.0).then_inc(scan_done, 1)
                    g.wait_ge(rms_arg, 1)
                    g.tensor_tensor(rms[:, 1], rms[:, 0], expo[:].unsqueeze(2).to_broadcast([P, MT, SSDG]),
                                    ALU.pow).then_inc(rms_pow, 1)
                    for p, n in enumerate(n for n, u in enumerate(STREAM) if u in SPLIT for _ in range(2)):
                        g.wait_ge(hi_done, p + 1)
                        raw = ring[:, n % NSLOT, (p % 2) * PIECE:(p % 2 + 1) * PIECE]
                        g.tensor_tensor(w_lo[:, p % NPART], raw, w_hi[:, p % NPART].bitcast(F32),
                                        ALU.subtract).then_inc(lo_done, 1)
                    for m in range(MT):
                        g.wait_ge(var_done, m + 1)
                        g.tensor_tensor(mv[:, m, 2:3], mv[:, m, 2:3], expo[:, 0:1], ALU.pow).then_inc(rstd_done, 1)

                @block.tensor
                def _(t):
                    def unit(kind, i=0):
                        n = AT[kind, i]
                        t.wait_ge(slot_full[n % NSLOT], 16 * (n // NSLOT + 1))
                        return ring[:, n % NSLOT, :]

                    def piece(kind, i, half):
                        p = 2 * SPLIT[kind, i] + half
                        t.wait_ge(lo_done, p + 1)
                        return w_hi[:, p % NPART], w_lo[:, p % NPART]

                    def bank_free(n):
                        if n >= 4:
                            t.wait_ge(taken, n - 3)

                    def proj_t(kind, i, moving=xT):
                        b = START[kind, i]
                        wt = unit(kind, i)
                        bank_free(b)
                        for k in range(KT):
                            mm = t.matmul(gp[b % 4][:, 0:SEQ], wt[:, k * P:(k + 1) * P], moving[:, k, :],
                                          start=k == 0, stop=k == KT - 1)
                        mm.then_inc(units_done, 1)

                    def proj_m(kind, i, n, cols, src=xT, then=lambda j: None):
                        b = START[kind, i]
                        per = KT // n
                        bank_free(b + 1)
                        for j in range(n):
                            wt = unit(kind, i * n + j)
                            for m in range(MT):
                                for k in range(per):
                                    kk = j * per + k
                                    mm = t.matmul(gp[(b + m) % 4][:, 0:cols], src[:, kk, m * P:(m + 1) * P],
                                                  wt[:, k * cols:(k + 1) * cols], start=kk == 0, stop=kk == KT - 1)
                            mm.then_inc(units_done, 1)
                            then(j)

                    def four(out_bank, tiles, done):
                        for j, tile in enumerate(tiles):
                            mm = t.transpose(out_bank[:, j * P:(j + 1) * P], tile, ident[:])
                        mm.then_inc(done, 1)

                    for i in range(4):
                        proj_t('u5', i)
                    t.wait_ge(v5_ready, 1)
                    for r in range(2):
                        for q in range(4):
                            if r:
                                t.wait_ge(w5_out, q + 1)
                            four(sp[q], [V5[:, r, gi * P:(gi + 1) * P] for gi in range(4 * q, 4 * q + 4)], w5_ps)
                        if r == 0:
                            proj_m('small', 0, 1, SMALL)
                    proj_t('xbc', 0)
                    t.wait_ge(g5_ready, 1)
                    for q in range(4):
                        t.wait_ge(w5_out, 5 + q)
                        for j in range(4):
                            gi = 4 * q + j
                            for r in range(2):
                                mm = t.matmul(sp[q][0:32, j * P:(j + 1) * P], BD[:, r, gi, :],
                                              GD[:, r, gi, 0:Q5, :].rearrange("p j h -> p (j h)"),
                                              start=r == 0, stop=r == 1)
                        mm.then_inc(k5_ps, 1)
                    for i in range(1, 6):
                        proj_t('xbc', i)
                    t.wait_ge(taken, 4)
                    t.wait_ge(k5_out, 4)
                    for q in range(4):
                        r, half = q % 2, q // 2
                        for j in range(8):
                            gi = 8 * half + j
                            mm = t.matmul(sp[q][:, j * C5:(j + 1) * C5], W5[:, r, gi, :], U[:, gi, :],
                                          start=True, stop=True)
                        mm.then_inc(in5_ps, 1)
                    for i in range(6, XT):
                        proj_t('xbc', i)
                    for i in range(2):
                        proj_m('tok', i, 4, BANK)
                    t.wait_ge(da_done, 1)
                    t.wait_ge(in5_out, 4)
                    t.matmul(sp[0][:, 0:MT * SSDH], tri[:], da.rearrange("p m h -> p (m h)"), start=True, stop=True)
                    t.matmul(sp[0][:, 64:64 + SSDH], ones[:], da[:, 0, :], start=True, stop=True).then_inc(acs_ps, 1)
                    t.wait_ge(xbc_done, XT)
                    for c in range(MT):
                        for g in range(SSDG):
                            n = c * SSDG + g
                            mm = t.matmul(sp[1][:, n * P:(n + 1) * P], xb[:, 8 + g, steps(c)],
                                          xb[:, 10 + g, steps(c)], start=True, stop=True)
                    mm.then_inc(cb_ps, 1)

                    def xs_turn(n):
                        if n >= 2:
                            t.wait_ge(xs_out, n - 1)
                        four(sp[2 + n % 2], [xb[:, 4 * (n % 2) + j, steps(n // 2)] for j in range(4)] if n < 4 else
                             [xb[:, 8 + g, steps(0)] for g in range(SSDG)], xs_ps)

                    xs_turn(0)
                    xs_turn(1)
                    proj_t('z5', 0)
                    xs_turn(2)
                    xs_turn(3)
                    proj_t('z5', 1)
                    xs_turn(4)
                    proj_t('z5', 2)
                    t.wait_ge(scan_done, 1)
                    t.wait_ge(t5_out, 1)
                    t.wait_ge(xs_out, 5)
                    for half in range(2):
                        for j in range(8):
                            gi = 8 * half + j
                            o = sp[2 + half][:, j * C5:(j + 1) * C5]
                            t.matmul(o, T5[:, gi, :], U[:, gi, :], start=True, stop=False)
                            for r in range(2):
                                mm = t.matmul(o, GD[:, r, gi, 1:Q5 + 1, :].rearrange("p j h -> p (j h)"),
                                              ST[:, 0:C5, r, gi], start=False, stop=r == 1)
                        mm.then_inc(y5_ps, 1)
                    proj_t('z5', 3)
                    t.wait_ge(rope_done, 1)
                    t.wait_ge(cb_out, 1)
                    t.wait_ge(acs_arg, 1)

                    def qk_turn(n):
                        m, h = n // 2, n % 2
                        if n >= 2:
                            t.wait_ge(qk_out, n - 1)
                        four(sp[n % 2], [tok[:, m, f * P:(f + 1) * P] if f < 7 else
                                         ik2[:, m].rearrange("p a e -> p (a e)")
                                         for f in range(4 * h, 4 * h + 4)], qk_ps)

                    qk_turn(0)
                    qk_turn(1)

                    def glu():
                        t.wait_ge(gelu_done, 1)
                        wt = unit('glu')
                        t.wait_ge(y5_out, 2)
                        for j in range(4):
                            for k in range(4):
                                mm = t.matmul(sp[2 + j // 2][:, (j % 2) * SEQ:(j % 2 + 1) * SEQ],
                                              wt[:, k * BANK + j * P:k * BANK + (j + 1) * P], y5[:, k, :],
                                              start=k == 0, stop=k == 3)
                        mm.then_inc(units_done, 1)

                    def index(qb):
                        nk = (qb + 1) * P
                        if qb:
                            t.wait_ge(ix_out, 1)
                        else:
                            t.wait_ge(qk_out, 4)
                        for h in range(IH):
                            r = slice(HD * (h % 2), HD * (h % 2 + 1))
                            mm = t.matmul(sp[h % 2][:, (h // 2) * SEQ:(h // 2) * SEQ + nk],
                                          qkT[r, 5 + h // 2, qb * P:(qb + 1) * P], qkT[r, 7, 0:nk],
                                          start=True, stop=True)
                        mm.then_inc(ix_ps, 1)

                    def diag(n):
                        c, rd = n // 4, n % 4
                        t.wait_ge(m_done, n + 1)
                        if n == 4:
                            t.wait_ge(yd_out, 2)
                        for j in range(4):
                            h = 4 * rd + j
                            mm = t.matmul(sp[2 + h // 8][:, (h % 8) * HD:(h % 8 + 1) * HD],
                                          seg[:, n % 2, j * P:(j + 1) * P], xdt[:, c, h * HD:(h + 1) * HD],
                                          start=True, stop=True)
                        mm.then_inc(yd_ps, 1)

                    def ssd_round(n):
                        if n:
                            t.wait_ge(seg_done, n)
                        else:
                            t.wait_ge(ix_out, 2)
                            t.wait_ge(st_out, 2)
                        for j in range(4):
                            h = 4 * (n % 4) + j
                            mm = t.matmul(sp[0][:, j * P:(j + 1) * P], da[:, n // 4, h:h + 1].to_broadcast([P, P]),
                                          tri[:], start=True, stop=True)
                        mm.then_inc(ab_ps, 1)
                        if n:
                            diag(n - 1)

                    def carried(g):
                        if g:
                            t.wait_ge(yo_out, 1)
                        t.matmul(sp[1][:], xb[:, 10 + g, steps(1)], prev[:, g * BANK:(g + 1) * BANK],
                                 start=True, stop=True).then_inc(yo_ps, 1)

                    def state():
                        t.wait_ge(xdt_done, 1)
                        t.wait_ge(xs_out, 5)
                        t.wait_ge(glu_t, 4)
                        for g in range(SSDG):
                            t.matmul(sp[2 + g][:], Bt[:, g, :], xdd[:, g * BANK:(g + 1) * BANK], start=True,
                                     stop=True).then_inc(st_ps, 1)

                    def meanwhile(j):
                        if j == 0:
                            qk_turn(2)
                            qk_turn(3)
                            glu()
                            index(0)
                        elif j == 1:
                            index(1)
                            state()
                        elif j == 3:
                            ssd_round(0)

                    proj_m('zssd', 0, 4, BANK, then=meanwhile)
                    proj_m('zssd', 1, 4, BANK, then=lambda j: ssd_round(j + 1))
                    for i in range(3):
                        proj_t('zatt', i)
                        ssd_round(5 + i)
                    proj_t('zatt', 3)
                    carried(0)
                    diag(7)
                    proj_t('qmem', 0)
                    carried(1)
                    proj_t('qmem', 1)

                    def logits(b):
                        sparse, qb, heads = BATCH[b]
                        nk = keys_of(b)
                        if b:
                            t.wait_ge(lg_out, b)
                        for n, (f, half) in enumerate(heads):
                            r = slice(HD * half, HD * (half + 1))
                            q = (qkT if sparse else qmT)[r, f, qb * P:(qb + 1) * P]
                            k = qkT[r, 4, 0:nk] if sparse else kmT[r, f, 0:nk]
                            c = (n % (len(heads) // 2)) * nk
                            mm = t.matmul(sp[half][:, c:c + nk], q, k, start=True, stop=True)
                        mm.then_inc(lg_ps, 1)

                    def weighted(b):
                        sparse, qb, heads = BATCH[b]
                        t.wait_ge(pt_out, b + 1)
                        if b:
                            t.wait_ge(o_out, b)
                        tiles = keys_of(b) // P
                        for n, (f, half) in enumerate(heads):
                            for s in range(tiles):
                                v = (tok[:, s, C_V + half * HD:C_V + (half + 1) * HD] if sparse else
                                     vm[:, s, (2 * f + half) * HD:(2 * f + half + 1) * HD])
                                blk = n * tiles + s
                                o = n % (len(heads) // 2)
                                mm = t.matmul(sp[3][HD * half:HD * (half + 1), o * P:(o + 1) * P], v,
                                              pT[:, b % 2, blk * P:(blk + 1) * P], start=s == 0, stop=s == tiles - 1)
                        mm.then_inc(o_ps, 1)

                    def attend(b):
                        if b < len(BATCH):
                            t.wait_ge(p_done, b + 1)
                            if b:
                                t.wait_ge(pt_out, b)
                            four(sp[2], [LG[:, b % 2, j * P:(j + 1) * P] for j in range(4)], pt_ps)
                        if b:
                            weighted(b - 1)
                        if b + 1 < len(BATCH):
                            if b == NSPARSE - 1:
                                t.wait_ge(taken, START['kmem', 1] + 1)
                            elif b == NSPARSE:
                                t.wait_ge(taken, NPROJ)
                            logits(b + 1)

                    def ys_turn(m):
                        t.wait_ge(ys_done, m + 1)
                        for q in range(2):
                            if m:
                                t.wait_ge(ys_out, q + 1)
                            four(sp[2 + q], [xs[:, m, (4 * q + j) * P:(4 * q + j + 1) * P] for j in range(4)], ys_ps)

                    t.wait_ge(yo_out, 2)
                    logits(0)
                    proj_t('kmem', 0, memT)
                    t.wait_ge(yd_out, 4)
                    attend(0)
                    proj_t('kmem', 1, memT)
                    attend(1)
                    for i in range(2):
                        proj_t('zmem', i)
                        attend(2 + i)
                    proj_m('vmem', 0, 2, MEMH * HD, memT, then=lambda j: attend(4 + j))

                    def branch(d):
                        pair = 2 * (d % 2)
                        wt = unit('branch', d)
                        if d >= 2:
                            t.wait_ge(mg_done, d - 1)
                        elif d == 0:
                            t.wait_ge(s5_done, 1)
                            t.wait_ge(ys_out, 4)
                        for b, (lo, hi) in enumerate(KOF):
                            for k in range(lo, hi):
                                mm = t.matmul(sp[pair + b // 2][:, (b % 2) * SEQ:(b % 2 + 1) * SEQ],
                                              wt[:, k * P:(k + 1) * P], yT[:, k, :], start=k == lo, stop=k == hi - 1)
                        mm.then_inc(units_done, 1)

                    for d in range(KT):
                        pair = 2 * ((d + 1) % 2)
                        for b in range(NB):
                            if d < 2 and b == 0:
                                t.wait_ge(taken, NPROJ - 2 + 2 * d)
                            if b == 0 and d >= 2:
                                t.wait_ge(gate_t, NB * (d - 1))
                            o = gp[pair + b // 2][:, (b % 2) * SEQ:(b % 2 + 1) * SEQ]
                            if d < 2:
                                wt = unit('gate', NB * d + b)
                                for k in range(KT):
                                    mm = t.matmul(o, wt[:, k * P:(k + 1) * P], xT[:, k, :], start=k == 0,
                                                  stop=k == KT - 1)
                                mm.then_inc(units_done, 1)
                            else:
                                for hf in range(2):
                                    wh, wl = piece('gate', NB * d + b, hf)
                                    for j in range(KT // 2):
                                        k = hf * KT // 2 + j
                                        js = slice(j * P, (j + 1) * P)
                                        t.matmul(o, wh[:, js], x_hi[:, k, :], start=k == 0, stop=False)
                                        t.matmul(o, wh[:, js], x_lo[:, k, :], start=False, stop=False)
                                        mm = t.matmul(o, wl[:, js], x_hi[:, k, :], start=False, stop=k == KT - 1)
                                    mm.then_inc(pieces_done, 1)
                            n = NSPARSE + NB * d + b
                            if n <= len(BATCH):
                                attend(n)
                            elif n <= len(BATCH) + MT:
                                if n == len(BATCH) + 1:
                                    t.wait_ge(o_out, len(BATCH))
                                ys_turn(n - len(BATCH) - 1)
                        if d == 0:
                            continue
                        for dd in ([0, 1] if d == 1 else [d]):
                            branch(dd)
                        if d == 1:
                            t.wait_ge(xlo_done, 1)
                    for c in range(4):
                        for j in range(4):
                            if c == 0:
                                t.wait_ge(mg_done, 4 * j + 4)
                                if j == 0:
                                    t.wait_ge(gate_t, NB * (KT - 1))
                            if j == 0 and c == 1:
                                t.wait_ge(gate_t, NB * KT)
                            if j == 0 and c >= 2:
                                t.wait_ge(res_done, MT * (c - 1))
                            for hf in range(2):
                                wh, wl = piece('out', 4 * c + j, hf)
                                for m in range(MT):
                                    o = gp[2 * ((c + 1) % 2) + m][:]
                                    for k in range(2):
                                        kk = 4 * j + 2 * hf + k
                                        ks, ms = slice(k * BANK, (k + 1) * BANK), slice(m * P, (m + 1) * P)
                                        t.matmul(o, m_hi[:, kk, ms], wh[:, ks], start=kk == 0, stop=False)
                                        t.matmul(o, m_hi[:, kk, ms], wl[:, ks], start=False, stop=False)
                                        mm = t.matmul(o, m_lo[:, kk, ms], wh[:, ks], start=False, stop=kk == KT - 1)
                                mm.then_inc(pieces_done, 1)
                    for n in range(8):
                        m, q = n // 4, n % 4
                        t.wait_ge(ln_done, m + 1)
                        if n >= 4:
                            t.wait_ge(xt_out, n - 3)
                        four(sp[q], [xtok[:, m, f * P:(f + 1) * P] for f in range(4 * q, 4 * q + 4)], xt_ps)

                @block.scalar
                def _(a):
                    def done(kind, i=0):
                        a.wait_ge(units_done, LAST.get((kind, i), AT[kind, 0] + i) + 1)
                        return START[kind, i]

                    def copy(o, i, **k):
                        return a.activation(o, i, ACT.Copy, **k)

                    a.wait_ge(par_in, 16)
                    a.activation(s5s[:, 0], pv('ldt'), ACT.Exp).then_inc(disc_act, 1)
                    a.wait_ge(disc_arg, 1)
                    a.activation(s5s[:, 1], s5s[:, 1], ACT.Exp)
                    a.activation(dts[:, 5, 0], pv('alog'), ACT.Exp).then_inc(a_step, 1)
                    a.activation(s5s[:, 3:5], s5s[:, 3:5], ACT.Sin).then_inc(disc_act, 1)
                    for i in range(4):
                        b = done('u5', i)
                        for pr in range(4):
                            src = gp[b % 4][32 * pr:32 * pr + 32, 0:SEQ].rearrange("p (c q) -> p q c", q=Q5)
                            for q in range(Q5):
                                ins = copy(U[32 * q:32 * q + 32, 4 * i + pr, :], src[:, q, :])
                        ins.then_inc(taken, 1)
                    def w5_evac(r):
                        for q in range(4):
                            a.wait_ge(w5_ps, 4 * r + q + 1)
                            copy(W5[:, r, 4 * q:4 * q + 4, :],
                                 sp[q][:].rearrange("p (g n) -> p g n", g=4)).then_inc(w5_out, 1)

                    w5_evac(0)
                    b = done('small')
                    for m in range(MT):
                        copy(tok[:, m, 2 * BANK:TOKW], gp[(b + m) % 4][:, 0:SMALL]).then_inc(taken, 1)
                    a.wait_ge(dt_arg, 1)
                    a.activation(dts[:, 6], dts[:, 6], ACT.Exp).then_inc(dt_exp, 1)
                    def xbc_evac(i):
                        b = done('xbc', i)
                        copy(xb[:, i, CONV - 1:], gp[b % 4][:, 0:SEQ]).then_inc(taken, 1)

                    w5_evac(1)
                    xbc_evac(0)
                    for q in range(4):
                        a.wait_ge(k5_ps, q + 1)
                        copy(K5[:, q * BANK:(q + 1) * BANK], sp[q][0:32, :]).then_inc(k5_out, 1)
                    a.wait_ge(dt_u, 1)
                    a.activation(dts[:, 8], dts[:, 7], ACT.Ln).then_inc(dt_ln, 1)
                    a.wait_ge(gd_zero, 1)
                    a.wait_ge(k5_diag, 1)
                    k5v = K5.rearrange("p (g n) -> p g n", g=PAIRS)
                    for s in range(Q5):
                        ins = copy(T5[32 * s:32 * s + 32, :, 32 * s:P], k5v[:, :, 0:P - 32 * s])
                    ins.then_inc(t5_out, 1)

                    def xbc_tanh(i):
                        a.wait_ge(conv_done, i + 1)
                        if i >= 2:
                            a.wait_ge(xbc_done, i - 1)
                        a.activation(th[:, i % 2], cv[:, i % 2], ACT.Tanh).then_inc(conv_t, 1)

                    for i in range(1, 6):
                        xbc_evac(i)
                        xbc_tanh(i - 1)
                    a.wait_ge(t5_out, 1)
                    for q in range(4):
                        r, half = q % 2, q // 2
                        a.wait_ge(in5_ps, q + 1)
                        copy(ST[:, 1:C5 + 1, r, 8 * half:8 * half + 8],
                             sp[q][:].rearrange("p (g c) -> p c g", g=8)).then_inc(in5_out, 1)
                    for i in range(6, XT):
                        xbc_evac(i)
                        xbc_tanh(i - 1)
                    xbc_tanh(XT - 1)
                    for i in range(2):
                        b = done('tok', i)
                        for m in range(MT):
                            copy(tok[:, m, i * BANK:(i + 1) * BANK], gp[(b + m) % 4][:]).then_inc(taken, 1)
                    a.wait_ge(acs_out, 1)
                    a.activation(eacs, acs, ACT.Exp)
                    a.wait_ge(acs_arg, 1)
                    a.activation(dec[:, 0], dec[:, 0], ACT.Exp).then_inc(acs_exp, 1)
                    def z_evac(bank, cols, dst, th_dst):
                        copy(dst, bank[:, 0:cols])
                        a.activation(th_dst, bank[:, 0:cols], ACT.Tanh, scale=0.5).then_inc(taken, 1)

                    for n in range(5):
                        a.wait_ge(xs_ps, n + 1)
                        bank = sp[2 + n % 2]
                        (copy(xs[:, n // 2, (n % 2) * BANK:(n % 2 + 1) * BANK], bank[:]) if n < 4 else
                         copy(Bt[:].rearrange("p g n -> p (g n)"), bank[:, 0:SSDG * P])).then_inc(xs_out, 1)
                        if n % 2:
                            b = done('z5', n // 2)
                            z_evac(gp[b % 4], SEQ, z5[:, n // 2, :], tg[:, 0, n // 2, :])
                    for i in range(2, 4):
                        b = done('z5', i)
                        z_evac(gp[b % 4], SEQ, z5[:, i, :], tg[:, 0, i, :])

                    def qk_evac(n):
                        a.wait_ge(qk_ps, n + 1)
                        m, h = n // 2, n % 2
                        copy(qkT[:, 4 * h:4 * h + 4, m * P:(m + 1) * P],
                             sp[n % 2][:].rearrange("p (f t) -> p f t", f=4)).then_inc(qk_out, 1)

                    qk_evac(0)
                    qk_evac(1)
                    a.wait_ge(gelu_arg, 1)
                    a.activation(LG.rearrange("p a n -> p (a n)"), LG.rearrange("p a n -> p (a n)"), ACT.Tanh,
                                 scale=GELU_C).then_inc(gelu_t, 1)
                    qk_evac(2)
                    qk_evac(3)
                    a.wait_ge(units_done, AT['glu', 0] + 1)
                    a.wait_ge(half_done, 1)
                    for j in range(4):
                        a.activation(pT[:, j // 2, (j % 2) * SEQ:(j % 2 + 1) * SEQ],
                                     sp[2 + j // 2][:, (j % 2) * SEQ:(j % 2 + 1) * SEQ], ACT.Tanh, scale=0.5,
                                     bias=bgh[:, KT * NB + j:KT * NB + j + 1]).then_inc(glu_t, 1)
                    for g in range(SSDG):
                        a.wait_ge(st_ps, g + 1)
                        copy(prev[:, g * BANK:(g + 1) * BANK], sp[2 + g][:]).then_inc(st_out, 1)
                    a.wait_ge(z_done, 1)
                    tgf = tg[:].rearrange("p a b n -> p (a b n)").rearrange("p (m n) -> p m n", m=MT)

                    def seg_act(n):
                        a.wait_ge(seg_done, n + 1)
                        a.activation(seg[:, n % 2], seg[:, n % 2], ACT.Exp).then_inc(seg_exp, 1)

                    def zssd_evac(i):
                        b = done('zssd', i)
                        for m in range(MT):
                            z_evac(gp[(b + m) % 4], BANK, zssd[:, m, i * BANK:(i + 1) * BANK],
                                   tgf[:, m, i * BANK:(i + 1) * BANK])

                    def zatt_evac(i):
                        b = done('zatt', i)
                        z_evac(gp[b % 4], SEQ, zatt[:, i, :], tg[:, 0, i, :])

                    zssd_evac(0)
                    for n in range(4):
                        seg_act(n)
                    zssd_evac(1)
                    seg_act(4)
                    a.wait_ge(z_done, 2)
                    for i in range(4):
                        zatt_evac(i)
                        if i < 3:
                            seg_act(5 + i)
                    for i in range(2):
                        b = done('qmem', i)
                        copy(qmT[:, i, :], gp[b % 4][:, 0:SEQ]).then_inc(taken, 1)

                    def softmax(b):
                        nh, nk = len(BATCH[b][2]), keys_of(b)
                        a.wait_ge(lg_out, b + 1)
                        for n in range(nh):
                            v = LG[:, b % 2, n * nk:(n + 1) * nk]
                            ins = a.activation(v, v, ACT.Exp, bias=smx[:, 0, b % 2, n:n + 1],
                                               accum_out=smx[:, 1, b % 2, n:n + 1])
                        ins.then_inc(lg_exp, 1)

                    def turned(b):
                        a.wait_ge(pt_ps, b + 1)
                        if b >= 2:
                            a.wait_ge(o_ps, b - 1)
                        copy(pT[:, b % 2], sp[2][:]).then_inc(pt_out, 1)

                    def gate_tanh(d, b):
                        for b in (b, b + 1):
                            if d < 2:
                                a.wait_ge(units_done, WHOLE['gate', NB * d + (b | 1)] + 1)
                            else:
                                a.wait_ge(pieces_done, 2 * (SPLIT['gate', NB * d + (b | 1)] + 1))
                            a.activation(tg[:, d % 2, b, :], gp[2 * ((d + 1) % 2) + b // 2][:, (b % 2) * SEQ:(b % 2 + 1) * SEQ],
                                         ACT.Tanh, scale=0.5,
                                         bias=bgh[:, NB * d + b:NB * d + b + 1]).then_inc(gate_t, 1)

                    ng = pv('ng')

                    def ys_evac(m):
                        for q in range(2):
                            a.wait_ge(ys_ps, 2 * m + q + 1)
                            for j in range(4):
                                f = 4 * q + j
                                ins = copy(yT[:, 8 + f, m * P:(m + 1) * P], sp[2 + q][:, j * P:(j + 1) * P],
                                           scale=ng[:, f:f + 1])
                            ins.then_inc(ys_out, 1)

                    for n in range(NSPARSE):
                        softmax(n)
                        if n < 2:
                            b = done('kmem', n)
                            copy(kmT[:, n, :], gp[b % 4][:, 0:SEQ]).then_inc(taken, 1)
                        elif n < 4:
                            b = done('zmem', n - 2)
                            z_evac(gp[b % 4], SEQ, zmem[:, n - 2, :], tg[:, 1, n - 2, :])
                        turned(n)
                    b = done('vmem')
                    for m in range(MT):
                        copy(vm[:, m, :], gp[(b + m) % 4][:, 0:MEMH * HD]).then_inc(taken, 1)
                    for n in range(NSPARSE, len(BATCH)):
                        softmax(n)
                        if n == NSPARSE + 1:
                            a.wait_ge(z_done, 4)
                            gate_tanh(0, 0)
                        turned(n)
                    gate_tanh(0, 2)
                    ys_evac(0)
                    gate_tanh(1, 0)
                    ys_evac(1)
                    gate_tanh(1, 2)
                    copy(x_hi[:], xT[:]).then_inc(xhi_done, 1)

                    piece_slot = [n for n, u in enumerate(STREAM) if u in SPLIT for _ in range(2)]

                    def split(first, last):
                        for p in range(first, min(last, NPIECE)):
                            n = piece_slot[p]
                            if p % 2 == 0:
                                a.wait_ge(slot_full[n % NSLOT], 16 * (n // NSLOT + 1))
                            if p >= NPART:
                                a.wait_ge(pieces_done, p - NPART + 1)
                            copy(w_hi[:, p % NPART], ring[:, n % NSLOT, (p % 2) * PIECE:(p % 2 + 1) * PIECE]
                                 ).then_inc(hi_done, 1)

                    a.wait_ge(o_out, len(BATCH))
                    split(0, NPART)
                    for d in range(2, KT):
                        a.wait_ge(mg_done, d - 1)
                        for b in range(0, NB, 2):
                            first = 2 * SPLIT['gate', NB * d + b]
                            split(first + NPART, first + NPART + 4)
                            gate_tanh(d, b)
                    first = 2 * SPLIT['out', 0] + NPART
                    split(first, first + NPART)
                    a.wait_ge(x_in, 16)
                    for m in range(MT):
                        copy(xtok[:, m, :], xtok[:, m, :], scale=ALPHA).then_inc(ax_done, 1)
                    split(first + NPART, NPIECE)
                    for n in range(8):
                        m, q = n // 4, n % 4
                        a.wait_ge(xt_ps, n + 1)
                        copy(xT[:, 4 * q:4 * q + 4, m * P:(m + 1) * P],
                             sp[q][:].rearrange("p (f t) -> p f t", f=4)).then_inc(xt_out, 1)
                    a.wait_ge(xt_out, 8)

                @block.vector
                def _(v):
                    link, tell = signals(v, v_step)
                    tt, ts, stt = v.tensor_tensor, v.tensor_scalar, v.scalar_tensor_tensor

                    v.wait_ge(par_in, 16)
                    lre, lim = pv('lre'), pv('lim')
                    v.wait_ge(disc_act, 1)
                    link(tt(s5s[:, 1], lre, s5s[:, 0], ALU.mult))
                    link(tt(s5s[:, 2], lim, s5s[:, 0], ALU.mult))
                    link(wrap_angle(v, link, s5s[:, 2], s5s[:, 3], s5s[:, 5], 0.25))
                    tell(wrap_angle(v, link, s5s[:, 2], s5s[:, 4], s5s[:, 5], 0.0), disc_arg)
                    v.wait_ge(disc_act, 2)
                    link(tt(s5s[:, 6], s5s[:, 1], s5s[:, 3], ALU.mult))
                    link(tt(s5s[:, 7], s5s[:, 1], s5s[:, 4], ALU.mult))
                    link(tt(s5s[:, 8], lre, lre, ALU.mult))
                    link(tt(s5s[:, 5], lim, lim, ALU.mult))
                    link(tt(s5s[:, 8], s5s[:, 8], s5s[:, 5], ALU.add))
                    link(v.reciprocal(s5s[:, 8], s5s[:, 8]))
                    link(ts(s5s[:, 9], s5s[:, 6], -1.0, None, ALU.add))
                    link(tt(s5s[:, 10], s5s[:, 9], lre, ALU.mult))
                    link(tt(s5s[:, 5], s5s[:, 7], lim, ALU.mult))
                    link(tt(s5s[:, 10], s5s[:, 10], s5s[:, 5], ALU.add))
                    link(tt(s5s[:, 10], s5s[:, 10], s5s[:, 8], ALU.mult))
                    link(tt(s5s[:, 11], s5s[:, 7], lre, ALU.mult))
                    link(tt(s5s[:, 5], s5s[:, 9], lim, ALU.mult))
                    link(tt(s5s[:, 11], s5s[:, 11], s5s[:, 5], ALU.subtract))
                    link(tt(s5s[:, 11], s5s[:, 11], s5s[:, 8], ALU.mult))
                    link(v.memset(pw5[:, 0, :, 0], 1.0))
                    link(v.memset(pw5[:, 1, :, 0], 0.0))
                    link(v.tensor_copy(pw5[:, 0, :, 1], s5s[:, 6]))
                    link(v.tensor_copy(pw5[:, 1, :, 1], s5s[:, 7]))
                    for j in range(2, Q5 + 1):
                        x1, x2 = j // 2, j - j // 2
                        link(tt(s5s[:, 12], pw5[:, 0, :, x1], pw5[:, 0, :, x2], ALU.mult))
                        link(tt(s5s[:, 13], pw5[:, 1, :, x1], pw5[:, 1, :, x2], ALU.mult))
                        link(tt(pw5[:, 0, :, j], s5s[:, 12], s5s[:, 13], ALU.subtract))
                        link(tt(s5s[:, 12], pw5[:, 0, :, x1], pw5[:, 1, :, x2], ALU.mult))
                        link(tt(s5s[:, 13], pw5[:, 1, :, x1], pw5[:, 0, :, x2], ALU.mult))
                        link(tt(pw5[:, 1, :, j], s5s[:, 12], s5s[:, 13], ALU.add))
                    link(ts(pw5[:, 2], pw5[:, 1], -1.0, None, ALU.mult))
                    for i, k in ((0, 0), (1, 0)):
                        link(v.tensor_copy(am5[:, 0, i], pw5[:, k, :, Q5]))
                    link(v.tensor_copy(am5[:, 1, 0], pw5[:, 2, :, Q5]))
                    link(v.tensor_copy(am5[:, 1, 1], pw5[:, 1, :, Q5]))
                    bre = pv('bre').rearrange("p (g h) -> p g h", g=PAIRS)
                    bim = pv('bim').rearrange("p (g h) -> p g h", g=PAIRS)
                    cre = pv('cre').rearrange("p (g h) -> p g h", g=PAIRS)
                    cim = pv('cim').rearrange("p (g h) -> p g h", g=PAIRS)
                    fr = s5s[:, 10].unsqueeze(2).to_broadcast([P, PAIRS, H5])
                    fi = s5s[:, 11].unsqueeze(2).to_broadcast([P, PAIRS, H5])
                    xsf = wide[:, 0:D]
                    gflat1 = sflat
                    gflat2 = tg[:].rearrange("p a b n -> p (a b n)")
                    v.memset(xb[:, :, 0:CONV - 1], 0.0)
                    t1 = xsf[:, 0:PAIRS * H5].rearrange("p (g h) -> p g h", g=PAIRS)
                    t2 = xsf[:, BANK:BANK + PAIRS * H5].rearrange("p (g h) -> p g h", g=PAIRS)
                    for r, (fa, fb, op) in enumerate(((fr, fi, ALU.subtract), (fi, fr, ALU.add))):
                        link(tt(t1, bre, fa, ALU.mult))
                        link(tt(t2, bim, fb, ALU.mult))
                        for h in range(2):
                            rows = slice(P5 * h, P5 * (h + 1))
                            link(tt(BD[rows, r, :, H5 * h:H5 * (h + 1)], t1[rows], t2[rows], op))
                    big = xsf.rearrange("p (g s h) -> p g s h", g=PAIRS, s=Q5)
                    for r in range(2):
                        dst = V5[:, r, :].rearrange("p (g s h) -> p g s h", g=PAIRS, s=Q5)
                        pa, pb = (0, 1) if r == 0 else (1, 0)

                        def pw(k):
                            return pw5[:, k, :, 0:Q5][:, :, ::-1].unsqueeze(3).to_broadcast([P, PAIRS, Q5, 2 * H5])

                        def bd(k):
                            return BD[:, k].unsqueeze(2).to_broadcast([P, PAIRS, Q5, 2 * H5])

                        link(tt(dst, bd(0), pw(pa), ALU.mult))
                        link(tt(big, bd(1), pw(pb), ALU.mult))
                        ins = tt(dst, dst, big, ALU.subtract if r == 0 else ALU.add)
                        if r == 0:
                            link(ins)
                    tell(ins, v5_ready)
                    g1 = gflat1[:, 0:PAIRS * (Q5 + 1) * H5].rearrange("p (g j h) -> p g j h", g=PAIRS, j=Q5 + 1)
                    g2 = gflat2[:, 0:PAIRS * (Q5 + 1) * H5].rearrange("p (g j h) -> p g j h", g=PAIRS, j=Q5 + 1)
                    v.wait_ge(v5_ready, 1)
                    v.wait_ge(gd_zero, 1)
                    full = [P, PAIRS, Q5 + 1, H5]
                    for r, (ka, kb) in enumerate(((0, 1), (2, 0))):
                        link(tt(g1, cre.unsqueeze(2).to_broadcast(full), pw5[:, ka].unsqueeze(3).to_broadcast(full),
                                ALU.mult))
                        link(tt(g2, cim.unsqueeze(2).to_broadcast(full), pw5[:, kb].unsqueeze(3).to_broadcast(full),
                                ALU.mult))
                        for h in range(2):
                            rows = slice(P5 * h, P5 * (h + 1))
                            ins = tt(GD[rows, r, :, :, H5 * h:H5 * (h + 1)], g1[rows], g2[rows], ALU.subtract)
                        if r == 0:
                            link(ins)
                    tell(ins, g5_ready)
                    v.wait_ge(g5_ready, 1)
                    link(ts(bgh[:, 0:KT * NB], pv('bg'), 0.5, None, ALU.mult))
                    tell(ts(bgh[:, KT * NB:], pv('bglu'), 0.5, None, ALU.mult), half_done)
                    link(ts(wconv[:], prm[:, PO['cw'][0]:PO['cb'][1]], 0.5, None, ALU.mult))
                    b = START['small', 0]
                    v.wait_ge(taken, b + 2)
                    link(tt(dts[:, 9], tok[:, :, C_DT:TOKW], pv('dtb').unsqueeze(1).to_broadcast([P, MT, SSDH]),
                            ALU.add))
                    tell(stt(dts[:, 6], dts[:, 9], -1.0, dts[:, 9], ALU.mult, ALU.min), dt_arg)
                    v.wait_ge(dt_exp, 1)
                    tell(ts(dts[:, 7], dts[:, 6], 1.0, None, ALU.add), dt_u)
                    v.wait_ge(dt_u, 1)
                    link(ts(dts[:, 2], dts[:, 7], -1.0, None, ALU.add))
                    link(tt(dts[:, 2], dts[:, 6], dts[:, 2], ALU.subtract))
                    link(v.reciprocal(dts[:, 3], dts[:, 7]))
                    link(tt(dts[:, 2], dts[:, 2], dts[:, 3], ALU.mult))
                    v.wait_ge(k5_out, 4)
                    kd = gflat2[0:32, 0:PAIRS * 32].rearrange("p (g n) -> p g n", g=PAIRS)
                    link(tt(kd, ident[0:32, 0:32].unsqueeze(1).to_broadcast([32, PAIRS, 32]),
                            pv('dsk', 32).unsqueeze(2).to_broadcast([32, PAIRS, 32]), ALU.mult))
                    k0 = K5.rearrange("p (g n) -> p g n", g=PAIRS)[:, :, 0:32]
                    tell(tt(k0, k0, kd, ALU.add), k5_diag)
                    v.wait_ge(dt_ln, 1)
                    link(tt(dts[:, 2], dts[:, 8], dts[:, 2], ALU.add))
                    link(stt(dt, dts[:, 9], 0.0, dts[:, 2], ALU.max, ALU.add))
                    v.wait_ge(a_step, 1)
                    link(tt(da, dt, dts[:, 5, 0].unsqueeze(1).to_broadcast([P, MT, SSDH]), ALU.mult))
                    tell(ts(da, da, -1.0, None, ALU.mult), da_done)

                    def conv(i):
                        v.wait_ge(taken, START['xbc', i] + 1)
                        c = cv[:, i % 2]
                        wc = wconv[:, CONV * i:CONV * (i + 1)]
                        link(ts(c, xb[:, i, 0:SEQ], wc[:, 0:1], wconv[:, XT * CONV + i:XT * CONV + i + 1],
                                ALU.mult, ALU.add))
                        for j in range(1, CONV):
                            ins = stt(c, xb[:, i, j:j + SEQ], wc[:, j:j + 1], c, ALU.mult, ALU.add)
                            if j < CONV - 1:
                                link(ins)
                        tell(ins, conv_done)

                    def silu(i):
                        v.wait_ge(conv_t, i + 1)
                        tell(stt(xb[:, i, CONV - 1:], th[:, i % 2], 1.0, cv[:, i % 2], ALU.add,
                            ALU.mult), xbc_done)

                    for i in range(XT):
                        conv(i)
                        if i:
                            silu(i - 1)
                    silu(XT - 1)
                    v.wait_ge(taken, START['tok', 1] + 2)
                    heads = tok[:, :, 0:ROPED * HD].rearrange("p m (h e) -> p m h e", e=HD)
                    half = ROPE // 2
                    xa, xc = heads[:, :, :, 0:half], heads[:, :, :, half:ROPE]
                    shape = [P, MT, ROPED, half]
                    co = cs[:, 0].unsqueeze(2).to_broadcast(shape)
                    si = cs[:, 1].unsqueeze(2).to_broadcast(shape)
                    for m in range(MT):
                        link(tt(rt[:, 0, m], xa[:, m], co[:, m], ALU.mult))
                        link(tt(rt[:, 1, m], xc[:, m], si[:, m], ALU.mult))
                        link(tt(rt[:, 2, m], xc[:, m], co[:, m], ALU.mult))
                        link(tt(rt[:, 3, m], xa[:, m], si[:, m], ALU.mult))
                        link(tt(xa[:, m], rt[:, 0, m], rt[:, 1, m], ALU.subtract))
                        ins = tt(xc[:, m], rt[:, 2, m], rt[:, 3, m], ALU.add)
                        if m == 0:
                            link(ins)
                    link(ins)
                    v.tensor_copy(ik2[:, :, 0], tok[:, :, 14 * HD:15 * HD])
                    tell(v.tensor_copy(ik2[:, :, 1], tok[:, :, 14 * HD:15 * HD]), rope_done)
                    link(ts(wi[:], tok[:, :, C_IW:C_DT], IDX_SCALE, None, ALU.mult))
                    v.wait_ge(acs_ps, 1)
                    tell(v.tensor_copy(acs, sp[0][:, 0:MT * SSDH].rearrange("p (m h) -> p m h", m=MT)), acs_out)
                    v.wait_ge(acs_out, 1)
                    tell(tt(dec[:, 0], sp[0][:, 64:64 + SSDH], acs[:, 0], ALU.subtract), acs_arg)
                    v.wait_ge(cb_ps, 1)
                    tell(v.tensor_copy(cbT[:].rearrange("p c g n -> p (c g n)"), sp[1][:]), cb_out)
                    v.wait_ge(xs_out, 4)
                    hp = [P, MT, SSDH, HD]
                    x4 = xs.rearrange("p m (h e) -> p m h e", e=HD)
                    d4 = xdt.rearrange("p m (h e) -> p m h e", e=HD)
                    for m in range(MT):
                        link(tt(d4[:, m], x4[:, m], dt[:, m].unsqueeze(2).to_broadcast(hp[0:1] + hp[2:]), ALU.mult))
                    v.wait_ge(acs_exp, 1)
                    tell(tt(xdd.rearrange("p (h e) -> p h e", e=HD), d4[:, 0],
                       dec[:, 0].unsqueeze(2).to_broadcast([P, SSDH, HD]), ALU.mult), xdt_done)
                    for m in range(MT):
                        link(tt(x4[:, m], x4[:, m], pv('dh').unsqueeze(2).to_broadcast([P, SSDH, HD]), ALU.mult))
                    for hf in range(2):
                        v.wait_ge(y5_ps, hf + 1)
                        for j in range(8):
                            gi = 8 * hf + j
                            dst = y5[32 * (gi % 4):32 * (gi % 4) + 32, gi // 4, :].rearrange("p (c q) -> p q c", q=Q5)
                            for q in range(Q5):
                                ins = v.tensor_copy(dst[:, q, :], sp[2 + hf][32 * q:32 * q + 32, j * C5:(j + 1) * C5])
                        tell(ins, y5_out)
                    v.wait_ge(y5_out, 2)
                    yf = y5[:].rearrange("p a t -> p (a t)")
                    lf = LG.rearrange("p a n -> p (a n)")
                    link(tt(lf, yf, yf, ALU.mult))
                    link(ts(lf, lf, 0.044715, 1.0, ALU.mult, ALU.add))
                    tell(tt(lf, lf, yf, ALU.mult), gelu_arg)
                    link(ts(yf, yf, 0.5, None, ALU.mult))
                    zf = z5[:].rearrange("p a t -> p (a t)")
                    v.wait_ge(taken, START['z5', 3] + 1)
                    tell(stt(zf, tg[:, 0].rearrange("p b n -> p (b n)"), 1.0, zf, ALU.add, ALU.mult), z_done)
                    v.wait_ge(gelu_t, 1)
                    tell(stt(yf, lf, 1.0, yf, ALU.add, ALU.mult), gelu_done)

                    for qb in range(MT):
                        nk = (qb + 1) * P
                        sc, sm = sco[:, 0:nk], stm[:, 0:nk]
                        v.wait_ge(ix_ps, qb + 1)
                        for h in range(IH):
                            ps = sp[h % 2][:, (h // 2) * SEQ:(h // 2) * SEQ + nk]
                            ins = ts(sm if h else sc, ps, 0.0, wi[:, qb, h:h + 1], ALU.max, ALU.mult)
                            if h == IH - 1:
                                tell(ins, ix_out)
                                v.wait_ge(ix_out, qb + 1)
                            else:
                                link(ins)
                            if h:
                                link(tt(sc, sc, sm, ALU.add))
                        vis = seen[:, SEQ - nk:SEQ]
                        link(tt(sc, sc, vis, ALU.add))
                        for _r in range(TOPK // 8):
                            link(v.max(top[:], sc))
                            link(v.match_replace(sc, top[:], sc, TAKEN))
                        link(ts(sc, sc, TAKEN / 1.5, MASKED, ALU.is_gt, ALU.mult))
                        link(tt(amask[:, qb, 0:nk], sc, vis, ALU.add))
                    v.wait_ge(glu_t, 4)
                    link(stt(yf, pT.rearrange("p a n -> p (a n)"), 1.0, yf, ALU.add, ALU.mult))
                    tell(stt(yT[:, 0:4, :].rearrange("p a t -> p (a t)"), yf, 0.25, zf, ALU.mult,
                        ALU.mult), s5_done)

                    def seg_arg(n):
                        c, rd = n // 4, n % 4
                        sg = seg[:, n % 2].rearrange("p (h l) -> p h l", h=4)
                        if n >= 2:
                            v.wait_ge(yd_ps, n - 1)
                        v.wait_ge(ab_ps, n + 1)
                        link(tt(sg, sp[0][:].rearrange("p (h l) -> p h l", h=4),
                                acs[:, c, 4 * rd:4 * rd + 4].unsqueeze(2).to_broadcast([P, 4, P]), ALU.subtract))
                        tell(tt(sg, sg, maskT[:].unsqueeze(1).to_broadcast([P, 4, P]), ALU.add), seg_done)

                    def seg_mul(n):
                        c, rd = n // 4, n % 4
                        sg = seg[:, n % 2].rearrange("p (h l) -> p h l", h=4)
                        v.wait_ge(seg_exp, n + 1)
                        tell(tt(sg, sg, cbT[:, c, rd // 2].unsqueeze(1).to_broadcast([P, 4, P]), ALU.mult), m_done)

                    def y_in(c):
                        v.wait_ge(yd_ps, 4 * (c + 1))
                        for b in range(2):
                            d = xs[:, c, b * BANK:(b + 1) * BANK]
                            tell(tt(d, d, sp[2 + b][:], ALU.add), yd_out)

                    for n in range(8):
                        if n:
                            seg_mul(n - 1)
                        seg_arg(n)
                        if n == 4:
                            y_in(0)
                            v.wait_ge(taken, START['zssd', 1] + 2)
                            zsf = zssd.rearrange("p m n -> p (m n)")
                            tell(stt(zsf, tg[:].rearrange("p a b n -> p (a b n)"), 1.0, zsf, ALU.add, ALU.mult),
                                 z_done)
                    seg_mul(7)
                    for g in range(SSDG):
                        v.wait_ge(yo_ps, g + 1)
                        tmp = cv.rearrange("p a n -> p (a n)").rearrange("p (h e) -> p h e", e=HD)
                        tell(tt(tmp, sp[1][:].rearrange("p (h e) -> p h e", e=HD),
                           eacs[:, 1, 8 * g:8 * g + 8].unsqueeze(2).to_broadcast([P, 8, HD]),
                           ALU.mult), yo_out)
                        v.wait_ge(yo_out, g + 1)
                        d = x4[:, 1, 8 * g:8 * g + 8]
                        link(tt(d, d, tmp, ALU.add))
                    y_in(1)
                    v.wait_ge(yd_out, 4)
                    v.wait_ge(z_done, 2)
                    link(stt(xsf, xsf, 0.5, zsf, ALU.mult, ALU.mult))
                    for m in range(MT):
                        for g in range(SSDG):
                            y = xs[:, m, g * BANK:(g + 1) * BANK]
                            link(stt(cv.rearrange("p a n -> p (a n)"), y, 1.0, y, ALU.mult, ALU.mult,
                                     accum_out=rms[:, 0, m, g:g + 1]))
                    tell(ts(rms[:, 0], rms[:, 0], 1.0 / BANK, RMS_EPS, ALU.mult, ALU.add), rms_arg)
                    v.wait_ge(rms_pow, 1)
                    for m in range(MT):
                        for g in range(SSDG):
                            y = xs[:, m, g * BANK:(g + 1) * BANK]
                            ins = ts(y, y, rms[:, 1, m, g:g + 1], None, ALU.mult)
                        tell(ins, ys_done)
                    v.wait_ge(taken, START['zatt', 3] + 1)
                    zaf = zatt[:].rearrange("p a t -> p (a t)")
                    zmf = zmem[:].rearrange("p a t -> p (a t)")
                    tell(stt(zaf, tg[:, 0].rearrange("p b n -> p (b n)"), 1.0, zaf, ALU.add, ALU.mult), z_done)

                    def scaled(b):
                        sparse, qb, heads = BATCH[b]
                        nk, nh = keys_of(b), len(BATCH[b][2])
                        v.wait_ge(lg_ps, b + 1)
                        if b >= 2:
                            v.wait_ge(pt_ps, b - 1)
                        lg = LG[:, b % 2].rearrange("p (h k) -> p h k", h=nh)
                        for half in range(2):
                            ps = sp[half][:, 0:SEQ].rearrange("p (h k) -> p h k", k=nk)
                            lh = lg[:, half * nh // 2:(half + 1) * nh // 2]
                            if sparse:
                                link(stt(lh, ps, ATT_SCALE,
                                         amask[:, qb, 0:nk].unsqueeze(1).to_broadcast([P, nh // 2, nk]),
                                         ALU.mult, ALU.add))
                            else:
                                link(ts(lh, ps, ATT_SCALE, None, ALU.mult))
                        tell(v.tensor_reduce(smx[:, 0, b % 2, 0:nh], lg, AX.X, ALU.max, negate=True), lg_out)

                    def normed(b):
                        nk, nh = keys_of(b), len(BATCH[b][2])
                        v.wait_ge(lg_exp, b + 1)
                        link(v.reciprocal(smx[:, 2, b % 2, 0:nh], smx[:, 1, b % 2, 0:nh]))
                        lg = LG[:, b % 2].rearrange("p (h k) -> p h k", h=nh)
                        tell(tt(lg, lg, smx[:, 2, b % 2, 0:nh].unsqueeze(2).to_broadcast([P, nh, nk]),
                           ALU.mult), p_done)

                    def gated(b):
                        sparse, qb, heads = BATCH[b]
                        v.wait_ge(o_ps, b + 1)
                        f, n = heads[0][0], len(heads) // 2
                        z = (zatt if sparse else zmem)[:, f:f + n, qb * P:(qb + 1) * P]
                        k = KOF[1 if sparse else 3][0]
                        tell(stt(yT[:, k + f:k + f + n, qb * P:(qb + 1) * P], sp[3][:, 0:n * P].rearrange("p (f t) -> p f t", f=n),
                            0.5, z, ALU.mult, ALU.mult), o_out)

                    for b in range(len(BATCH)):
                        scaled(b)
                        normed(b)
                        if b:
                            gated(b - 1)
                        if b == NSPARSE - 1:
                            v.wait_ge(taken, START['zmem', 1] + 1)
                            tell(stt(zmf, tg[:, 1, 0:2].rearrange("p b n -> p (b n)"), 1.0, zmf, ALU.add,
                                ALU.mult), z_done)
                    gated(len(BATCH) - 1)
                    v.wait_ge(xhi_done, 1)
                    tell(tt(x_lo[:], xT[:], x_hi[:].bitcast(F32), ALU.subtract), xlo_done)
                    for d in range(KT):
                        pair = 2 * (d % 2)
                        v.wait_ge(units_done, WHOLE['branch', d] + 1)
                        v.wait_ge(gate_t, NB * (d + 1))
                        for i in range(2):
                            link(stt(mg[:, i], tg[:, d % 2, 2 * i:2 * i + 2].rearrange("p b n -> p (b n)"), 1.0,
                                     sp[pair + i][:], ALU.add, ALU.mult))
                        link(tt(mg[:, 0], mg[:, 0], mg[:, 1], ALU.add))
                        total = mg[:, 1, 0:SEQ]
                        link(tt(total, mg[:, 0, 0:SEQ], mg[:, 0, SEQ:], ALU.add))
                        link(v.tensor_copy(m_hi[:, d, :], total))
                        tell(tt(m_lo[:, d, :], total, m_hi[:, d, :].bitcast(F32), ALU.subtract), mg_done)
                    v.wait_ge(ax_done, MT)
                    for c in range(4):
                        v.wait_ge(pieces_done, 2 * (SPLIT['out', 4 * c + 3] + 1))
                        for m in range(MT):
                            n = MT * c + m
                            xv = xtok[:, m, c * BANK:(c + 1) * BANK]
                            tell(stt(xv, gp[2 * ((c + 1) % 2) + m][:], 0.5, xv, ALU.mult, ALU.add), res_done)
                            v.wait_ge(res_done, n + 1)
                            link(v.bn_stats(st6[:, m, c, :], xv))
                    v.wait_ge(lng_in, 16)
                    v.wait_ge(lnb_in, 16)
                    gf, bf = lng, lnb
                    for m in range(MT):
                        link(v.bn_aggr(mv[:, m, 0:2], st6[:, m].rearrange("p c s -> p (c s)")))
                        tell(ts(mv[:, m, 2:3], mv[:, m, 1:2], LN_EPS, None, ALU.add), var_done)
                    for m in range(MT):
                        v.wait_ge(rstd_done, m + 1)
                        xm = xtok[:, m, :]
                        link(ts(xm, xm, mv[:, m, 0:1], mv[:, m, 2:3], ALU.subtract, ALU.mult))
                        link(tt(xm, xm, gf, ALU.mult))
                        tell(tt(xm, xm, bf, ALU.add), ln_done)
            nc.multi_engine_barrier(mybir.ALL_ENGINES, sems_to_clear=clear)


def kernel(**inputs):
    import concourse.bacc as bacc
    from concourse.bass_utils import run_bass_kernel_spmd

    a = {k: np.asarray(v) for k, v in inputs.items()}
    sizes = (('s5_u', 512), ('s5_z', 512), ('att_q', 512), ('att_k', 128), ('att_v', 128), ('att_z', 512),
             ('idx_q', 256), ('idx_k', 64), ('idx_w', 4), ('ssd_z', 1024), ('ssd_xbc', XBC), ('ssd_dt', 16),
             ('mem_q', 256), ('mem_z', 256), ('gates', NB * D))
    col, o = {}, 0
    for name, n in sizes:
        col[name] = np.arange(o, o + n)
        o += n
    order = np.concatenate([np.arange(HD) + HD * (j + AKV * 2 * h) for j in range(4) for h in range(2)])
    win, wkv = a['w_in'], a['mem_w_kv']

    def t_units(m):
        n = m.shape[2] // P
        return m.reshape(DEPTH, KT, P, n, P).transpose(0, 3, 2, 1, 4).reshape(DEPTH, n, P, KT * P)

    def m_units(m, cols, per):
        k, n = m.shape[1] // P, m.shape[2] // cols
        u = m.reshape(DEPTH, k // per, per, P, n, cols).transpose(0, 4, 1, 3, 2, 5)
        return u.reshape(DEPTH, n * (k // per), P, per * cols)

    tokc = np.concatenate([col['att_q'][order], col['att_k'], col['idx_q'], col['idx_k'], col['att_v'],
                           col['idx_w'], col['ssd_dt']])
    gates = win[:, :, col['gates']].reshape(DEPTH, D, NB, KT, P).transpose(0, 1, 3, 2, 4).reshape(DEPTH, D, NB * D)
    wbr = np.concatenate([a['w_br_s5'], a['w_br_attn'][:, order], a['w_br_ssd'], a['w_br_mem']], axis=1)
    arrays = {
        'u5': t_units(win[:, :, col['s5_u']]), 'z5': t_units(win[:, :, col['s5_z']]),
        'xbc': t_units(win[:, :, col['ssd_xbc']]), 'zatt': t_units(win[:, :, col['att_z'][order]]),
        'qmem': t_units(win[:, :, col['mem_q']]), 'zmem': t_units(win[:, :, col['mem_z']]),
        'kmem': t_units(wkv[:, :, :MEMH * HD]), 'vmem': m_units(wkv[:, :, MEMH * HD:], MEMH * HD, 8),
        'gate': t_units(gates), 'tok': m_units(win[:, :, tokc[:2 * BANK]], BANK, 4),
        'small': m_units(win[:, :, tokc[2 * BANK:]], SMALL, KT), 'zssd': m_units(win[:, :, col['ssd_z']], BANK, 4),
        'glu': m_units(a['s5_w_glu'], BANK, 4), 'out': m_units(a['w_out'], BANK, 4),
        'branch': wbr.reshape(DEPTH, KB, P, KT, P).transpose(0, 3, 2, 1, 4).reshape(DEPTH, KT, P, SLOT),
    }
    kinds = list(arrays)

    def state(m):
        rest = m.shape[3:]
        m = m.reshape((DEPTH, PAIRS, 2, P5) + rest)
        return np.moveaxis(m, 1, 3).reshape(DEPTH, P, -1)

    def rows(m):
        return np.broadcast_to(m[:, None, :], (DEPTH, P, m.shape[1]))

    def per_feature(m):
        return m.reshape(DEPTH, -1, P).transpose(0, 2, 1)

    dsk = a['s5_d'].reshape(DEPTH, PAIRS, 2 * H5).transpose(0, 2, 1)
    parts = {
        'lre': state(a['s5_lam_re']), 'lim': state(a['s5_lam_im']),
        'ldt': state(np.broadcast_to(a['s5_log_dt'][:, :, None], (DEPTH, G5, P5))),
        'bre': state(a['s5_b_re']), 'bim': state(a['s5_b_im']),
        'cre': state(a['s5_c_re'].transpose(0, 1, 3, 2)), 'cim': state(a['s5_c_im'].transpose(0, 1, 3, 2)),
        'dsk': np.tile(dsk, (1, 4, 1)), 'bglu': per_feature(a['s5_b_glu']),
        'cw': a['ssd_conv_w'].reshape(DEPTH, CONV, XT, P).transpose(0, 3, 2, 1).reshape(DEPTH, P, XT * CONV),
        'cb': per_feature(a['ssd_conv_b']), 'dtb': rows(a['ssd_dt_bias']), 'alog': rows(a['ssd_a_log']),
        'dh': rows(a['ssd_d']), 'ng': per_feature(a['ssd_norm_g']),
        'bg': a['b_gate'].reshape(DEPTH, NB, KT, P).transpose(0, 3, 2, 1).reshape(DEPTH, P, KT * NB),
    }
    arrays['par'] = np.concatenate([parts[n] for n, _ in PARAMS], axis=2)

    def t_tokens(m):
        return m[0].T.reshape(KT, P, SEQ).transpose(1, 0, 2)

    arrays['x'] = a['x'][0]
    arrays['x_t'] = t_tokens(a['x'])
    arrays['mem_t'] = t_tokens(a['mem'])
    arrays['pos'] = a['positions'][0].reshape(MT, P).T
    arrays['ln_g'] = a['ln_g']
    arrays['ln_b'] = a['ln_b']
    arrays = {f"in_{k}": np.ascontiguousarray(v) for k, v in arrays.items()}
    nc = bacc.Bacc("TRN2", target_bir_lowering=False, num_devices=1)
    ap = {k: nc.dram_tensor(k, v.shape, mybir.dt.from_np(v.dtype), kind="ExternalInput").ap()
          for k, v in arrays.items()}
    out = nc.dram_tensor("out", (SEQ, D), F32, kind="ExternalOutput").ap()
    build(nc, ap['in_x'], ap['in_x_t'], ap['in_mem_t'], ap['in_pos'], {k: ap[f"in_{k}"] for k in kinds},
          ap['in_par'], ap['in_ln_g'], ap['in_ln_b'], out)
    r = run_bass_kernel_spmd(nc, [arrays], core_ids=[0])
    return r.results[0]["out"].reshape(1, SEQ, D)
```

```python
import math
from contextlib import ExitStack

import numpy as np
import concourse.bass as bass
from concourse import mybir

F32 = mybir.dt.float32
F32R = mybir.dt.float32r
I32 = mybir.dt.int32
ALU = mybir.AluOpType
ACT = mybir.ActivationFunctionType
AX = mybir.AxisListType

P = 128
D = 2048
SEQ = 256
DEPTH = 2
KT = D // P
MT = SEQ // P
BANK = 512
S5W, G5, H5, P5 = 512, 32, 16, 64
PAIRS = G5 // 2
Q5 = 4
GDW = 2 * PAIRS * (Q5 + 1) * 2 * H5
C5 = SEQ // Q5
HD = 64
AH, AKV, IH = 8, 2, 4
TOPK = 64
SSDW, SSDH, SSDN, SSDG = 1024, 16, 128, 2
XBC = SSDW + 2 * SSDG * SSDN
XT = XBC // P
CONV = 4
MEMH = 4
NB = 4
ROPE = 16
THETA = 500000.0
ALPHA = (2 * DEPTH) ** 0.25
LN_EPS = 1e-5
RMS_EPS = 1e-5
IDX_SCALE = (IH ** -0.5) * (HD ** -0.5)
ATT_SCALE = HD ** -0.5
MASKED = -1e30
TAKEN = -3e38
GELU_C = math.sqrt(2.0 / math.pi)
ROUND = 12582912.0
TWO_PI = (6.28125, 0.0019340515136718750, 1.2556659146e-06)
PI_LO = 3.1415925

UNIT = KT * P
KB = (S5W + AH * HD + SSDW + MEMH * HD) // P
SLOT = KB * P // 2
NRAW = 4
NPART = 3
EARLY = 1

ROPED = AH + AKV + IH + 1
C_V = ROPED * HD
C_IW = C_V + AKV * HD
C_DT = C_IW + IH
TOKW = C_DT + SSDH
SMALL = TOKW - 2 * BANK

PARAMS = (('lre', PAIRS), ('lim', PAIRS), ('ldt', PAIRS), ('bre', PAIRS * H5), ('bim', PAIRS * H5),
          ('cre', PAIRS * H5), ('cim', PAIRS * H5), ('dsk', PAIRS), ('bglu', S5W // P), ('cw', XT * CONV),
          ('cb', XT), ('dtb', SSDH), ('alog', SSDH), ('dh', SSDH), ('ng', SSDW // P), ('bg', KT * NB))
PW = sum(n for _, n in PARAMS)
PO = {}
_o = 0
for _n, _w in PARAMS:
    PO[_n] = (_o, _o + _w)
    _o += _w

STREAM = ([('u5', i) for i in range(4)] + [('small', 0)] + [('kmem', i) for i in range(2)]
          + [('vmem', i) for i in range(2)] + [('xbc', i) for i in range(XT)]
          + [('tok', i) for i in range(8)] + [('z5', i) for i in range(4)]
          + [('zssd', 0), ('glu', 0)] + [('zssd', i) for i in range(1, 8)] + [('zatt', i) for i in range(4)]
          + [('qmem', i) for i in range(2)] + [('zmem', i) for i in range(2)])
for _d in range(KT):
    STREAM += [('gate', NB * _d + _b) for _b in range(NB)]
    if _d >= 2:
        STREAM += [('branch', 0), ('branch', 1)] if _d == 2 else [('branch', _d - 1)]
STREAM += [('branch', KT - 1)] + [('out', i) for i in range(16)]
AT = {u: n for n, u in enumerate(STREAM)}
WIDTH = {'small': KT * SMALL, 'branch': KB * P}
WHOLE = {u: n for n, u in enumerate(u for u in STREAM if u[0] in ('kmem', 'vmem', 'glu'))}
SPLIT = {u: n for n, u in enumerate(u for u in STREAM if u not in WHOLE)}
NPIECE = 2 * len(SPLIT)
PIECES = [(2 * AT[u] + half, WIDTH.get(u[0], UNIT) // 2) for u in SPLIT for half in range(2)]


def build(nc, x, x_t, mem_t, pos, w, par, ln_g, ln_b, out):
    ctx = ExitStack()
    with ctx:
        def sb(name, shape, dt=F32):
            return ctx.enter_context(nc.sbuf_tensor(name, shape, dt))

        def place():
            return -(-nc.sbuf_base // 32) * 32

        sems = []

        def sem(name):
            s = ctx.enter_context(nc.semaphore(name))
            sems.append(s)
            return s

        x_at = place()
        xT = sb("xT", [P, KT, SEQ])
        x_hi = sb("x_hi", [P, KT, SEQ], F32R)
        ring = sb("ring", [P, NRAW, SLOT])
        w_hi = sb("w_hi", [P, NPART, SLOT], F32R)
        w_lo = sb("w_lo", [P, NPART, SLOT], F32R)
        y_at = place()
        yT = sb("yT", [P, KB, SEQ])
        prm = sb("prm", [P, PW])
        ident = sb("ident", [P, P])
        tri = sb("tri", [P, P])
        maskT = sb("maskT", [P, P])
        seen = sb("seen", [P, SEQ])
        ones = sb("ones", [P, P])
        cs = sb("cs", [P, 2, MT, ROPE // 2])
        posi = sb("posi", [P, MT], I32)
        angw = sb("angw", [P, 4, MT * ROPE // 2])
        expo = sb("expo", [P, MT])

        U = sb("U", [P, PAIRS, C5])
        wide_at = place()
        wide = sb("wide", [P, 2 * D])
        W5 = wide[:, :].rearrange("p (r g n) -> p r g n", r=2, g=PAIRS)
        xs = wide[:, 0:D].rearrange("p (m n) -> p m n", m=MT)
        xdt = wide[:, D:2 * D].rearrange("p (m n) -> p m n", m=MT)
        gd_at = place()
        GD = sb("GD", [P, 2, PAIRS, Q5 + 1, 2 * H5])
        xb_at = place()
        xb = sb("xb", [P, XT, SEQ + CONV - 1])
        ST = sb("ST", [P, C5 + 1, 2, PAIRS])
        y5 = sb("y5", [P, 4, SEQ])
        BD = y5[:, :, :].rearrange("p a t -> p (a t)").rearrange(
            "p (r g h) -> p r g h", r=2, g=PAIRS)
        z5 = sb("z5", [P, 4, SEQ])
        yflat = yT[:, :, :].rearrange("p f t -> p (f t)")
        T5 = yflat[:, 8 * SEQ:16 * SEQ].rearrange("p (g n) -> p g n", g=PAIRS)
        sflat = ST[:, 1:C5 + 1, :, :].rearrange("p c r g -> p (c r g)")
        K5 = sflat[0:32, :]
        zssd = sflat.rearrange("p (m n) -> p m n", m=MT)
        V5 = yT[:, 0:16, :].rearrange("p (r a) t -> p r (a t)", r=2)
        s5s = sb("s5s", [P, 16, PAIRS])
        pw5 = sb("pw5", [P, 3, PAIRS, Q5 + 1])
        sc5 = sb("sc5", [P, 2, 2, PAIRS])
        am5 = sb("am5", [P, 2, 2, PAIRS])

        tok = sb("tok", [P, MT, TOKW])
        ik2 = sb("ik2", [P, MT, 2, HD])
        qkT = sb("qkT", [P, 8, SEQ])
        gflat = GD[:, :, :, :, :].rearrange("p r g j h -> p (r g j h)")
        LG = gflat[:, 0:2 * BANK].rearrange("p (a n) -> p a n", a=2)
        pT = gflat[:, 2 * BANK:4 * BANK].rearrange("p (a n) -> p a n", a=2)
        sco = gflat[:, 2048:2048 + SEQ]
        stm = gflat[:, 2304:2304 + SEQ]
        amask = gflat[:, 2560:2560 + 2 * SEQ].rearrange("p (m n) -> p m n", m=MT)
        top = sb("top", [P, 8])
        wi = sb("wi", [P, MT, IH])
        smx = sb("smx", [P, 3, 2, 4])

        xflat = xb[:, :, :].rearrange("p f t -> p (f t)")
        zatt = xflat[:, 0:1024].rearrange("p (f t) -> p f t", f=4)
        qmT = xflat[:, 1024:1536].rearrange("p (f t) -> p f t", f=2)
        kv = prm[:, PO['bre'][0]:PO['cim'][1]]
        kmT = kv[:, 0:2 * SEQ].rearrange("p (f t) -> p f t", f=2)
        vm = kv[:, 2 * SEQ:4 * SEQ].rearrange("p (m n) -> p m n", m=MT)
        zmem = xflat[:, 2048:2560].rearrange("p (f t) -> p f t", f=2)
        cvth = sb("cvth", [P, 4, SEQ])
        cv, th = cvth[:, 0:2, :], cvth[:, 2:4, :]
        mg = cvth[:, :, :].rearrange("p (a b) n -> p a (b n)", a=2)
        Bt = yflat[:, 6 * SEQ:6 * SEQ + SSDG * SSDN].rearrange("p (g n) -> p g n", g=SSDG)
        prev = U[:, :, :].rearrange("p g c -> p (g c)")
        cbT = yflat[:, 4 * SEQ:4 * SEQ + MT * SSDG * P].rearrange("p (m g n) -> p m g n", m=MT, g=SSDG)
        seg = z5[:, :, :].rearrange("p (a b) t -> p a (b t)", a=2)
        rt = yflat[:, 0:4 * MT * ROPED * ROPE // 2].rearrange(
            "p (i m h f) -> p i m h f", i=4, m=MT, h=ROPED)
        dts = sb("dts", [P, 10, MT, SSDH])
        wconv = sb("wconv", [P, XT * (CONV + 1)])
        rms = sb("rms", [P, 2, MT, SSDG])

        def over(name, shape, at, dt=F32R):
            return nc.alloc_sbuf_tensor_at(name, shape, dt, offset=at)

        x_lo = over("x_lo", [P, KT, SEQ], x_at)
        memT = over("memT", [P, KT, SEQ], xb_at, F32)
        y_hi = over("y_hi", [P, KB, SEQ], xb_at)
        y_lo = over("y_lo", [P, KB, SEQ], y_at)
        xtok = over("xtok", [P, MT, D], xb_at, F32)
        m_hi = over("m_hi", [P, KT, SEQ], wide_at)
        m_lo = over("m_lo", [P, KT, SEQ], gd_at)

        tg = sb("tg", [P, 2, NB, SEQ])
        bgh = sb("bgh", [P, KT * NB + 4])
        lng = tok[:, :, :].rearrange("p m n -> p (m n)")[:, 0:D]
        lnb = qkT[:, :, :].rearrange("p f t -> p (f t)")
        st6 = sb("st6", [P, MT, 4, 6])
        mv = sb("mv", [P, MT, 4])

        gp = [ctx.enter_context(nc.psum_tensor(f"gp{i}", [P, BANK], F32)) for i in range(4)]
        sp = [ctx.enter_context(nc.psum_tensor(f"sp{i}", [P, BANK], F32)) for i in range(4)]

        slot_full = [sem(f"slot_full{i}") for i in range(NRAW)]
        (whole_done, taken, next_in, mem_in, x_in, lng_in, lnb_in, xout, v_step, a_step, g_step,
         disc_arg, disc_act, v5_ready, g5_ready, w5_ps, w5_out, k5_ps, k5_out, k5_diag, t5_out,
         in5_ps, in5_out, scan_done, y5_ps, y5_out, gelu_arg, gelu_t, gelu_done, glu_t, s5_done,
         dt_arg, dt_exp, dt_u, dt_ln, da_done, acs_ps, acs_out, acs_arg, acs_exp,
         conv_done, conv_t, xbc_done, xs_ps, xs_out, cb_ps, cb_out, xdt_done, st_ps, st_out,
         ab_ps, seg_done, seg_exp, m_done, yd_ps, yd_out, yo_ps, yo_out, rms_arg, rms_pow, ys_done, ys_ps, ys_out,
         z_done, rope_done, qk_ps, qk_out, ix_ps, ix_out, lg_ps, lg_out, lg_exp, p_done, pt_ps, pt_out, o_ps, o_out,
         half_done, gate_t, mg_done, ax_done, res_done, var_done, rstd_done, ln_done, xt_ps, xt_out,
         xhi_out, gain_done, c_in, c_out, c_arg, zeroed, hi_done, lo_done, pieces_done, yhi_done, ylo_done) = [sem(n) for n in (
            "whole_done taken next_in mem_in x_in lng_in lnb_in xout v_step a_step g_step "
            "disc_arg disc_act v5_ready g5_ready w5_ps w5_out k5_ps k5_out k5_diag t5_out "
            "in5_ps in5_out scan_done y5_ps y5_out gelu_arg gelu_t gelu_done glu_t s5_done "
            "dt_arg dt_exp dt_u dt_ln da_done acs_ps acs_out acs_arg acs_exp "
            "conv_done conv_t xbc_done xs_ps xs_out cb_ps cb_out xdt_done st_ps st_out "
            "ab_ps seg_done seg_exp m_done yd_ps yd_out yo_ps yo_out rms_arg rms_pow ys_done ys_ps ys_out "
            "z_done rope_done qk_ps qk_out ix_ps ix_out lg_ps lg_out lg_exp p_done pt_ps pt_out o_ps o_out "
            "half_done gate_t mg_done ax_done res_done var_done rstd_done ln_done xt_ps xt_out "
            "xhi_out gain_done c_in c_out c_arg zeroed hi_done lo_done pieces_done yhi_done ylo_done").split()]

        def pv(name, rows=P):
            a, b = PO[name]
            return prm[0:rows, a:b]

        def after(eng, s):
            n = [0]

            def link(ins, also=None):
                n[0] += 1
                ins.then_inc(s, 1)
                eng.wait_ge(s, n[0])
            return link

        def signals(eng, step):
            count = {}

            def tell(ins, s):
                count[s.num] = count.get(s.num, 0) + 1
                ins.then_inc(s, 1)
                eng.wait_ge(s, count[s.num])

            return (lambda ins: tell(ins, step)), tell

        def wrap_angle(v, link, src, dst, t, quarter):
            link(v.tensor_scalar(t, src, 1.0 / (2 * math.pi), quarter, ALU.mult, ALU.add))
            link(v.tensor_scalar(t, t, ROUND, None, ALU.add))
            link(v.tensor_scalar(t, t, -ROUND, None, ALU.add))
            link(v.scalar_tensor_tensor(dst, t, -TWO_PI[0], src, ALU.mult, ALU.add))
            for part in TWO_PI[1:]:
                link(v.scalar_tensor_tensor(dst, t, -part, dst, ALU.mult, ALU.add))
            if quarter:
                link(v.tensor_scalar(dst, dst, quarter * 2 * math.pi, PI_LO, ALU.add, ALU.min))
            else:
                link(v.tensor_scalar(dst, dst, PI_LO, None, ALU.min))
            return v.tensor_scalar(dst, dst, -PI_LO, None, ALU.max)

        def first_loads(s, index):
            for q in range(NRAW):
                kind, i = STREAM[q // 2]
                wd = WIDTH.get(kind, UNIT) // 2
                src = w[kind][index, i, :, q % 2 * wd:(q % 2 + 1) * wd]
                s.dma_start(ring[:, q, 0:wd], src.rearrange("a p n -> p (a n)")).then_inc(next_in, 16)
            s.dma_start(prm[:], par[index].rearrange("a p n -> p (a n)")).then_inc(next_in, 16)

        def first_high(a):
            a.wait_ge(next_in, 16 * (NRAW + 1))
            for p in range(NPART):
                a.activation(w_hi[:, p, 0:PIECES[p][1]], ring[:, p, 0:PIECES[p][1]], ACT.Copy).then_inc(hi_done, 1)

        def low_part(g, p):
            q, wd = PIECES[p]
            g.tensor_tensor(w_lo[:, p % NPART, 0:wd], ring[:, q % NRAW, 0:wd],
                            w_hi[:, p % NPART, 0:wd].bitcast(F32), ALU.subtract).then_inc(lo_done, 1)

        with nc.Block() as block:
            @block.sync
            def _(s):
                s.dma_start(posi[:], pos).then_inc(c_in, 16)
                s.dma_start(xT[:, 0:KT // 2], x_t[:, 0:KT // 2]).then_inc(x_in, 16)
                s.dma_start(xT[:, KT // 2:], x_t[:, KT // 2:]).then_inc(mem_in, 16)
                first_loads(s, slice(0, 1))
                s.dma_start(out, x).then_inc(xout, 16)
                s.wait_ge(xout, 16)

            @block.gpsimd
            def _(g):
                link = after(g, g_step)
                link(g.memset(ident[:], 0.0))
                link(g.affine_select(out=ident[:], in_=ident[:], compare_op=ALU.not_equal, fill=1.0, base=0,
                                     pattern=[[-1, P]], channel_multiplier=1))
                link(g.memset(ones[:], 1.0))
                link(g.affine_select(out=tri[:], in_=ones[:], compare_op=ALU.is_ge, fill=0.0, base=0,
                                     pattern=[[1, P]], channel_multiplier=-1))
                link(g.memset(maskT[:], 0.0))
                link(g.affine_select(out=maskT[:], in_=maskT[:], compare_op=ALU.is_ge, fill=MASKED, base=0,
                                     pattern=[[1, P]], channel_multiplier=-1))
                link(g.memset(seen[:], 0.0))
                link(g.affine_select(out=seen[:, P:SEQ], in_=seen[:, P:SEQ], compare_op=ALU.is_ge, fill=MASKED,
                                     base=0, pattern=[[-1, P]], channel_multiplier=1))
                link(g.memset(expo[:], -0.5))
                g.wait_ge(hi_done, NPART)
                for p in range(EARLY):
                    low_part(g, p)
                g.wait_ge(lo_done, EARLY)

            @block.vector
            def _(v):
                link = after(v, v_step)
                inv = angw[:, 3, 0:ROPE // 2]
                for i in range(ROPE // 2):
                    last = v.memset(angw[:, 3, i:i + 1], float(np.float32(THETA) ** np.float32(-i * 2.0 / ROPE)))
                link(last)
                v.wait_ge(c_in, 16)
                link(v.tensor_copy(mv[:, :, 0], posi[:]))
                ang = angw[:, 0, :].rearrange("p (m f) -> p m f", m=MT)
                link(v.tensor_tensor(ang, mv[:, :, 0:1].to_broadcast([P, MT, ROPE // 2]),
                                     inv.unsqueeze(1).to_broadcast([P, MT, ROPE // 2]), ALU.mult))
                link(wrap_angle(v, link, angw[:, 0, :], cs[:, 0].rearrange("p m f -> p (m f)"), angw[:, 1, :], 0.25))
                wrap_angle(v, link, angw[:, 0, :], cs[:, 1].rearrange("p m f -> p (m f)"), angw[:, 1, :],
                           0.0).then_inc(c_arg, 1)
                for half in range(2):
                    v.wait_ge(xhi_out, half + 1)
                    ks = slice(half * KT // 2, (half + 1) * KT // 2)
                    v.tensor_tensor(x_lo[:, ks], xT[:, ks], x_hi[:, ks].bitcast(F32), ALU.subtract).then_inc(xt_out, 1)
                v.wait_ge(xt_out, 2)

            @block.scalar
            def _(a):
                for half in range(2):
                    a.wait_ge((x_in, mem_in)[half], 16)
                    ks = slice(half * KT // 2, (half + 1) * KT // 2)
                    a.activation(x_hi[:, ks], xT[:, ks], ACT.Copy).then_inc(xhi_out, 1)
                first_high(a)
                a.wait_ge(c_arg, 1)
                a.activation(cs[:], cs[:], ACT.Sin).then_inc(c_out, 1)
                a.wait_ge(c_out, 1)

        first, last_sem = min(s.num for s in sems), max(s.num for s in sems)
        clear = range(first, last_sem + 1)
        nc.multi_engine_barrier(mybir.ALL_ENGINES, sems_to_clear=clear)

        JOBS = ([('u5', i, 1) for i in range(4)] + [('small', 0, 2)] + [('kmem', i, 1) for i in range(2)]
                + [('vmem', 0, 2)] + [('xbc', i, 1) for i in range(XT)]
                + [('tok', 0, 2), ('tok', 1, 2)] + [('z5', i, 1) for i in range(4)]
                + [('zssd', 0, 2), ('zssd', 1, 2)] + [('zatt', i, 1) for i in range(4)]
                + [('qmem', i, 1) for i in range(2)] + [('zmem', i, 1) for i in range(2)])
        START = {}
        nbank = 0
        for name, i, b in JOBS:
            START[name, i] = nbank
            nbank += b
        NPROJ = nbank
        LAST = {('tok', 0): ('tok', 3), ('tok', 1): ('tok', 7), ('zssd', 0): ('zssd', 3), ('zssd', 1): ('zssd', 7),
                ('vmem', 0): ('vmem', 1)}

        def finished(eng, kind, i=0):
            if (kind, i) in SPLIT:
                eng.wait_ge(pieces_done, 2 * (SPLIT[kind, i] + 1))
            else:
                eng.wait_ge(whole_done, 2 * (WHOLE[kind, i] + 1))

        BATCH = ([(True, 0, [(2 * j, 0), (2 * j + 1, 0), (2 * j, 1), (2 * j + 1, 1)]) for j in range(2)]
                 + [(True, 1, [(j, 0), (j, 1)]) for j in range(4)]
                 + [(False, qb, [(j, 0), (j, 1)]) for qb in range(MT) for j in range(2)])
        NSPARSE = sum(sparse for sparse, _, _ in BATCH)
        KOF = [(0, 4), (4, 8), (8, 16), (16, 18)]

        def keys_of(b):
            sparse, qb, _ = BATCH[b]
            return P if sparse and qb == 0 else SEQ

        def steps(c):
            return slice(CONV - 1 + c * P, CONV - 1 + (c + 1) * P)

        dt, da, acs, eacs, dec = (dts[:, i] for i in range(5))
        xdd = mg[:, :, :].rearrange("p a n -> p (a n)")

        with nc.Fori(0, DEPTH) as layer:
            with nc.Block() as block:
                @block.sync
                def _(s):
                    for n, (kind, i) in enumerate(STREAM):
                        wd = WIDTH.get(kind, UNIT) // 2
                        for half in range(2):
                            q = 2 * n + half
                            if q < NRAW:
                                continue
                            last, lh = STREAM[(q - NRAW) // 2], (q - NRAW) % 2
                            if last in WHOLE or q >= NRAW + EARLY:
                                if last in SPLIT:
                                    s.wait_ge(lo_done, 2 * SPLIT[last] + lh + 1 - EARLY)
                                else:
                                    s.wait_ge(whole_done, 2 * WHOLE[last] + lh + 1)
                            src = w[kind][bass.ds(layer, 1), i, :, half * wd:(half + 1) * wd]
                            s.dma_start(ring[:, q % NRAW, 0:wd], src.rearrange("a p n -> p (a n)")
                                        ).then_inc(slot_full[q % NRAW], 16)
                        if n == 1:
                            s.dma_start(memT[:], mem_t).then_inc(mem_in, 16)
                        if n == AT['branch', 0]:
                            s.wait_ge(o_ps, len(BATCH))
                            s.dma_start(lng, ln_g[bass.ds(layer, 1)].to_broadcast([P, D])).then_inc(lng_in, 16)
                            s.dma_start(lnb, ln_b[bass.ds(layer, 1)].to_broadcast([P, D])).then_inc(lnb_in, 16)
                        if n == AT['out', 2]:
                            finished(s, 'branch', KT - 1)
                            s.dma_start(xtok[:], out.rearrange("(m p) n -> p m n", p=P)).then_inc(x_in, 16)
                    s.wait_ge(lo_done, NPIECE - EARLY)
                    first_loads(s, bass.ds((layer + 1) % DEPTH, 1))
                    for m in range(MT):
                        s.wait_ge(ln_done, 4 * (m + 1))
                        s.dma_start(out[m * P:(m + 1) * P, :], xtok[:, m, :]).then_inc(xout, 16)
                    s.wait_ge(xout, 16 * MT)
                    s.wait_ge(next_in, 16 * (NRAW + 1))

                @block.gpsimd
                def _(g):
                    def low(first, last):
                        for p in range(first, last):
                            if p >= NPART:
                                g.wait_ge(hi_done, p + 1 - NPART)
                            low_part(g, p)

                    start = 2 * (SPLIT['small', 0] + 1)
                    low(EARLY, 2)
                    g.memset(BD, 0.0).then_inc(zeroed, 1)
                    for p in range(4):
                        low(2 + p, 3 + p)
                        ins = g.memset(gflat[:, p * GDW // 4:(p + 1) * GDW // 4], 0.0)
                    ins.then_inc(zeroed, 1)
                    low(6, start)
                    g.wait_ge(w5_ps, 8)
                    g.memset(T5, 0.0)
                    low(start, start + 2)
                    finished(g, 'vmem', 1)
                    g.memset(ST[:, 0], 0.0).then_inc(zeroed, 1)
                    middle = 2 * (SPLIT['gate', 1] + 1)
                    low(start + 2, middle)
                    g.wait_ge(rms_arg, 1)
                    g.tensor_tensor(rms[:, 1], rms[:, 0], expo[:].unsqueeze(2).to_broadcast([P, MT, SSDG]),
                                    ALU.pow).then_inc(rms_pow, 1)
                    low(middle, NPIECE)
                    for m in range(MT):
                        g.wait_ge(var_done, m + 1)
                        g.tensor_tensor(mv[:, m, 2:3], mv[:, m, 2:3], expo[:, 0:1], ALU.pow).then_inc(rstd_done, 1)
                    g.wait_ge(lnb_in, 16)
                    for n in range(8):
                        m, cols = n // 4, slice(n % 4 * BANK, (n % 4 + 1) * BANK)
                        g.wait_ge(gain_done, n + 1)
                        g.tensor_tensor(xtok[:, m, cols], xtok[:, m, cols], lnb[:, cols], ALU.add).then_inc(ln_done, 1)
                    g.wait_ge(hi_done, NPIECE)
                    for p in range(EARLY):
                        low_part(g, p)
                    g.wait_ge(lo_done, NPIECE)

                @block.tensor
                def _(t):
                    def whole(kind, i, half):
                        q = 2 * AT[kind, i] + half
                        t.wait_ge(slot_full[q % NRAW], 16 * (q // NRAW))
                        return ring[:, q % NRAW, :]

                    def piece(kind, i, half):
                        p = 2 * SPLIT[kind, i] + half
                        if p >= EARLY:
                            t.wait_ge(lo_done, p + 1 - EARLY)
                        return w_hi[:, p % NPART, :], w_lo[:, p % NPART, :]

                    def three(o, a_hi, a_lo, b_hi, b_lo, start, stop):
                        t.matmul(o, a_hi, b_hi, start=start, stop=False)
                        t.matmul(o, a_hi, b_lo, start=False, stop=False)
                        return t.matmul(o, a_lo, b_hi, start=False, stop=stop)

                    def bank_free(n):
                        if n >= 4:
                            t.wait_ge(taken, n - 3)

                    def x_product(o, kind, i):
                        for half in range(2):
                            wh, wl = piece(kind, i, half)
                            for j in range(KT // 2):
                                k, js = half * KT // 2 + j, slice(j * P, (j + 1) * P)
                                mm = three(o, wh[:, js], wl[:, js], x_hi[:, k, :], x_lo[:, k, :], k == 0, k == KT - 1)
                            mm.then_inc(pieces_done, 1)

                    def proj_t(kind, i):
                        b = START[kind, i]
                        bank_free(b)
                        x_product(gp[b % 4][:, 0:SEQ], kind, i)

                    def proj_m(kind, i, n, cols, then=lambda j: None):
                        b = START[kind, i]
                        per = KT // n // 2
                        bank_free(b + 1)
                        for j in range(n):
                            for half in range(2):
                                wh, wl = piece(kind, i * n + j, half)
                                for m in range(MT):
                                    ms = slice(m * P, (m + 1) * P)
                                    for k in range(per):
                                        kk, ks = (2 * j + half) * per + k, slice(k * cols, (k + 1) * cols)
                                        mm = three(gp[(b + m) % 4][:, 0:cols], x_hi[:, kk, ms], x_lo[:, kk, ms],
                                                   wh[:, ks], wl[:, ks], kk == 0, kk == KT - 1)
                                mm.then_inc(pieces_done, 1)
                            then(j)

                    def mem_keys(i):
                        b = START['kmem', i]
                        bank_free(b)
                        for half in range(2):
                            wt = whole('kmem', i, half)
                            for j in range(KT // 2):
                                k = half * KT // 2 + j
                                mm = t.matmul(gp[b % 4][:, 0:SEQ], wt[:, j * P:(j + 1) * P], memT[:, k, :],
                                              start=k == 0, stop=k == KT - 1)
                            mm.then_inc(whole_done, 1)

                    def mem_values():
                        b, cols = START['vmem', 0], MEMH * HD
                        bank_free(b + 1)
                        for q in range(4):
                            wt = whole('vmem', q // 2, q % 2)
                            for m in range(MT):
                                for k in range(KT // 4):
                                    kk = q * KT // 4 + k
                                    mm = t.matmul(gp[(b + m) % 4][:, 0:cols], memT[:, kk, m * P:(m + 1) * P],
                                                  wt[:, k * cols:(k + 1) * cols], start=kk == 0, stop=kk == KT - 1)
                            mm.then_inc(whole_done, 1)

                    def four(out_bank, tiles, done):
                        for j, tile in enumerate(tiles):
                            mm = t.transpose(out_bank[:, j * P:(j + 1) * P], tile, ident[:])
                        mm.then_inc(done, 1)

                    for i in range(4):
                        proj_t('u5', i)
                    proj_m('small', 0, 1, SMALL)

                    def w5_turn(r):
                        for q in range(4):
                            if r:
                                t.wait_ge(w5_out, q + 1)
                            four(sp[q], [V5[:, r, gi * P:(gi + 1) * P] for gi in range(4 * q, 4 * q + 4)], w5_ps)

                    t.wait_ge(mem_in, 16)
                    mem_keys(0)
                    t.wait_ge(v5_ready, 1)
                    w5_turn(0)
                    mem_keys(1)
                    w5_turn(1)
                    mem_values()
                    t.wait_ge(g5_ready, 1)
                    for q in range(4):
                        t.wait_ge(w5_out, 5 + q)
                        for j in range(4):
                            gi = 4 * q + j
                            for r in range(2):
                                mm = t.matmul(sp[q][0:32, j * P:(j + 1) * P], BD[:, r, gi, :],
                                              GD[:, r, gi, 0:Q5, :].rearrange("p j h -> p (j h)"),
                                              start=r == 0, stop=r == 1)
                        mm.then_inc(k5_ps, 1)
                    for i in range(6):
                        proj_t('xbc', i)
                    t.wait_ge(taken, 4)
                    t.wait_ge(k5_out, 4)
                    for q in range(4):
                        r, half = q % 2, q // 2
                        for j in range(8):
                            gi = 8 * half + j
                            mm = t.matmul(sp[q][:, j * C5:(j + 1) * C5], W5[:, r, gi, :], U[:, gi, :],
                                          start=True, stop=True)
                        mm.then_inc(in5_ps, 1)
                    for i in range(6, XT):
                        proj_t('xbc', i)
                    for i in range(2):
                        proj_m('tok', i, 4, BANK)
                    t.wait_ge(da_done, 1)
                    t.wait_ge(in5_out, 4)
                    t.matmul(sp[0][:, 0:MT * SSDH], tri[:], da.rearrange("p m h -> p (m h)"), start=True, stop=True)
                    t.matmul(sp[0][:, 64:64 + SSDH], ones[:], da[:, 0, :], start=True, stop=True).then_inc(acs_ps, 1)
                    t.wait_ge(xbc_done, XT)
                    for c in range(MT):
                        for g in range(SSDG):
                            n = c * SSDG + g
                            mm = t.matmul(sp[1][:, n * P:(n + 1) * P], xb[:, 8 + g, steps(c)],
                                          xb[:, 10 + g, steps(c)], start=True, stop=True)
                    mm.then_inc(cb_ps, 1)

                    def xs_turn(n):
                        if n >= 2:
                            t.wait_ge(xs_out, n - 1)
                        four(sp[2 + n % 2], [xb[:, 4 * (n % 2) + j, steps(n // 2)] for j in range(4)] if n < 4 else
                             [xb[:, 8 + g, steps(0)] for g in range(SSDG)], xs_ps)

                    xs_turn(0)
                    xs_turn(1)
                    proj_t('z5', 0)
                    xs_turn(2)
                    xs_turn(3)
                    proj_t('z5', 1)
                    xs_turn(4)
                    proj_t('z5', 2)
                    t.wait_ge(scan_done, 1)
                    t.wait_ge(t5_out, 1)
                    t.wait_ge(xs_out, 5)
                    for half in range(2):
                        for j in range(8):
                            gi = 8 * half + j
                            o = sp[2 + half][:, j * C5:(j + 1) * C5]
                            t.matmul(o, T5[:, gi, :], U[:, gi, :], start=True, stop=False)
                            for r in range(2):
                                mm = t.matmul(o, GD[:, r, gi, 1:Q5 + 1, :].rearrange("p j h -> p (j h)"),
                                              ST[:, 0:C5, r, gi], start=False, stop=r == 1)
                        mm.then_inc(y5_ps, 1)
                    proj_t('z5', 3)
                    t.wait_ge(rope_done, 1)
                    t.wait_ge(cb_out, 1)
                    t.wait_ge(acs_arg, 1)

                    def qk_turn(n):
                        m, h = n // 2, n % 2
                        if n >= 2:
                            t.wait_ge(qk_out, n - 1)
                        four(sp[n % 2], [tok[:, m, f * P:(f + 1) * P] if f < 7 else
                                         ik2[:, m].rearrange("p a e -> p (a e)")
                                         for f in range(4 * h, 4 * h + 4)], qk_ps)

                    qk_turn(0)
                    qk_turn(1)

                    def glu():
                        t.wait_ge(gelu_done, 1)
                        t.wait_ge(y5_out, 2)
                        halves = [whole('glu', 0, half) for half in range(2)]
                        for j in range(4):
                            for k in range(4):
                                mm = t.matmul(sp[2 + j // 2][:, (j % 2) * SEQ:(j % 2 + 1) * SEQ],
                                              halves[k // 2][:, (k % 2) * BANK + j * P:(k % 2) * BANK + (j + 1) * P],
                                              y5[:, k, :], start=k == 0, stop=k == 3)
                        mm.then_inc(whole_done, 2)

                    def index(qb):
                        nk = (qb + 1) * P
                        if qb:
                            t.wait_ge(ix_out, 1)
                        else:
                            t.wait_ge(qk_out, 4)
                        for h in range(IH):
                            r = slice(HD * (h % 2), HD * (h % 2 + 1))
                            mm = t.matmul(sp[h % 2][:, (h // 2) * SEQ:(h // 2) * SEQ + nk],
                                          qkT[r, 5 + h // 2, qb * P:(qb + 1) * P], qkT[r, 7, 0:nk],
                                          start=True, stop=True)
                        mm.then_inc(ix_ps, 1)

                    def diag(n):
                        c, rd = n // 4, n % 4
                        t.wait_ge(m_done, n + 1)
                        if n == 4:
                            t.wait_ge(yd_out, 2)
                        for j in range(4):
                            h = 4 * rd + j
                            mm = t.matmul(sp[2 + h // 8][:, (h % 8) * HD:(h % 8 + 1) * HD],
                                          seg[:, n % 2, j * P:(j + 1) * P], xdt[:, c, h * HD:(h + 1) * HD],
                                          start=True, stop=True)
                        mm.then_inc(yd_ps, 1)

                    def ssd_round(n):
                        if n:
                            t.wait_ge(seg_done, n)
                        else:
                            t.wait_ge(ix_out, 2)
                            t.wait_ge(st_out, 2)
                        for j in range(4):
                            h = 4 * (n % 4) + j
                            mm = t.matmul(sp[0][:, j * P:(j + 1) * P], da[:, n // 4, h:h + 1].to_broadcast([P, P]),
                                          tri[:], start=True, stop=True)
                        mm.then_inc(ab_ps, 1)
                        if n:
                            diag(n - 1)

                    def carried(g):
                        if g:
                            t.wait_ge(yo_out, 1)
                        t.matmul(sp[1][:], xb[:, 10 + g, steps(1)], prev[:, g * BANK:(g + 1) * BANK],
                                 start=True, stop=True).then_inc(yo_ps, 1)

                    def state():
                        t.wait_ge(xdt_done, 1)
                        t.wait_ge(xs_out, 5)
                        t.wait_ge(glu_t, 4)
                        for g in range(SSDG):
                            t.matmul(sp[2 + g][:], Bt[:, g, :], xdd[:, g * BANK:(g + 1) * BANK], start=True,
                                     stop=True).then_inc(st_ps, 1)

                    def meanwhile(j):
                        if j == 0:
                            qk_turn(2)
                            qk_turn(3)
                            glu()
                            index(0)
                        elif j == 1:
                            index(1)
                            state()
                        elif j == 3:
                            ssd_round(0)

                    proj_m('zssd', 0, 4, BANK, then=meanwhile)
                    proj_m('zssd', 1, 4, BANK, then=lambda j: ssd_round(j + 1))
                    for i in range(3):
                        proj_t('zatt', i)
                        ssd_round(5 + i)
                    proj_t('zatt', 3)
                    carried(0)
                    diag(7)
                    proj_t('qmem', 0)
                    carried(1)
                    proj_t('qmem', 1)

                    def logits(b):
                        sparse, qb, heads = BATCH[b]
                        nk = keys_of(b)
                        if b:
                            t.wait_ge(lg_out, b)
                        for n, (f, half) in enumerate(heads):
                            r = slice(HD * half, HD * (half + 1))
                            q = (qkT if sparse else qmT)[r, f, qb * P:(qb + 1) * P]
                            k = qkT[r, 4, 0:nk] if sparse else kmT[r, f, 0:nk]
                            c = (n % (len(heads) // 2)) * nk
                            mm = t.matmul(sp[half][:, c:c + nk], q, k, start=True, stop=True)
                        mm.then_inc(lg_ps, 1)

                    def weighted(b):
                        sparse, qb, heads = BATCH[b]
                        t.wait_ge(pt_out, b + 1)
                        if b:
                            t.wait_ge(o_out, b)
                        tiles = keys_of(b) // P
                        for n, (f, half) in enumerate(heads):
                            for s in range(tiles):
                                v = (tok[:, s, C_V + half * HD:C_V + (half + 1) * HD] if sparse else
                                     vm[:, s, (2 * f + half) * HD:(2 * f + half + 1) * HD])
                                blk = n * tiles + s
                                o = n % (len(heads) // 2)
                                mm = t.matmul(sp[3][HD * half:HD * (half + 1), o * P:(o + 1) * P], v,
                                              pT[:, b % 2, blk * P:(blk + 1) * P], start=s == 0, stop=s == tiles - 1)
                        mm.then_inc(o_ps, 1)

                    def attend(b):
                        if b < len(BATCH):
                            t.wait_ge(p_done, b + 1)
                            if b:
                                t.wait_ge(pt_out, b)
                            four(sp[2], [LG[:, b % 2, j * P:(j + 1) * P] for j in range(4)], pt_ps)
                        if b:
                            weighted(b - 1)
                        if b + 1 < len(BATCH):
                            if b == NSPARSE - 1:
                                t.wait_ge(taken, START['qmem', 1] + 1)
                            logits(b + 1)

                    def ys_turn(m):
                        t.wait_ge(ys_done, m + 1)
                        for q in range(2):
                            if m:
                                t.wait_ge(ys_out, q + 1)
                            four(sp[2 + q], [xs[:, m, (4 * q + j) * P:(4 * q + j + 1) * P] for j in range(4)], ys_ps)

                    t.wait_ge(yo_out, 2)
                    logits(0)
                    proj_t('zmem', 0)
                    t.wait_ge(yd_out, 4)
                    attend(0)
                    proj_t('zmem', 1)
                    attend(1)

                    def branch(d):
                        pair = 2 * (d % 2)
                        if d >= 2:
                            t.wait_ge(mg_done, d - 1)
                        elif d == 0:
                            t.wait_ge(ylo_done, 1)
                        for half in range(2):
                            wh, wl = piece('branch', d, half)
                            for j in range(KB // 2):
                                k, js = half * KB // 2 + j, slice(j * P, (j + 1) * P)
                                b, (lo, hi) = next((b, r) for b, r in enumerate(KOF) if r[0] <= k < r[1])
                                mm = three(sp[pair + b // 2][:, (b % 2) * SEQ:(b % 2 + 1) * SEQ],
                                           wh[:, js], wl[:, js], y_hi[:, k, :], y_lo[:, k, :], k == lo, k == hi - 1)
                            mm.then_inc(pieces_done, 1)

                    for d in range(KT):
                        pair = 2 * ((d + 1) % 2)
                        for b in range(NB):
                            if d < 2 and b == 0:
                                t.wait_ge(taken, NPROJ - 2 + 2 * d)
                            if b == 0 and d >= 2:
                                t.wait_ge(gate_t, NB * (d - 1))
                            x_product(gp[pair + b // 2][:, (b % 2) * SEQ:(b % 2 + 1) * SEQ], 'gate', NB * d + b)
                            n = 2 + NB * d + b
                            if n <= len(BATCH):
                                attend(n)
                            elif n <= len(BATCH) + MT:
                                if n == len(BATCH) + 1:
                                    t.wait_ge(o_out, len(BATCH))
                                ys_turn(n - len(BATCH) - 1)
                        if d == 2:
                            branch(0)
                        if d >= 2:
                            branch(d - 1)
                    branch(KT - 1)
                    for c in range(4):
                        for j in range(4):
                            if c == 0:
                                t.wait_ge(mg_done, 4 * j + 4)
                                if j == 0:
                                    t.wait_ge(gate_t, NB * (KT - 1))
                            if j == 0 and c == 1:
                                t.wait_ge(gate_t, NB * KT)
                            if j == 0 and c >= 2:
                                t.wait_ge(res_done, MT * (c - 1))
                            for hf in range(2):
                                wh, wl = piece('out', 4 * c + j, hf)
                                for m in range(MT):
                                    o = gp[2 * ((c + 1) % 2) + m][:]
                                    for k in range(2):
                                        kk = 4 * j + 2 * hf + k
                                        ks, ms = slice(k * BANK, (k + 1) * BANK), slice(m * P, (m + 1) * P)
                                        mm = three(o, m_hi[:, kk, ms], m_lo[:, kk, ms], wh[:, ks], wl[:, ks],
                                                   kk == 0, kk == KT - 1)
                                mm.then_inc(pieces_done, 1)
                    for n in range(8):
                        m, q = n // 4, n % 4
                        t.wait_ge(ln_done, n + 1)
                        if n >= 4:
                            t.wait_ge(xt_out, n - 3)
                        four(sp[q], [xtok[:, m, f * P:(f + 1) * P] for f in range(4 * q, 4 * q + 4)], xt_ps)

                @block.scalar
                def _(a):
                    def copy(o, i, **k):
                        return a.activation(o, i, ACT.Copy, **k)

                    split_to = [NPART]

                    def split(upto):
                        for p in range(split_to[0], min(upto, NPIECE)):
                            q, wd = PIECES[p]
                            if q >= NRAW:
                                a.wait_ge(slot_full[q % NRAW], 16 * (q // NRAW))
                            a.wait_ge(pieces_done, p - NPART + 1)
                            copy(w_hi[:, p % NPART, 0:wd], ring[:, q % NRAW, 0:wd]).then_inc(hi_done, 1)
                        split_to[0] = max(split_to[0], upto)

                    def ahead(kind, i=0):
                        end = 2 * (SPLIT[kind, i] + 1)
                        full = min([2 * AT[u] for u in WHOLE if AT[u] > AT[kind, i]], default=2 * len(STREAM)) + NRAW
                        split(end + sum(q < full for q, _ in PIECES[end:end + NPART]))

                    def done(kind, i=0):
                        last = LAST.get((kind, i), (kind, i))
                        if last in SPLIT:
                            ahead(*last)
                        finished(a, *last)
                        return START[kind, i]

                    a.activation(s5s[:, 0], pv('ldt'), ACT.Exp).then_inc(disc_act, 1)
                    a.wait_ge(disc_arg, 1)
                    a.activation(s5s[:, 1], s5s[:, 1], ACT.Exp)
                    a.activation(dts[:, 5, 0], pv('alog'), ACT.Exp).then_inc(a_step, 1)
                    a.activation(s5s[:, 3:5], s5s[:, 3:5], ACT.Sin).then_inc(disc_act, 1)
                    for i in range(4):
                        b = done('u5', i)
                        for pr in range(4):
                            src = gp[b % 4][32 * pr:32 * pr + 32, 0:SEQ].rearrange("p (c q) -> p q c", q=Q5)
                            for q in range(Q5):
                                ins = copy(U[32 * q:32 * q + 32, 4 * i + pr, :], src[:, q, :])
                        ins.then_inc(taken, 1)
                    def w5_evac(r):
                        for q in range(4):
                            a.wait_ge(w5_ps, 4 * r + q + 1)
                            copy(W5[:, r, 4 * q:4 * q + 4, :],
                                 sp[q][:].rearrange("p (g n) -> p g n", g=4)).then_inc(w5_out, 1)

                    b = done('small')
                    for m in range(MT):
                        copy(tok[:, m, 2 * BANK:TOKW], gp[(b + m) % 4][:, 0:SMALL]).then_inc(taken, 1)
                    def xbc_evac(i):
                        b = done('xbc', i)
                        copy(xb[:, i, CONV - 1:], gp[b % 4][:, 0:SEQ]).then_inc(taken, 1)

                    w5_evac(0)
                    a.wait_ge(g5_ready, 1)
                    for i in range(2):
                        b = done('kmem', i)
                        copy(kmT[:, i, :], gp[b % 4][:, 0:SEQ]).then_inc(taken, 1)
                    w5_evac(1)
                    a.wait_ge(dt_arg, 1)
                    a.activation(dts[:, 6], dts[:, 6], ACT.Exp).then_inc(dt_exp, 1)
                    xbc_start = 2 * SPLIT['xbc', 0]
                    split(xbc_start + 2)
                    b = done('vmem')
                    split(xbc_start + NPART)
                    for m in range(MT):
                        copy(vm[:, m, :], gp[(b + m) % 4][:, 0:MEMH * HD]).then_inc(taken, 1)
                    for q in range(4):
                        a.wait_ge(k5_ps, q + 1)
                        copy(K5[:, q * BANK:(q + 1) * BANK], sp[q][0:32, :]).then_inc(k5_out, 1)
                    a.wait_ge(dt_u, 1)
                    a.activation(dts[:, 8], dts[:, 7], ACT.Ln).then_inc(dt_ln, 1)
                    a.wait_ge(zeroed, 3)
                    a.wait_ge(k5_diag, 1)
                    k5v = K5.rearrange("p (g n) -> p g n", g=PAIRS)
                    for s in range(Q5):
                        ins = copy(T5[32 * s:32 * s + 32, :, 32 * s:P], k5v[:, :, 0:P - 32 * s])
                    ins.then_inc(t5_out, 1)

                    def xbc_tanh(i):
                        a.wait_ge(conv_done, i + 1)
                        if i >= 2:
                            a.wait_ge(xbc_done, i - 1)
                        a.activation(th[:, i % 2], cv[:, i % 2], ACT.Tanh).then_inc(conv_t, 1)

                    for i in range(6):
                        xbc_evac(i)
                        if i:
                            xbc_tanh(i - 1)
                    a.wait_ge(t5_out, 1)
                    for q in range(4):
                        r, half = q % 2, q // 2
                        a.wait_ge(in5_ps, q + 1)
                        copy(ST[:, 1:C5 + 1, r, 8 * half:8 * half + 8],
                             sp[q][:].rearrange("p (g c) -> p c g", g=8)).then_inc(in5_out, 1)
                    for i in range(6, XT):
                        xbc_evac(i)
                        xbc_tanh(i - 1)
                    ahead('tok', 0)
                    xbc_tanh(XT - 1)
                    for i in range(2):
                        b = done('tok', i)
                        for m in range(MT):
                            copy(tok[:, m, i * BANK:(i + 1) * BANK], gp[(b + m) % 4][:]).then_inc(taken, 1)
                    a.wait_ge(acs_out, 1)
                    a.activation(eacs, acs, ACT.Exp)
                    a.wait_ge(acs_arg, 1)
                    a.activation(dec[:, 0], dec[:, 0], ACT.Exp).then_inc(acs_exp, 1)
                    def z_evac(bank, cols, dst, th_dst):
                        copy(dst, bank[:, 0:cols])
                        a.activation(th_dst, bank[:, 0:cols], ACT.Tanh, scale=0.5).then_inc(taken, 1)

                    for n in range(5):
                        a.wait_ge(xs_ps, n + 1)
                        bank = sp[2 + n % 2]
                        (copy(xs[:, n // 2, (n % 2) * BANK:(n % 2 + 1) * BANK], bank[:]) if n < 4 else
                         copy(Bt[:].rearrange("p g n -> p (g n)"), bank[:, 0:SSDG * P])).then_inc(xs_out, 1)
                        if n % 2:
                            b = done('z5', n // 2)
                            z_evac(gp[b % 4], SEQ, z5[:, n // 2, :], tg[:, 0, n // 2, :])
                    for i in range(2, 4):
                        b = done('z5', i)
                        z_evac(gp[b % 4], SEQ, z5[:, i, :], tg[:, 0, i, :])

                    def qk_evac(n):
                        a.wait_ge(qk_ps, n + 1)
                        m, h = n // 2, n % 2
                        copy(qkT[:, 4 * h:4 * h + 4, m * P:(m + 1) * P],
                             sp[n % 2][:].rearrange("p (f t) -> p f t", f=4)).then_inc(qk_out, 1)

                    qk_evac(0)
                    qk_evac(1)
                    a.wait_ge(gelu_arg, 1)
                    a.activation(LG.rearrange("p a n -> p (a n)"), LG.rearrange("p a n -> p (a n)"), ACT.Tanh,
                                 scale=GELU_C).then_inc(gelu_t, 1)
                    qk_evac(2)
                    qk_evac(3)
                    ahead('zssd', 0)
                    finished(a, 'glu')
                    a.wait_ge(half_done, 1)
                    for j in range(4):
                        a.activation(pT[:, j // 2, (j % 2) * SEQ:(j % 2 + 1) * SEQ],
                                     sp[2 + j // 2][:, (j % 2) * SEQ:(j % 2 + 1) * SEQ], ACT.Tanh, scale=0.5,
                                     bias=bgh[:, KT * NB + j:KT * NB + j + 1]).then_inc(glu_t, 1)
                    ahead('zssd', 1)
                    for g in range(SSDG):
                        a.wait_ge(st_ps, g + 1)
                        copy(prev[:, g * BANK:(g + 1) * BANK], sp[2 + g][:]).then_inc(st_out, 1)
                    ahead('zssd', 2)
                    a.wait_ge(z_done, 1)
                    tgf = tg[:].rearrange("p a b n -> p (a b n)").rearrange("p (m n) -> p m n", m=MT)

                    def seg_act(n):
                        a.wait_ge(seg_done, n + 1)
                        a.activation(seg[:, n % 2], seg[:, n % 2], ACT.Exp).then_inc(seg_exp, 1)

                    def zssd_evac(i):
                        b = done('zssd', i)
                        for m in range(MT):
                            z_evac(gp[(b + m) % 4], BANK, zssd[:, m, i * BANK:(i + 1) * BANK],
                                   tgf[:, m, i * BANK:(i + 1) * BANK])

                    def zatt_evac(i):
                        b = done('zatt', i)
                        z_evac(gp[b % 4], SEQ, zatt[:, i, :], tg[:, 0, i, :])

                    zssd_evac(0)
                    for n in range(4):
                        seg_act(n)
                        ahead('zssd', 4 + n)
                    zssd_evac(1)
                    seg_act(4)
                    a.wait_ge(z_done, 2)
                    for i in range(4):
                        zatt_evac(i)
                        if i < 3:
                            seg_act(5 + i)
                    for i in range(2):
                        b = done('qmem', i)
                        copy(qmT[:, i, :], gp[b % 4][:, 0:SEQ]).then_inc(taken, 1)

                    def softmax(b):
                        nh, nk = len(BATCH[b][2]), keys_of(b)
                        a.wait_ge(lg_out, b + 1)
                        for n in range(nh):
                            v = LG[:, b % 2, n * nk:(n + 1) * nk]
                            ins = a.activation(v, v, ACT.Exp, bias=smx[:, 0, b % 2, n:n + 1],
                                               accum_out=smx[:, 1, b % 2, n:n + 1])
                        ins.then_inc(lg_exp, 1)

                    def turned(b):
                        a.wait_ge(pt_ps, b + 1)
                        if b >= 2:
                            a.wait_ge(o_ps, b - 1)
                        copy(pT[:, b % 2], sp[2][:]).then_inc(pt_out, 1)

                    def gate_tanh(d, b):
                        ahead('gate', NB * d + b + 1)
                        finished(a, 'gate', NB * d + b + 1)
                        for b in (b, b + 1):
                            a.activation(tg[:, d % 2, b, :], gp[2 * ((d + 1) % 2) + b // 2][:, (b % 2) * SEQ:(b % 2 + 1) * SEQ],
                                         ACT.Tanh, scale=0.5,
                                         bias=bgh[:, NB * d + b:NB * d + b + 1]).then_inc(gate_t, 1)

                    ng = pv('ng')

                    def ys_evac(m):
                        for q in range(2):
                            a.wait_ge(ys_ps, 2 * m + q + 1)
                            for j in range(4):
                                f = 4 * q + j
                                ins = copy(yT[:, 8 + f, m * P:(m + 1) * P], sp[2 + q][:, j * P:(j + 1) * P],
                                           scale=ng[:, f:f + 1])
                            ins.then_inc(ys_out, 1)

                    for n in range(len(BATCH)):
                        softmax(n)
                        if n < 2:
                            b = done('zmem', n)
                            z_evac(gp[b % 4], SEQ, zmem[:, n, :], tg[:, 1, n, :])
                        else:
                            ahead('gate', n - 2)
                            if n in (3, 7):
                                a.wait_ge(z_done, 3 + n // 7)
                            if n % 2:
                                gate_tanh((n - 2) // NB, (n - 3) % NB)
                        turned(n)
                    ahead('gate', 2 * NB)
                    a.wait_ge(o_out, len(BATCH))
                    for lo, hi in (KOF[0], KOF[1], KOF[3]):
                        ins = copy(y_hi[:, lo:hi], yT[:, lo:hi])
                    ins.then_inc(yhi_done, 1)
                    for m in range(MT):
                        ahead('gate', 2 * NB + 1 + m)
                        ys_evac(m)
                    a.wait_ge(ys_out, 4)
                    lo, hi = KOF[2]
                    copy(y_hi[:, lo:hi], yT[:, lo:hi]).then_inc(yhi_done, 1)
                    ahead('gate', 3 * NB - 1)
                    ahead('branch', 0)
                    a.wait_ge(mg_done, 1)
                    gate_tanh(2, 0)
                    gate_tanh(2, 2)
                    ahead('branch', 1)
                    for d in range(3, KT):
                        ahead('gate', NB * d + 1)
                        a.wait_ge(mg_done, d - 1)
                        gate_tanh(d, 0)
                        gate_tanh(d, 2)
                        ahead('branch', d - 1)
                    ahead('out', 3)
                    a.wait_ge(x_in, 16)
                    for m in range(MT):
                        copy(xtok[:, m, :], xtok[:, m, :], scale=ALPHA).then_inc(ax_done, 1)
                        ahead('out', 4 + m)
                    split(NPIECE)
                    a.wait_ge(pieces_done, NPIECE)
                    first_high(a)
                    for n in range(8):
                        m, q = n // 4, n % 4
                        a.wait_ge(xt_ps, n + 1)
                        copy(x_hi[:, 4 * q:4 * q + 4, m * P:(m + 1) * P],
                             sp[q][:].rearrange("p (f t) -> p f t", f=4)).then_inc(xhi_out, 1)

                @block.vector
                def _(v):
                    link, tell = signals(v, v_step)
                    tt, ts, stt = v.tensor_tensor, v.tensor_scalar, v.scalar_tensor_tensor

                    lre, lim = pv('lre'), pv('lim')
                    v.wait_ge(disc_act, 1)
                    link(tt(s5s[:, 1], lre, s5s[:, 0], ALU.mult))
                    link(tt(s5s[:, 2], lim, s5s[:, 0], ALU.mult))
                    link(wrap_angle(v, link, s5s[:, 2], s5s[:, 3], s5s[:, 5], 0.25))
                    tell(wrap_angle(v, link, s5s[:, 2], s5s[:, 4], s5s[:, 5], 0.0), disc_arg)
                    v.wait_ge(disc_act, 2)
                    link(tt(s5s[:, 6], s5s[:, 1], s5s[:, 3], ALU.mult))
                    link(tt(s5s[:, 7], s5s[:, 1], s5s[:, 4], ALU.mult))
                    link(tt(s5s[:, 8], lre, lre, ALU.mult))
                    link(tt(s5s[:, 5], lim, lim, ALU.mult))
                    link(tt(s5s[:, 8], s5s[:, 8], s5s[:, 5], ALU.add))
                    link(v.reciprocal(s5s[:, 8], s5s[:, 8]))
                    link(ts(s5s[:, 9], s5s[:, 6], -1.0, None, ALU.add))
                    link(tt(s5s[:, 10], s5s[:, 9], lre, ALU.mult))
                    link(tt(s5s[:, 5], s5s[:, 7], lim, ALU.mult))
                    link(tt(s5s[:, 10], s5s[:, 10], s5s[:, 5], ALU.add))
                    link(tt(s5s[:, 10], s5s[:, 10], s5s[:, 8], ALU.mult))
                    link(tt(s5s[:, 11], s5s[:, 7], lre, ALU.mult))
                    link(tt(s5s[:, 5], s5s[:, 9], lim, ALU.mult))
                    link(tt(s5s[:, 11], s5s[:, 11], s5s[:, 5], ALU.subtract))
                    link(tt(s5s[:, 11], s5s[:, 11], s5s[:, 8], ALU.mult))
                    link(v.memset(pw5[:, 0, :, 0], 1.0))
                    link(v.memset(pw5[:, 1, :, 0], 0.0))
                    link(v.tensor_copy(pw5[:, 0, :, 1], s5s[:, 6]))
                    link(v.tensor_copy(pw5[:, 1, :, 1], s5s[:, 7]))
                    for j in range(2, Q5 + 1):
                        x1, x2 = j // 2, j - j // 2
                        link(tt(s5s[:, 12], pw5[:, 0, :, x1], pw5[:, 0, :, x2], ALU.mult))
                        link(tt(s5s[:, 13], pw5[:, 1, :, x1], pw5[:, 1, :, x2], ALU.mult))
                        link(tt(pw5[:, 0, :, j], s5s[:, 12], s5s[:, 13], ALU.subtract))
                        link(tt(s5s[:, 12], pw5[:, 0, :, x1], pw5[:, 1, :, x2], ALU.mult))
                        link(tt(s5s[:, 13], pw5[:, 1, :, x1], pw5[:, 0, :, x2], ALU.mult))
                        link(tt(pw5[:, 1, :, j], s5s[:, 12], s5s[:, 13], ALU.add))
                    link(ts(pw5[:, 2], pw5[:, 1], -1.0, None, ALU.mult))
                    for part in range(2):
                        for to, k in enumerate(((0, 1), (2, 0))[part]):
                            link(v.tensor_copy(am5[:, part, to], pw5[:, k, :, Q5]))
                    bre = pv('bre').rearrange("p (g h) -> p g h", g=PAIRS)
                    bim = pv('bim').rearrange("p (g h) -> p g h", g=PAIRS)
                    cre = pv('cre').rearrange("p (g h) -> p g h", g=PAIRS)
                    cim = pv('cim').rearrange("p (g h) -> p g h", g=PAIRS)
                    fr = s5s[:, 10].unsqueeze(2).to_broadcast([P, PAIRS, H5])
                    fi = s5s[:, 11].unsqueeze(2).to_broadcast([P, PAIRS, H5])
                    xsf = wide[:, 0:D]
                    gflat1 = qkT[:, :, :].rearrange("p f t -> p (f t)")
                    gflat2 = tg[:].rearrange("p a b n -> p (a b n)")
                    v.wait_ge(zeroed, 1)
                    t1 = xsf[:, 0:PAIRS * H5].rearrange("p (g h) -> p g h", g=PAIRS)
                    t2 = xsf[:, BANK:BANK + PAIRS * H5].rearrange("p (g h) -> p g h", g=PAIRS)
                    for r, (fa, fb, op) in enumerate(((fr, fi, ALU.subtract), (fi, fr, ALU.add))):
                        link(tt(t1, bre, fa, ALU.mult))
                        link(tt(t2, bim, fb, ALU.mult))
                        for h in range(2):
                            rows = slice(P5 * h, P5 * (h + 1))
                            link(tt(BD[rows, r, :, H5 * h:H5 * (h + 1)], t1[rows], t2[rows], op))
                    big = xsf.rearrange("p (g s h) -> p g s h", g=PAIRS, s=Q5)
                    for r in range(2):
                        dst = V5[:, r, :].rearrange("p (g s h) -> p g s h", g=PAIRS, s=Q5)
                        pa, pb = (0, 1) if r == 0 else (1, 0)

                        def pw(k):
                            return pw5[:, k, :, 0:Q5][:, :, ::-1].unsqueeze(3).to_broadcast([P, PAIRS, Q5, 2 * H5])

                        def bd(k):
                            return BD[:, k].unsqueeze(2).to_broadcast([P, PAIRS, Q5, 2 * H5])

                        link(tt(dst, bd(0), pw(pa), ALU.mult))
                        link(tt(big, bd(1), pw(pb), ALU.mult))
                        ins = tt(dst, dst, big, ALU.subtract if r == 0 else ALU.add)
                        if r == 0:
                            link(ins)
                    tell(ins, v5_ready)
                    g1 = gflat1[:, 0:PAIRS * (Q5 + 1) * H5].rearrange("p (g j h) -> p g j h", g=PAIRS, j=Q5 + 1)
                    g2 = gflat2[:, 0:PAIRS * (Q5 + 1) * H5].rearrange("p (g j h) -> p g j h", g=PAIRS, j=Q5 + 1)
                    v.wait_ge(v5_ready, 1)
                    v.wait_ge(zeroed, 2)
                    full = [P, PAIRS, Q5 + 1, H5]
                    for r, (ka, kb) in enumerate(((0, 1), (2, 0))):
                        link(tt(g1, cre.unsqueeze(2).to_broadcast(full), pw5[:, ka].unsqueeze(3).to_broadcast(full),
                                ALU.mult))
                        link(tt(g2, cim.unsqueeze(2).to_broadcast(full), pw5[:, kb].unsqueeze(3).to_broadcast(full),
                                ALU.mult))
                        for h in range(2):
                            rows = slice(P5 * h, P5 * (h + 1))
                            ins = tt(GD[rows, r, :, :, H5 * h:H5 * (h + 1)], g1[rows], g2[rows], ALU.subtract)
                        if r == 0:
                            link(ins)
                    tell(ins, g5_ready)
                    v.wait_ge(g5_ready, 1)
                    link(ts(bgh[:, 0:KT * NB], pv('bg'), 0.5, None, ALU.mult))
                    tell(ts(bgh[:, KT * NB:], pv('bglu'), 0.5, None, ALU.mult), half_done)
                    link(ts(wconv[:], prm[:, PO['cw'][0]:PO['cb'][1]], 0.5, None, ALU.mult))
                    b = START['small', 0]
                    v.wait_ge(taken, b + 2)
                    link(tt(dts[:, 9], tok[:, :, C_DT:TOKW], pv('dtb').unsqueeze(1).to_broadcast([P, MT, SSDH]),
                            ALU.add))
                    tell(stt(dts[:, 6], dts[:, 9], -1.0, dts[:, 9], ALU.mult, ALU.min), dt_arg)
                    v.wait_ge(dt_exp, 1)
                    tell(ts(dts[:, 7], dts[:, 6], 1.0, None, ALU.add), dt_u)
                    link(ts(dts[:, 2], dts[:, 7], -1.0, None, ALU.add))
                    link(tt(dts[:, 2], dts[:, 6], dts[:, 2], ALU.subtract))
                    link(v.reciprocal(dts[:, 3], dts[:, 7]))
                    link(tt(dts[:, 2], dts[:, 2], dts[:, 3], ALU.mult))
                    v.wait_ge(k5_out, 4)
                    kd = gflat2[0:32, 0:PAIRS * 32].rearrange("p (g n) -> p g n", g=PAIRS)
                    link(tt(kd, ident[0:32, 0:32].unsqueeze(1).to_broadcast([32, PAIRS, 32]),
                            pv('dsk', 32).unsqueeze(2).to_broadcast([32, PAIRS, 32]), ALU.mult))
                    k0 = K5.rearrange("p (g n) -> p g n", g=PAIRS)[:, :, 0:32]
                    tell(tt(k0, k0, kd, ALU.add), k5_diag)
                    v.wait_ge(dt_ln, 1)
                    link(tt(dts[:, 2], dts[:, 8], dts[:, 2], ALU.add))
                    link(stt(dt, dts[:, 9], 0.0, dts[:, 2], ALU.max, ALU.add))
                    v.wait_ge(a_step, 1)
                    link(tt(da, dt, dts[:, 5, 0].unsqueeze(1).to_broadcast([P, MT, SSDH]), ALU.mult))
                    tell(ts(da, da, -1.0, None, ALU.mult), da_done)

                    def conv(i):
                        v.wait_ge(taken, START['xbc', i] + 1)
                        c = cv[:, i % 2]
                        wc = wconv[:, CONV * i:CONV * (i + 1)]
                        link(ts(c, xb[:, i, 0:SEQ], wc[:, 0:1], wconv[:, XT * CONV + i:XT * CONV + i + 1],
                                ALU.mult, ALU.add))
                        for j in range(1, CONV):
                            ins = stt(c, xb[:, i, j:j + SEQ], wc[:, j:j + 1], c, ALU.mult, ALU.add)
                            if j < CONV - 1:
                                link(ins)
                        tell(ins, conv_done)

                    def silu(i):
                        v.wait_ge(conv_t, i + 1)
                        tell(stt(xb[:, i, CONV - 1:], th[:, i % 2], 1.0, cv[:, i % 2], ALU.add,
                            ALU.mult), xbc_done)

                    def scan(first, last):
                        for c in range(first, min(last, C5)):
                            link(tt(sc5[:], ST[:, c].unsqueeze(2).to_broadcast([P, 2, 2, PAIRS]), am5[:], ALU.mult))
                            link(tt(sc5[:, 0], sc5[:, 0], sc5[:, 1], ALU.add))
                            ins = tt(ST[:, c + 1], ST[:, c + 1], sc5[:, 0], ALU.add)
                            if c == C5 - 1:
                                tell(ins, scan_done)
                            else:
                                link(ins)

                    finished(v, 'vmem', 1)
                    link(v.memset(xb[:, :, 0:CONV - 1], 0.0))
                    for i in range(XT):
                        conv(i)
                        if i:
                            silu(i - 1)
                        if i > 6:
                            if i == 7:
                                v.wait_ge(in5_out, 4)
                                v.wait_ge(zeroed, 3)
                            scan(4 * (i - 7), 4 * (i - 6))
                    silu(XT - 1)
                    scan(4 * (XT - 7), C5)
                    v.wait_ge(taken, START['tok', 1] + 2)
                    heads = tok[:, :, 0:ROPED * HD].rearrange("p m (h e) -> p m h e", e=HD)
                    half = ROPE // 2
                    xa, xc = heads[:, :, :, 0:half], heads[:, :, :, half:ROPE]
                    shape = [P, MT, ROPED, half]
                    co = cs[:, 0].unsqueeze(2).to_broadcast(shape)
                    si = cs[:, 1].unsqueeze(2).to_broadcast(shape)
                    for m in range(MT):
                        link(tt(rt[:, 0, m], xa[:, m], co[:, m], ALU.mult))
                        link(tt(rt[:, 1, m], xc[:, m], si[:, m], ALU.mult))
                        link(tt(rt[:, 2, m], xc[:, m], co[:, m], ALU.mult))
                        link(tt(rt[:, 3, m], xa[:, m], si[:, m], ALU.mult))
                        link(tt(xa[:, m], rt[:, 0, m], rt[:, 1, m], ALU.subtract))
                        ins = tt(xc[:, m], rt[:, 2, m], rt[:, 3, m], ALU.add)
                        if m == 0:
                            link(ins)
                    link(ins)
                    v.tensor_copy(ik2[:, :, 0], tok[:, :, 14 * HD:15 * HD])
                    tell(v.tensor_copy(ik2[:, :, 1], tok[:, :, 14 * HD:15 * HD]), rope_done)
                    link(ts(wi[:], tok[:, :, C_IW:C_DT], IDX_SCALE, None, ALU.mult))
                    v.wait_ge(acs_ps, 1)
                    tell(v.tensor_copy(acs, sp[0][:, 0:MT * SSDH].rearrange("p (m h) -> p m h", m=MT)), acs_out)
                    tell(tt(dec[:, 0], sp[0][:, 64:64 + SSDH], acs[:, 0], ALU.subtract), acs_arg)
                    v.wait_ge(cb_ps, 1)
                    tell(v.tensor_copy(cbT[:].rearrange("p c g n -> p (c g n)"), sp[1][:]), cb_out)
                    v.wait_ge(xs_out, 4)
                    hp = [P, MT, SSDH, HD]
                    x4 = xs.rearrange("p m (h e) -> p m h e", e=HD)
                    d4 = xdt.rearrange("p m (h e) -> p m h e", e=HD)
                    for m in range(MT):
                        link(tt(d4[:, m], x4[:, m], dt[:, m].unsqueeze(2).to_broadcast(hp[0:1] + hp[2:]), ALU.mult))
                    v.wait_ge(acs_exp, 1)
                    tell(tt(xdd.rearrange("p (h e) -> p h e", e=HD), d4[:, 0],
                       dec[:, 0].unsqueeze(2).to_broadcast([P, SSDH, HD]), ALU.mult), xdt_done)
                    for m in range(MT):
                        link(tt(x4[:, m], x4[:, m], pv('dh').unsqueeze(2).to_broadcast([P, SSDH, HD]), ALU.mult))
                    for hf in range(2):
                        v.wait_ge(y5_ps, hf + 1)
                        for j in range(8):
                            gi = 8 * hf + j
                            dst = y5[32 * (gi % 4):32 * (gi % 4) + 32, gi // 4, :].rearrange("p (c q) -> p q c", q=Q5)
                            for q in range(Q5):
                                ins = v.tensor_copy(dst[:, q, :], sp[2 + hf][32 * q:32 * q + 32, j * C5:(j + 1) * C5])
                        tell(ins, y5_out)
                    yf = y5[:].rearrange("p a t -> p (a t)")
                    lf = LG.rearrange("p a n -> p (a n)")
                    link(tt(lf, yf, yf, ALU.mult))
                    link(ts(lf, lf, 0.044715, 1.0, ALU.mult, ALU.add))
                    tell(tt(lf, lf, yf, ALU.mult), gelu_arg)
                    link(ts(yf, yf, 0.5, None, ALU.mult))
                    zf = z5[:].rearrange("p a t -> p (a t)")
                    v.wait_ge(taken, START['z5', 3] + 1)
                    tell(stt(zf, tg[:, 0].rearrange("p b n -> p (b n)"), 1.0, zf, ALU.add, ALU.mult), z_done)
                    v.wait_ge(gelu_t, 1)
                    tell(stt(yf, lf, 1.0, yf, ALU.add, ALU.mult), gelu_done)

                    for qb in range(MT):
                        nk = (qb + 1) * P
                        sc, sm = sco[:, 0:nk], stm[:, 0:nk]
                        v.wait_ge(ix_ps, qb + 1)
                        for h in range(IH):
                            ps = sp[h % 2][:, (h // 2) * SEQ:(h // 2) * SEQ + nk]
                            ins = ts(sm if h else sc, ps, 0.0, wi[:, qb, h:h + 1], ALU.max, ALU.mult)
                            if h == IH - 1:
                                tell(ins, ix_out)
                            else:
                                link(ins)
                            if h:
                                link(tt(sc, sc, sm, ALU.add))
                        vis = seen[:, SEQ - nk:SEQ]
                        link(tt(sc, sc, vis, ALU.add))
                        for _r in range(TOPK // 8):
                            link(v.max(top[:], sc))
                            link(v.match_replace(sc, top[:], sc, TAKEN))
                        link(ts(sc, sc, TAKEN / 1.5, MASKED, ALU.is_gt, ALU.mult))
                        link(tt(amask[:, qb, 0:nk], sc, vis, ALU.add))
                    v.wait_ge(glu_t, 4)
                    link(stt(yf, pT.rearrange("p a n -> p (a n)"), 1.0, yf, ALU.add, ALU.mult))
                    tell(stt(yT[:, 0:4, :].rearrange("p a t -> p (a t)"), yf, 0.25, zf, ALU.mult,
                        ALU.mult), s5_done)

                    def seg_arg(n):
                        c, rd = n // 4, n % 4
                        sg = seg[:, n % 2].rearrange("p (h l) -> p h l", h=4)
                        if n >= 2:
                            v.wait_ge(yd_ps, n - 1)
                        v.wait_ge(ab_ps, n + 1)
                        link(tt(sg, sp[0][:].rearrange("p (h l) -> p h l", h=4),
                                acs[:, c, 4 * rd:4 * rd + 4].unsqueeze(2).to_broadcast([P, 4, P]), ALU.subtract))
                        tell(tt(sg, sg, maskT[:].unsqueeze(1).to_broadcast([P, 4, P]), ALU.add), seg_done)

                    def seg_mul(n):
                        c, rd = n // 4, n % 4
                        sg = seg[:, n % 2].rearrange("p (h l) -> p h l", h=4)
                        v.wait_ge(seg_exp, n + 1)
                        tell(tt(sg, sg, cbT[:, c, rd // 2].unsqueeze(1).to_broadcast([P, 4, P]), ALU.mult), m_done)

                    def y_in(c):
                        v.wait_ge(yd_ps, 4 * (c + 1))
                        for b in range(2):
                            d = xs[:, c, b * BANK:(b + 1) * BANK]
                            tell(tt(d, d, sp[2 + b][:], ALU.add), yd_out)

                    for n in range(8):
                        if n:
                            seg_mul(n - 1)
                        seg_arg(n)
                        if n == 4:
                            y_in(0)
                            v.wait_ge(taken, START['zssd', 1] + 2)
                            zsf = zssd.rearrange("p m n -> p (m n)")
                            tell(stt(zsf, tg[:].rearrange("p a b n -> p (a b n)"), 1.0, zsf, ALU.add, ALU.mult),
                                 z_done)
                    seg_mul(7)
                    for g in range(SSDG):
                        v.wait_ge(yo_ps, g + 1)
                        tmp = cv.rearrange("p a n -> p (a n)").rearrange("p (h e) -> p h e", e=HD)
                        tell(tt(tmp, sp[1][:].rearrange("p (h e) -> p h e", e=HD),
                           eacs[:, 1, 8 * g:8 * g + 8].unsqueeze(2).to_broadcast([P, 8, HD]),
                           ALU.mult), yo_out)
                        d = x4[:, 1, 8 * g:8 * g + 8]
                        link(tt(d, d, tmp, ALU.add))
                    y_in(1)
                    v.wait_ge(yd_out, 4)
                    v.wait_ge(z_done, 2)
                    v.wait_ge(taken, START['zatt', 3] + 1)
                    zaf = zatt[:].rearrange("p a t -> p (a t)")
                    zmf = zmem[:].rearrange("p a t -> p (a t)")
                    tell(stt(zaf, tg[:, 0].rearrange("p b n -> p (b n)"), 1.0, zaf, ALU.add, ALU.mult), z_done)

                    def scaled(b):
                        sparse, qb, heads = BATCH[b]
                        nk, nh = keys_of(b), len(BATCH[b][2])
                        v.wait_ge(lg_ps, b + 1)
                        if b >= 2:
                            v.wait_ge(pt_ps, b - 1)
                        lg = LG[:, b % 2].rearrange("p (h k) -> p h k", h=nh)
                        for half in range(2):
                            ps = sp[half][:, 0:SEQ].rearrange("p (h k) -> p h k", k=nk)
                            lh = lg[:, half * nh // 2:(half + 1) * nh // 2]
                            if sparse:
                                link(stt(lh, ps, ATT_SCALE,
                                         amask[:, qb, 0:nk].unsqueeze(1).to_broadcast([P, nh // 2, nk]),
                                         ALU.mult, ALU.add))
                            else:
                                link(ts(lh, ps, ATT_SCALE, None, ALU.mult))
                        tell(v.tensor_reduce(smx[:, 0, b % 2, 0:nh], lg, AX.X, ALU.max, negate=True), lg_out)

                    def normed(b):
                        nk, nh = keys_of(b), len(BATCH[b][2])
                        v.wait_ge(lg_exp, b + 1)
                        link(v.reciprocal(smx[:, 2, b % 2, 0:nh], smx[:, 1, b % 2, 0:nh]))
                        lg = LG[:, b % 2].rearrange("p (h k) -> p h k", h=nh)
                        tell(tt(lg, lg, smx[:, 2, b % 2, 0:nh].unsqueeze(2).to_broadcast([P, nh, nk]),
                           ALU.mult), p_done)

                    def gated(b):
                        sparse, qb, heads = BATCH[b]
                        v.wait_ge(o_ps, b + 1)
                        f, n = heads[0][0], len(heads) // 2
                        z = (zatt if sparse else zmem)[:, f:f + n, qb * P:(qb + 1) * P]
                        k = KOF[1 if sparse else 3][0]
                        tell(stt(yT[:, k + f:k + f + n, qb * P:(qb + 1) * P], sp[3][:, 0:n * P].rearrange("p (f t) -> p f t", f=n),
                            0.5, z, ALU.mult, ALU.mult), o_out)

                    for b in range(len(BATCH)):
                        scaled(b)
                        normed(b)
                        if b:
                            gated(b - 1)
                        if b == 0:
                            link(stt(xsf, xsf, 0.5, zsf, ALU.mult, ALU.mult))
                        if b == 1:
                            for m in range(MT):
                                for g in range(SSDG):
                                    y = xs[:, m, g * BANK:(g + 1) * BANK]
                                    link(stt(cv.rearrange("p a n -> p (a n)"), y, 1.0, y, ALU.mult, ALU.mult,
                                             accum_out=rms[:, 0, m, g:g + 1]))
                            tell(ts(rms[:, 0], rms[:, 0], 1.0 / BANK, RMS_EPS, ALU.mult, ALU.add), rms_arg)
                        if b == 3:
                            v.wait_ge(rms_pow, 1)
                            for m in range(MT):
                                for g in range(SSDG):
                                    y = xs[:, m, g * BANK:(g + 1) * BANK]
                                    ins = ts(y, y, rms[:, 1, m, g:g + 1], None, ALU.mult)
                                tell(ins, ys_done)
                        if b == 4:
                            v.wait_ge(taken, START['zmem', 1] + 1)
                            tell(stt(zmf, tg[:, 1, 0:2].rearrange("p b n -> p (b n)"), 1.0, zmf, ALU.add,
                                ALU.mult), z_done)
                    gated(len(BATCH) - 1)
                    v.wait_ge(yhi_done, 1)
                    for lo, hi in (KOF[0], KOF[1], KOF[3]):
                        link(tt(y_lo[:, lo:hi], yT[:, lo:hi], y_hi[:, lo:hi].bitcast(F32), ALU.subtract))
                    v.wait_ge(yhi_done, 2)
                    lo, hi = KOF[2]
                    tell(tt(y_lo[:, lo:hi], yT[:, lo:hi], y_hi[:, lo:hi].bitcast(F32), ALU.subtract), ylo_done)
                    for d in range(KT):
                        pair = 2 * (d % 2)
                        finished(v, 'branch', d)
                        v.wait_ge(gate_t, NB * (d + 1))
                        for i in range(2):
                            link(stt(mg[:, i], tg[:, d % 2, 2 * i:2 * i + 2].rearrange("p b n -> p (b n)"), 1.0,
                                     sp[pair + i][:], ALU.add, ALU.mult))
                        link(tt(mg[:, 0], mg[:, 0], mg[:, 1], ALU.add))
                        total = mg[:, 1, 0:SEQ]
                        link(tt(total, mg[:, 0, 0:SEQ], mg[:, 0, SEQ:], ALU.add))
                        link(v.tensor_copy(m_hi[:, d, :], total))
                        tell(tt(m_lo[:, d, :], total, m_hi[:, d, :].bitcast(F32), ALU.subtract), mg_done)
                    v.wait_ge(ax_done, MT)
                    for c in range(4):
                        finished(v, 'out', 4 * c + 3)
                        for m in range(MT):
                            xv = xtok[:, m, c * BANK:(c + 1) * BANK]
                            tell(stt(xv, gp[2 * ((c + 1) % 2) + m][:], 0.5, xv, ALU.mult, ALU.add), res_done)
                            link(v.bn_stats(st6[:, m, c, :], xv))
                            if c == 3:
                                link(v.bn_aggr(mv[:, m, 0:2], st6[:, m].rearrange("p c s -> p (c s)")))
                                tell(ts(mv[:, m, 2:3], mv[:, m, 1:2], LN_EPS, None, ALU.add), var_done)
                    v.wait_ge(lng_in, 16)

                    def low_x(n):
                        m, q = n // 4, n % 4
                        v.wait_ge(xhi_out, n + 1)
                        fs, ms = slice(4 * q, 4 * q + 4), slice(m * P, (m + 1) * P)
                        tell(tt(x_lo[:, fs, ms], sp[q][:].rearrange("p (f t) -> p f t", f=4),
                                x_hi[:, fs, ms].bitcast(F32), ALU.subtract), xt_out)

                    for n in range(8):
                        m, cols = n // 4, slice(n % 4 * BANK, (n % 4 + 1) * BANK)
                        v.wait_ge(rstd_done, m + 1)
                        xc = xtok[:, m, cols]
                        link(ts(xc, xc, mv[:, m, 0:1], mv[:, m, 2:3], ALU.subtract, ALU.mult))
                        tell(tt(xc, xc, lng[:, cols], ALU.mult), gain_done)
                        if n >= 4:
                            low_x(n - 4)
                    for n in range(4, 8):
                        low_x(n)
            nc.multi_engine_barrier(mybir.ALL_ENGINES, sems_to_clear=clear)


def kernel(**inputs):
    import concourse.bacc as bacc
    from concourse.bass_utils import run_bass_kernel_spmd

    a = {k: np.asarray(v) for k, v in inputs.items()}
    sizes = (('s5_u', 512), ('s5_z', 512), ('att_q', 512), ('att_k', 128), ('att_v', 128), ('att_z', 512),
             ('idx_q', 256), ('idx_k', 64), ('idx_w', 4), ('ssd_z', 1024), ('ssd_xbc', XBC), ('ssd_dt', 16),
             ('mem_q', 256), ('mem_z', 256), ('gates', NB * D))
    col, o = {}, 0
    for name, n in sizes:
        col[name] = np.arange(o, o + n)
        o += n
    order = np.concatenate([np.arange(HD) + HD * (j + AKV * 2 * h) for j in range(4) for h in range(2)])
    win, wkv = a['w_in'], a['mem_w_kv']

    def t_units(m):
        n = m.shape[2] // P
        return m.reshape(DEPTH, KT, P, n, P).transpose(0, 3, 2, 1, 4).reshape(DEPTH, n, P, KT * P)

    def m_units(m, cols, per):
        k, n = m.shape[1] // P, m.shape[2] // cols
        u = m.reshape(DEPTH, k // per, per, P, n, cols).transpose(0, 4, 1, 3, 2, 5)
        return u.reshape(DEPTH, n * (k // per), P, per * cols)

    tokc = np.concatenate([col['att_q'][order], col['att_k'], col['idx_q'], col['idx_k'], col['att_v'],
                           col['idx_w'], col['ssd_dt']])
    gates = win[:, :, col['gates']].reshape(DEPTH, D, NB, KT, P).transpose(0, 1, 3, 2, 4).reshape(DEPTH, D, NB * D)
    wbr = np.concatenate([a['w_br_s5'], a['w_br_attn'][:, order], a['w_br_ssd'], a['w_br_mem']], axis=1)
    arrays = {
        'u5': t_units(win[:, :, col['s5_u']]), 'z5': t_units(win[:, :, col['s5_z']]),
        'xbc': t_units(win[:, :, col['ssd_xbc']]), 'zatt': t_units(win[:, :, col['att_z'][order]]),
        'qmem': t_units(win[:, :, col['mem_q']]), 'zmem': t_units(win[:, :, col['mem_z']]),
        'kmem': t_units(wkv[:, :, :MEMH * HD]), 'vmem': m_units(wkv[:, :, MEMH * HD:], MEMH * HD, 8),
        'gate': t_units(gates), 'tok': m_units(win[:, :, tokc[:2 * BANK]], BANK, 4),
        'small': m_units(win[:, :, tokc[2 * BANK:]], SMALL, KT), 'zssd': m_units(win[:, :, col['ssd_z']], BANK, 4),
        'glu': m_units(a['s5_w_glu'], BANK, 4), 'out': m_units(a['w_out'], BANK, 4),
        'branch': wbr.reshape(DEPTH, KB, P, KT, P).transpose(0, 3, 2, 1, 4).reshape(DEPTH, KT, P, KB * P),
    }
    kinds = list(arrays)

    def state(m):
        rest = m.shape[3:]
        m = m.reshape((DEPTH, PAIRS, 2, P5) + rest)
        return np.moveaxis(m, 1, 3).reshape(DEPTH, P, -1)

    def rows(m):
        return np.broadcast_to(m[:, None, :], (DEPTH, P, m.shape[1]))

    def per_feature(m):
        return m.reshape(DEPTH, -1, P).transpose(0, 2, 1)

    dsk = a['s5_d'].reshape(DEPTH, PAIRS, 2 * H5).transpose(0, 2, 1)
    parts = {
        'lre': state(a['s5_lam_re']), 'lim': state(a['s5_lam_im']),
        'ldt': state(np.broadcast_to(a['s5_log_dt'][:, :, None], (DEPTH, G5, P5))),
        'bre': state(a['s5_b_re']), 'bim': state(a['s5_b_im']),
        'cre': state(a['s5_c_re'].transpose(0, 1, 3, 2)), 'cim': state(a['s5_c_im'].transpose(0, 1, 3, 2)),
        'dsk': np.tile(dsk, (1, 4, 1)), 'bglu': per_feature(a['s5_b_glu']),
        'cw': a['ssd_conv_w'].reshape(DEPTH, CONV, XT, P).transpose(0, 3, 2, 1).reshape(DEPTH, P, XT * CONV),
        'cb': per_feature(a['ssd_conv_b']), 'dtb': rows(a['ssd_dt_bias']), 'alog': rows(a['ssd_a_log']),
        'dh': rows(a['ssd_d']), 'ng': per_feature(a['ssd_norm_g']),
        'bg': a['b_gate'].reshape(DEPTH, NB, KT, P).transpose(0, 3, 2, 1).reshape(DEPTH, P, KT * NB),
    }
    arrays['par'] = np.concatenate([parts[n] for n, _ in PARAMS], axis=2)

    def t_tokens(m):
        return m[0].T.reshape(KT, P, SEQ).transpose(1, 0, 2)

    arrays['x'] = a['x'][0]
    arrays['x_t'] = t_tokens(a['x'])
    arrays['mem_t'] = t_tokens(a['mem'])
    arrays['pos'] = a['positions'][0].reshape(MT, P).T
    arrays['ln_g'] = a['ln_g']
    arrays['ln_b'] = a['ln_b']
    arrays = {f"in_{k}": np.ascontiguousarray(v) for k, v in arrays.items()}
    nc = bacc.Bacc("TRN2", target_bir_lowering=False, num_devices=1)
    ap = {k: nc.dram_tensor(k, v.shape, mybir.dt.from_np(v.dtype), kind="ExternalInput").ap()
          for k, v in arrays.items()}
    out = nc.dram_tensor("out", (SEQ, D), F32, kind="ExternalOutput").ap()
    build(nc, ap['in_x'], ap['in_x_t'], ap['in_mem_t'], ap['in_pos'], {k: ap[f"in_{k}"] for k in kinds},
          ap['in_par'], ap['in_ln_g'], ap['in_ln_b'], out)
    r = run_bass_kernel_spmd(nc, [arrays], core_ids=[0])
    return r.results[0]["out"].reshape(1, SEQ, D)
```
